# Optimizing a Trainium2 kernel written in Bass

```python
import jax, jax.numpy as jnp
from jax import lax
import numpy as np

D_MODEL = 1024
BATCH = 1
SEQ = 512
DEPTH = 2
DEC_BATCH = 8
DEC_SEQ = 1
PAST_LEN = 4096
PAGE_SIZE = 128

D_MIX = 2 * D_MODEL
CONV_WIDTH = 4
CHUNK = 64
NORM_EPS = 1e-6
SSD_WIDTH = D_MIX // 2
SSD_HEAD_DIM = 64
SSD_HEADS = SSD_WIDTH // SSD_HEAD_DIM
SSD_GROUPS = 2
SSD_HPG = SSD_HEADS // SSD_GROUPS
SSD_STATE = 128
SSD_CONV_DIM = SSD_WIDTH + 2 * SSD_GROUPS * SSD_STATE
RET_WIDTH = D_MIX // 4
RET_HEADS = 4
RET_HEAD_DIM = RET_WIDTH // RET_HEADS
ROPE_BASE = 10000.0
LRU_WIDTH = D_MIX // 4
LRU_BLOCKS = 8
LRU_BLOCK_DIM = LRU_WIDTH // LRU_BLOCKS
LRU_C = 8.0
IN_WIDTH = SSD_WIDTH + SSD_CONV_DIM + SSD_HEADS + 4 * RET_WIDTH + 2 * LRU_WIDTH
PEER_KEYS = 128
PEER_EXPERTS = PEER_KEYS * PEER_KEYS
PEER_HEADS = 8
PEER_TOPK = 16
PEER_QUERY_DIM = 256
PEER_HALF = PEER_QUERY_DIM // 2
PEER_TOKEN_BLOCK = 256

kernel_name = 'hymba_ssd_retnet_rglru_peer_step'

def rmsnorm(x, w=None):
    xf = x.astype(jnp.float32)
    xf = xf * lax.rsqrt(jnp.mean(xf * xf, axis=-1, keepdims=True) + NORM_EPS)
    if w is not None:
        xf = xf * w.astype(jnp.float32)
    return xf

def causal_conv(x, buf, w, b):
    l = x.shape[1]
    xp = jnp.concatenate([buf.astype(x.dtype), x], axis=1)
    y = b.astype(x.dtype)
    for tap in range(CONV_WIDTH):
        y = y + xp[:, tap:tap + l] * w[tap]
    return y, xp[:, l:]

def rotary(x, pos):
    half = x.shape[-1] // 2
    inv = ROPE_BASE ** (-jnp.arange(half, dtype=jnp.float32) / half)
    ang = pos.astype(jnp.float32)[:, None] * inv[None, :]
    cos = jnp.cos(ang)[None, :, None, :]
    sin = jnp.sin(ang)[None, :, None, :]
    x1 = x[..., :half].astype(jnp.float32)
    x2 = x[..., half:].astype(jnp.float32)
    return jnp.concatenate([x1 * cos - x2 * sin, x1 * sin + x2 * cos], axis=-1).astype(x.dtype)

def pad_seq(a, pad):
    return jnp.pad(a, [(0, 0), (0, pad)] + [(0, 0)] * (a.ndim - 2))

def chunked_scan(q, k, v, log_a, s0):
    b, l = q.shape[:2]
    c = min(CHUNK, l)
    nc = -(-l // c)
    pad = nc * c - l
    q, k, v, log_a = (pad_seq(a, pad) for a in (q, k, v, log_a))
    split = lambda a: a.reshape((b, nc, c) + a.shape[2:])
    q, k, v = split(q), split(k), split(v)
    cum = jnp.cumsum(split(log_a.astype(jnp.float32)), axis=2)
    causal = jnp.tril(jnp.ones((c, c), bool))[None, None, :, :, None, None]
    seg = cum[:, :, :, None] - cum[:, :, None, :]
    decay = jnp.exp(jnp.where(causal, seg, -jnp.inf))
    scores = jnp.einsum('bzign,bzjgn->bzijg', q, k)
    y_intra = jnp.einsum('bzijgr,bzjgrp->bzigrp', scores[..., None] * decay, v)
    to_end = jnp.exp(cum[:, :, -1:] - cum)
    chunk_states = jnp.einsum('bzjgn,bzjgrp->bzgrnp', k, v * to_end[..., None])
    chunk_decay = jnp.exp(cum[:, :, -1])

    def carry(s, inp):
        cs, cd = inp
        return s * cd[..., None, None] + cs, s

    s_final, s_in = lax.scan(carry, s0.astype(jnp.float32),
                             (jnp.moveaxis(chunk_states, 1, 0), jnp.moveaxis(chunk_decay, 1, 0)))
    s_in = jnp.moveaxis(s_in, 0, 1)
    y_inter = jnp.einsum('bzign,bzgrnp->bzigrp', q, s_in) * jnp.exp(cum)[..., None]
    y = (y_intra + y_inter).reshape((b, nc * c) + v.shape[3:])[:, :l]
    return y, s_final

def ssd_group(z, xbc, dt, s0, buf, conv_w, conv_b, dt_bias, a_log, d_skip, norm_w):
    b, l, _ = z.shape
    xbc, new_buf = causal_conv(xbc, buf, conv_w, conv_b)
    xbc = jax.nn.silu(xbc)
    xs = xbc[..., :SSD_WIDTH].reshape(b, l, SSD_GROUPS, SSD_HPG, SSD_HEAD_DIM)
    bm = xbc[..., SSD_WIDTH:SSD_WIDTH + SSD_GROUPS * SSD_STATE].reshape(b, l, SSD_GROUPS, SSD_STATE)
    cm = xbc[..., SSD_WIDTH + SSD_GROUPS * SSD_STATE:].reshape(b, l, SSD_GROUPS, SSD_STATE)
    dt = jax.nn.softplus(dt.astype(jnp.float32) + dt_bias.astype(jnp.float32)).reshape(b, l, SSD_GROUPS, SSD_HPG)
    log_a = -dt * jnp.exp(a_log.astype(jnp.float32)).reshape(SSD_GROUPS, SSD_HPG)
    y, s = chunked_scan(cm, bm, xs * dt[..., None], log_a,
                        s0.reshape(b, SSD_GROUPS, SSD_HPG, SSD_STATE, SSD_HEAD_DIM))
    y = y + d_skip.astype(jnp.float32).reshape(SSD_GROUPS, SSD_HPG, 1) * xs
    y = rmsnorm(y.reshape(b, l, SSD_WIDTH) * jax.nn.silu(z.astype(jnp.float32)), norm_w)
    return y, s.reshape(b, SSD_HEADS, SSD_STATE, SSD_HEAD_DIM), new_buf

def retention_group(q, k, v, g, s0, pos):
    b, l, _ = q.shape
    q = rotary(q.reshape(b, l, RET_HEADS, RET_HEAD_DIM), pos)
    k = rotary(k.reshape(b, l, RET_HEADS, RET_HEAD_DIM), pos) * (RET_HEAD_DIM ** -0.5)
    v = v.reshape(b, l, RET_HEADS, 1, RET_HEAD_DIM)
    log_gamma = jnp.log(1.0 - jnp.exp2(-5.0 - jnp.arange(RET_HEADS, dtype=jnp.float32)))
    log_a = jnp.broadcast_to(log_gamma[:, None], (b, l, RET_HEADS, 1))
    y, s = chunked_scan(q, k, v, log_a, s0.reshape(b, RET_HEADS, 1, RET_HEAD_DIM, RET_HEAD_DIM))
    y = rmsnorm(y[:, :, :, 0]).reshape(b, l, RET_WIDTH) * jax.nn.silu(g.astype(jnp.float32))
    return y, s.reshape(b, RET_HEADS, RET_HEAD_DIM, RET_HEAD_DIM)

def lru_combine(left, right):
    a_l, b_l = left
    a_r, b_r = right
    return a_l * a_r, a_r * b_l + b_r

def rglru_group(gate, xr, h0, buf, conv_w, conv_b, wa, ba, wi, bi, lam):
    b, l, _ = xr.shape
    xr, new_buf = causal_conv(xr, buf, conv_w, conv_b)
    xb = xr.reshape(b, l, LRU_BLOCKS, LRU_BLOCK_DIM)
    r = jax.nn.sigmoid(jnp.einsum('blhi,hij->blhj', xb, wa).reshape(b, l, LRU_WIDTH) + ba).astype(jnp.float32)
    i = jax.nn.sigmoid(jnp.einsum('blhi,hij->blhj', xb, wi).reshape(b, l, LRU_WIDTH) + bi).astype(jnp.float32)
    log_a = -LRU_C * r * jax.nn.softplus(-lam.astype(jnp.float32))
    u = jnp.sqrt(-jnp.expm1(2.0 * log_a)) * (i * xr.astype(jnp.float32))
    a_cum, h = lax.associative_scan(lru_combine, (jnp.exp(log_a), u), axis=1)
    h = h + a_cum * h0.astype(jnp.float32)[:, None]
    y = h * jax.nn.gelu(gate.astype(jnp.float32), approximate=False)
    return y, h[:, -1], new_buf

def peer_ffn(x, wq, keys, u_tab, v_tab):
    b, l, d = x.shape
    t = b * l
    tb = min(PEER_TOKEN_BLOCK, t)
    nb = -(-t // tb)
    xt = jnp.pad(x.reshape(t, d), ((0, nb * tb - t), (0, 0))).reshape(nb, tb, d)

    def block(xb):
        q = (xb @ wq).reshape(tb, PEER_HEADS, 2, PEER_HALF)
        s = jnp.einsum('thcn,hckn->thck', q, keys).astype(jnp.float32)
        s_top, i_top = lax.top_k(s, PEER_TOPK)
        cand = s_top[:, :, 0, :, None] + s_top[:, :, 1, None, :]
        cidx = i_top[:, :, 0, :, None] * PEER_KEYS + i_top[:, :, 1, None, :]
        sc, sel = lax.top_k(cand.reshape(tb, PEER_HEADS, PEER_TOPK * PEER_TOPK), PEER_TOPK)
        idx = jnp.take_along_axis(cidx.reshape(tb, PEER_HEADS, PEER_TOPK * PEER_TOPK), sel, axis=-1)
        gate = jax.nn.softmax(sc, axis=-1).reshape(tb, PEER_HEADS * PEER_TOPK)
        idx = idx.reshape(tb, PEER_HEADS * PEER_TOPK)
        act = jax.nn.gelu(jnp.einsum('td,ted->te', xb, u_tab[idx]).astype(jnp.float32), approximate=False)
        return jnp.einsum('te,ted->td', (gate * act).astype(xb.dtype), v_tab[idx])

    y = lax.map(block, xt).reshape(nb * tb, d)[:t]
    return y.reshape(b, l, d)

def layer(x, pos, state, w):
    (n1, w_in, scw, scb, dtb, alog, dsk, snw, lcw, lcb, wa, ba, wi, bi, lam,
     w_out, n2, wq, keys, u_tab, v_tab) = w
    ssd_s, ssd_buf, ret_s, lru_h, lru_buf = state
    h = rmsnorm(x, n1).astype(x.dtype)
    sizes = [SSD_WIDTH, SSD_CONV_DIM, SSD_HEADS, RET_WIDTH, RET_WIDTH, RET_WIDTH, RET_WIDTH, LRU_WIDTH]
    z, xbc, dt, q, k, vr, g, gate, xr = jnp.split(h @ w_in, np.cumsum(sizes).tolist(), axis=-1)
    y_ssd, ssd_s, ssd_buf = ssd_group(z, xbc, dt, ssd_s, ssd_buf, scw, scb, dtb, alog, dsk, snw)
    y_ret, ret_s = retention_group(q, k, vr, g, ret_s, pos)
    y_lru, lru_h, lru_buf = rglru_group(gate, xr, lru_h, lru_buf, lcw, lcb, wa, ba, wi, bi, lam)
    mix = jnp.concatenate([y_ssd, y_ret, y_lru], axis=-1).astype(x.dtype)
    x = x + mix @ w_out
    x = x + peer_ffn(rmsnorm(x, n2).astype(x.dtype), wq, keys, u_tab, v_tab)
    new_state = tuple(s.astype(x.dtype) for s in (ssd_s, ssd_buf, ret_s, lru_h, lru_buf))
    return x, new_state

def setup_inputs(seed: int = 0) -> dict:
    key = jax.random.key(seed)
    ks = iter(jax.random.split(key, 40))
    nrm = lambda shape, scale: jax.random.normal(next(ks), shape, jnp.float32) * scale
    gain = lambda shape: 1.0 + nrm(shape, 0.01)
    dt0 = jnp.exp(jax.random.uniform(next(ks), (DEPTH, SSD_HEADS), jnp.float32, np.log(1e-3), np.log(1e-1)))
    a0 = jax.random.uniform(next(ks), (DEPTH, LRU_WIDTH), jnp.float32, 0.9, 0.999) ** (1.0 / LRU_C)
    return {
        'x_prompt': nrm((BATCH, SEQ, D_MODEL), 1.0),
        'x_sample': nrm((DEC_BATCH, DEC_SEQ, D_MODEL), 1.0),
        'state_ssd': nrm((DEPTH, DEC_BATCH, SSD_HEADS, SSD_STATE, SSD_HEAD_DIM), 0.5),
        'state_ssd_conv': nrm((DEPTH, DEC_BATCH, CONV_WIDTH - 1, SSD_CONV_DIM), 1.0),
        'state_ret': nrm((DEPTH, DEC_BATCH, RET_HEADS, RET_HEAD_DIM, RET_HEAD_DIM), 1.0),
        'state_lru': nrm((DEPTH, DEC_BATCH, LRU_WIDTH), 1.0),
        'state_lru_conv': nrm((DEPTH, DEC_BATCH, CONV_WIDTH - 1, LRU_WIDTH), 1.0),
        'norm1_w': gain((DEPTH, D_MODEL)),
        'w_in': nrm((DEPTH, D_MODEL, IN_WIDTH), D_MODEL ** -0.5),
        'ssd_conv_w': nrm((DEPTH, CONV_WIDTH, SSD_CONV_DIM), CONV_WIDTH ** -0.5),
        'ssd_conv_b': nrm((DEPTH, SSD_CONV_DIM), 0.01),
        'ssd_dt_bias': dt0 + jnp.log(-jnp.expm1(-dt0)),
        'ssd_a_log': jnp.log(jax.random.uniform(next(ks), (DEPTH, SSD_HEADS), jnp.float32, 1.0, 16.0)),
        'ssd_d': gain((DEPTH, SSD_HEADS)),
        'ssd_norm_w': gain((DEPTH, SSD_WIDTH)),
        'lru_conv_w': nrm((DEPTH, CONV_WIDTH, LRU_WIDTH), CONV_WIDTH ** -0.5),
        'lru_conv_b': nrm((DEPTH, LRU_WIDTH), 0.01),
        'lru_wa': nrm((DEPTH, LRU_BLOCKS, LRU_BLOCK_DIM, LRU_BLOCK_DIM), LRU_BLOCK_DIM ** -0.5),
        'lru_ba': nrm((DEPTH, LRU_WIDTH), 0.01),
        'lru_wi': nrm((DEPTH, LRU_BLOCKS, LRU_BLOCK_DIM, LRU_BLOCK_DIM), LRU_BLOCK_DIM ** -0.5),
        'lru_bi': nrm((DEPTH, LRU_WIDTH), 0.01),
        'lru_lambda': jnp.log(a0) - jnp.log1p(-a0),
        'w_out': nrm((DEPTH, D_MIX, D_MODEL), D_MIX ** -0.5),
        'norm2_w': gain((DEPTH, D_MODEL)),
        'peer_wq': nrm((DEPTH, D_MODEL, PEER_HEADS * PEER_QUERY_DIM), D_MODEL ** -0.5),
        'peer_keys': nrm((DEPTH, PEER_HEADS, 2, PEER_KEYS, PEER_HALF), PEER_HALF ** -0.5),
        'peer_u': nrm((DEPTH, PEER_EXPERTS, D_MODEL), D_MODEL ** -0.5),
        'peer_v': nrm((DEPTH, PEER_EXPERTS, D_MODEL), PEER_HEADS ** -0.5),
        'final_norm_w': gain((D_MODEL,)),
    }

def reference(x_prompt, x_sample, state_ssd, state_ssd_conv, state_ret, state_lru, state_lru_conv,
              norm1_w, w_in, ssd_conv_w, ssd_conv_b, ssd_dt_bias, ssd_a_log, ssd_d, ssd_norm_w,
              lru_conv_w, lru_conv_b, lru_wa, lru_ba, lru_wi, lru_bi, lru_lambda, w_out,
              norm2_w, peer_wq, peer_keys, peer_u, peer_v, final_norm_w):
    bp, lp, _ = x_prompt.shape
    act_dtype = x_prompt.dtype
    pos_p = jnp.arange(lp)
    pos_s = PAST_LEN + jnp.arange(x_sample.shape[1])
    zero_state = (jnp.zeros((bp, SSD_HEADS, SSD_STATE, SSD_HEAD_DIM), act_dtype),
                  jnp.zeros((bp, CONV_WIDTH - 1, SSD_CONV_DIM), act_dtype),
                  jnp.zeros((bp, RET_HEADS, RET_HEAD_DIM, RET_HEAD_DIM), act_dtype),
                  jnp.zeros((bp, LRU_WIDTH), act_dtype),
                  jnp.zeros((bp, CONV_WIDTH - 1, LRU_WIDTH), act_dtype))
    hp, hs = x_prompt, x_sample
    new_p, new_s = [], []
    for i in range(DEPTH):
        w = (norm1_w[i], w_in[i], ssd_conv_w[i], ssd_conv_b[i], ssd_dt_bias[i], ssd_a_log[i], ssd_d[i],
             ssd_norm_w[i], lru_conv_w[i], lru_conv_b[i], lru_wa[i], lru_ba[i], lru_wi[i], lru_bi[i],
             lru_lambda[i], w_out[i], norm2_w[i], peer_wq[i], peer_keys[i], peer_u[i], peer_v[i])
        hp, st_p = layer(hp, pos_p, zero_state, w)
        hs, st_s = layer(hs, pos_s, (state_ssd[i], state_ssd_conv[i], state_ret[i], state_lru[i],
                                     state_lru_conv[i]), w)
        new_p.append(st_p)
        new_s.append(st_s)
    y_prompt = rmsnorm(hp, final_norm_w).astype(act_dtype)
    y_sample = rmsnorm(hs, final_norm_w).astype(x_sample.dtype)
    stk = lambda states, j: jnp.stack([s[j] for s in states])
    return (y_prompt, y_sample,
            stk(new_p, 0), stk(new_p, 1), stk(new_p, 2), stk(new_p, 3), stk(new_p, 4),
            stk(new_s, 0), stk(new_s, 1), stk(new_s, 2), stk(new_s, 3), stk(new_s, 4))


_drawn_inputs = setup_inputs


def setup_inputs(seed=0):
    import zlib

    import numpy as np

    out = dict(_drawn_inputs(seed))
    spreads = {}
    factors = {'ssd_d': 3.237, 'lru_ba': 8.0, 'lru_bi': 6.641, 'final_norm_w': 5.481}
    for name, (base, spread) in spreads.items():
        noise = np.random.default_rng([zlib.crc32(name.encode()), seed]).standard_normal(out[name].shape)
        drawn = base * np.exp(spread * noise) if base else spread * noise
        out[name] = __import__('jax').numpy.asarray(drawn.astype(out[name].dtype))
    for name, factor in factors.items():
        out[name] = (out[name] * factor).astype(out[name].dtype)
    return out
```

```python
from contextlib import ExitStack

import numpy as np

import concourse.bass as bass
from concourse import mybir

F32 = mybir.dt.float32
U32 = mybir.dt.uint32
ACT = mybir.ActivationFunctionType
ALU = mybir.AluOpType
AX = mybir.AxisListType

DEPTH, D, SEQ, NS = 2, 1024, 512, 8
T = SEQ + NS
HALF = T // 2
PAST = 4096
EPS = 1e-6
KT = D // 128
H_SSD, P_SSD, N_SSD = 16, 64, 128
H_RET, D_RET = 4, 128
KEYS, H_PEER, TOPK = 128, 8, 16
HC = 2 * H_PEER
SLOTS = H_PEER * TOPK
CH = 128
NCH = SEQ // CH

XBC, XR, KV, Q, Z, G, GATE = 0, 12, 16, 24, 28, 36, 40
NT = 44
Y_SSD, Y_RET, MIX = 16, 24, 28
UNITS = NT + 16 + 16
RING = 4
TILES_L = 1 + NT + 8 + 16

TT = T // 5
NB, BT = 13, T // 13
QUADS = BT // 4
GRP = 4
NG = KEYS // GRP

C_N1, C_N2, C_CW, C_CB, C_D, C_NW, C_BA, C_BI, C_LAM, NCOL = 0, 8, 16, 80, 96, 104, 112, 116, 120, 124
K_COS, K_SIN, K_PERM, K_ID, K_MASK, K_DM, K_GAM, K_TE, K_IOTA, K_ONE, K_FW, NCST = np.cumsum(
    [0, T, T, 128, 128, 128, 4 * CH, 4 * CH, 4, 128, 128, 8]).tolist()
CHEAD = 16

GAMMA_CH = [float((1.0 - 2.0 ** (-5 - h)) ** CH) for h in range(H_RET)]
GAMMA = [float(1.0 - 2.0 ** (-5 - h)) for h in range(H_RET)]
SCALE = D_RET ** -0.5


def decoder_step(nc, x, w, wdt, keys, u_tab, v_tab, cols, heads, cbuf, h0, wblk, s_ssd, s_ret, cst, gates,
                 y, o_ssd_p, o_ret_p, o_tail, o_cbuf, o_lru, o_ssd_s, o_ret_s):
    with ExitStack() as ctx:
        def sb(name, shape):
            return ctx.enter_context(nc.sbuf_tensor(name, shape, F32))

        def sem(name):
            return ctx.enter_context(nc.semaphore(name))

        xT = sb("xT", [128, KT, T])
        hT = sb("hT", [128, KT, T])
        ring = sb("ring", [128, RING, 8, 128])
        C = sb("C", [128, NCST])
        col = sb("col", [128, NCOL])
        head = sb("head", [H_SSD, 2])
        cb = sb("cb", [128, 16, 3, NS])
        cbn = sb("cbn", [128, 16, 3, NS])
        tail = sb("tail", [128, 16, 3])
        lru0 = sb("lru0", [128, 4, NS])
        lruo = sb("lruo", [128, 4, 1 + NS])
        blk = sb("blk", [128, 8, 128])
        wd = sb("wd", [128, 8, 16])
        eps = sb("eps", [128, 1])
        c8 = sb("c8", [128, 6, 4])
        nA = sb("nA", [H_SSD, 1])
        PN = NT * T
        AN = PN + 11312
        AR = sb("AR", [128, AN])
        P = AR[:, 0:PN].rearrange("p (i t) -> p i t", t=T)
        top = [PN]

        def take(shape):
            n = int(np.prod(shape))
            ap = AR[:, top[0]:top[0] + n]
            top[0] += n
            assert top[0] <= AN, (top[0], AN)
            if len(shape) == 2:
                ap = ap.rearrange("p (a b) -> p a b", b=shape[1])
            if len(shape) == 3:
                ap = ap.rearrange("p (a b c) -> p a b c", b=shape[1], c=shape[2])
            return ap

        xc = take((24, CH))
        vdt = take((H_SSD, P_SSD))
        vend = take((H_SSD, P_SSD))
        btok = take((2, CH))
        vtok = take((H_RET, CH))
        kend = take((H_RET, CH))
        sc = take((2, CH))
        mr = take((H_RET, CH))
        dec = take((2, 4, CH))
        ec = take((2, 4, CH))
        cd = take((H_SSD,))
        tok = take((2, H_SSD))
        crow = take((4, CH))
        S = take((H_SSD, P_SSD))
        Sr = take((H_RET, D_RET))
        top[0] = PN
        rs = take((T,))
        cv = take((2, T))
        rt = take((2, T))
        dtr = take((T,))
        top[0] = PN + T
        RW = H_SSD * P_SSD + H_SSD + H_RET * D_RET
        tk_s = take((RW,))
        rm_s = take((RW,))
        st_s_t = [take((H_SSD, P_SSD)) for _ in range(2)]
        sr_s_t = [take((H_RET, D_RET)) for _ in range(2)]
        ab_s = take((H_SSD,))
        sdt = take((H_SSD,))
        R_CUM, R_NCUM, R_DT, R_TE = range(4)

        def row(i):
            return hT[0:H_SSD, i, :]

        qT = P[:, 0:HC, :]
        top[0] = HC * T
        kT = take((HC, KEYS))
        qs = take((HC, TT))
        s_sb = take((HC, KEYS))
        s_top = take((HC, TOPK))
        i_u = take((HC, TOPK)).bitcast(U32)
        i_f = take((HC, TOPK))
        c_top = take((H_PEER, TOPK))
        sel = take((H_PEER, TOPK)).bitcast(U32)
        j_u = take((2, SLOTS)).bitcast(U32)
        j_f = take((2, SLOTS))
        gsum = take((2, H_PEER))
        gij = take((3, SLOTS))
        assert top[0] <= 4 * GRP * D
        top[0] = 4 * GRP * D
        oh = take((SLOTS, TOPK))
        cand = take((H_PEER, TOPK * TOPK))
        top[0] = 4 * GRP * D
        stage = [take((KEYS, BT)) for _ in range(2)]
        Ah = take((8, 128))
        Bh = take((8, 128))
        gijT = take((3, T))
        top[0] = 0
        U = [take((8, GRP * 128)) for _ in range(2)]
        V = [take((GRP, D)) for _ in range(2)]
        gt = [take((NB, GRP * BT)) for _ in range(2)]
        W = [take((GRP, T)) for _ in range(2)]
        gh = take((2, T))

        PS = ctx.enter_context(nc.psum_tensor("PS", [128, 8, 512], F32))
        ident, ones = C[:, K_ID:K_ID + 128], C[:, K_ONE:K_ONE + 128]
        iota = C[:, K_IOTA:K_IOTA + 128]

        def halves(bank):
            return PS[:, bank:bank + 2, 0:HALF]

        def two(ap):
            return ap.rearrange("p (h t) -> p h t", h=2)

        def hs(i):
            return slice(i * HALF, (i + 1) * HALF)

        ld_x, ld_small, ld_keys = sem("ld_x"), sem("ld_small"), sem("ld_keys")
        ld_w = [sem(f"ld_w{i}") for i in range(RING)]
        w_free, pj, pj_free = sem("w_free"), sem("pj"), sem("pj_free")
        n_sq, n_ss, n_rt, n_h = sem("n_sq"), sem("n_ss"), sem("n_rt"), sem("n_h")
        raw, dt_raw = sem("raw"), sem("dt_raw")
        conv, act_x, mixin = sem("conv"), sem("act_x"), sem("mixin")
        rot_p, rot_x = sem("rot_p"), sem("rot_x")
        dt_q, dt_e, dt_r = sem("dt_q"), sem("dt_e"), sem("dt_r")
        ck_x = sem("ck_x")
        ck_t, ck_tok, ck_atok = sem("ck_t"), sem("ck_tok"), sem("ck_atok")
        ck_s, ck_sc, ck_mr = sem("ck_s"), sem("ck_sc"), sem("ck_mr")
        ck_seg, ck_exp, ck_m = sem("ck_seg"), sem("ck_exp"), sem("ck_m")
        ck_y, ck_yr, ck_ye = sem("ck_y"), sem("ck_yr"), sem("ck_ye")
        ck_st, ck_S, st_p = sem("ck_st"), sem("ck_S"), sem("st_p")
        s_t, s_tk = sem("s_t"), sem("s_tk")
        s_rm, s_bc, s_new = sem("s_rm"), sem("s_bc"), sem("s_new")
        s_y, s_ye = sem("s_y"), sem("s_ye")
        ld_s, st_s = [sem("ld_s0"), sem("ld_s1")], [sem("st_s0"), sem("st_s1")]
        yn_y, yn_sq, yn_ss, yn_rt, yn_m = (sem(f"yn_{n}") for n in ("y", "sq", "ss", "rt", "m"))
        lr_p, lr_a, lr_t = sem("lr_p"), sem("lr_a"), sem("lr_t")
        lr_q, lr_r, lr_h = sem("lr_q"), sem("lr_r"), sem("lr_h")
        states_out, small_out = sem("states_out"), sem("small_out")
        x_mid, st_small = sem("x_mid"), sem("st_small")
        q_in, q_cp, q_s, q_sc = sem("q_in"), sem("q_cp"), sem("q_s"), sem("q_sc")
        q_sm, q_ex, q_g = sem("q_sm"), sem("q_ex"), sem("q_g")
        q_tp, q_tr = sem("q_tp"), sem("q_tr")
        g_ab, g_mm, g_cp = sem("g_ab"), sem("g_mm"), sem("g_cp")
        g_out = [sem("g_out0"), sem("g_out1")]
        ld_u, ld_v, ld_g = ([sem(f"ld_{n}{i}") for i in range(2)] for n in "uvg")
        m_h, m_gelu, m_w, m_y, m_acc = (sem(f"m_{n}") for n in ("h", "gelu", "w", "y", "acc"))
        st_y = sem("st_y")
        passed = sem("passed")
        v_seq, a_seq = sem("v_seq"), sem("a_seq")

        def apart(eng):
            eng.sem_inc(passed, 1)

        class Order:

            def __init__(self, eng, s):
                self.eng, self.s, self.n, self.settled = eng, s, 0, 0

            def restart(self):
                assert self.settled == self.n
                apart(self.eng)
                self.eng.sem_clear(self.s)
                self.n = self.settled = 0

            def mark(self, ins):
                ins.then_inc(self.s, 1)
                self.n += 1

            def settle(self):
                self.eng.wait_ge(self.s, self.n)
                self.settled = self.n

            def then(self, ins):
                self.mark(ins)
                self.settle()

        H0, W0, Y0, GE0, ACC0 = 2 * GRP, 2 * GRP, 2 * KT, 2, 2
        block = ctx.enter_context(nc.Block())

        @block.sync
        def _(sp):
            sp.dma_start(C[:, :], cst).then_inc(ld_x, 16)
            sp.dma_start(xT[:, :, :], x).then_inc(ld_x, 16)
            for s, n in ((w_free, RING), (pj_free, 2), (m_h, H0), (m_w, W0), (m_y, Y0), (m_gelu, GE0), (m_acc, ACC0),
                         (g_mm, 2), (g_cp, 2)):
                sp.sem_inc(s, n)
            for s in (small_out, states_out, ck_S, ck_ye, ck_st, ck_m, s_new, s_ye, s_bc, act_x, rot_x, q_s, q_sc, q_g, q_tp,
                      *st_s, *g_out):
                sp.sem_inc(s, 1)
            with sp.Fori(0, DEPTH) as l:
                with sp.Fori(0, UNITS // RING) as g:
                    for s in range(RING):
                        sp.wait_ge(w_free, (l * (UNITS // RING) + g) * RING + s + 1)
                        sp.dma_start(ring[:, s, :, :], w[l, g * RING + s]).then_inc(ld_w[s], 16)
                sp.wait_ge(q_tr, 5 * l + 5)
                apart(sp)
                with sp.Fori(0, NG // 2) as i:
                    for b in range(2):
                        n = l * NG + i * 2 + b
                        sp.wait_ge(m_h, n * GRP + H0 - GRP)
                        sp.dma_start(U[b], u_tab[l, i * 2 + b]).then_inc(ld_u[b], 16)
                        if b == 0:
                            sp.wait_ge(g_out[0], 16 * 7 * (l + 1) + 1)
                            apart(sp)
                            sp.wait_ge(g_out[1], 16 * 6 * (l + 1) + 1)
                            apart(sp)
                        sp.wait_ge(m_w, n * GRP + W0 - GRP)
                        sp.dma_start(gt[b], gates[:, :, bass.ds((i * 2 + b) * GRP * BT, GRP * BT)]
                                     .rearrange("n p c -> p n c")).then_inc(ld_g[b], 16)
                        sp.wait_ge(m_y, n * KT + Y0 - KT)
                        sp.dma_start(V[b], v_tab[l, i * 2 + b]).then_inc(ld_v[b], 16)
            sp.wait_ge(n_h, KT * (2 * DEPTH + 1))
            sp.dma_start(y, hT[:, :, :]).then_inc(st_y, 16)
            sp.wait_ge(st_y, 16)

        @block.gpsimd
        def _(pool):
            with pool.Fori(0, DEPTH) as l:
                pool.wait_ge(m_acc, l * NG * KT + ACC0)
                apart(pool)
                for dst, src in ((col[:, :], cols[l]), (head[:, :], heads[l]), (cb[:, :, :, :], cbuf[l]),
                                 (lru0[:, :, :], h0[l]), (blk[:, :, :], wblk[l]), (wd[:, :, :], wdt[l])):
                    pool.dma_start(dst, src).then_inc(ld_small, 16)
                pool.wait_ge(act_x, 16 * l + 16 + 1)
                pool.wait_ge(rot_x, 8 * l + 8 + 1)
                pool.wait_ge(dt_r, 2 * l + 2)
                apart(pool)
                with pool.Fori(0, NCH) as c:
                    pool.wait_ge(ck_S, 7 * (l * NCH + c) + 1)
                    Pc = P[:, :, 0:SEQ].rearrange("p i (c j) -> p i c j", j=CH)
                    pool.tensor_copy(xc[:, 0:12, :], Pc[:, XBC:XBC + 12, c, :]).then_inc(ck_x, 1)
                    pool.tensor_copy(xc[:, 12:24, :], Pc[:, KV:KV + 12, c, :]).then_inc(ck_x, 1)
                    rows = hT[0:H_SSD, 0:4, 0:SEQ].rearrange("p i (c j) -> p i c j", j=CH)
                    pool.tensor_copy(crow[0:H_SSD, :, :], rows[:, :, c, :]).then_inc(ck_x, 1)
                pool.wait_ge(ck_S, 7 * NCH * (l + 1) + 1)
                apart(pool)
                pool.dma_start(o_ssd_p[l], S.rearrange("p a b -> p (a b)")).then_inc(st_p, 16)
                pool.dma_start(o_ret_p[l], Sr.rearrange("p a b -> p (a b)")).then_inc(st_p, 16)
                with pool.Fori(0, NS // 2) as i:
                    for b in range(2):
                        pool.wait_ge(st_s[b], 32 * (l * (NS // 2) + i) + 1)
                        apart(pool)
                        pool.dma_start(st_s_t[b], s_ssd[l, i * 2 + b]).then_inc(ld_s[b], 16)
                        pool.dma_start(sr_s_t[b], s_ret[l, i * 2 + b]).then_inc(ld_s[b], 16)
                pool.wait_ge(st_p, 32 * l + 32)
                pool.sem_inc(states_out, 1)
                pool.wait_ge(lr_h, 3 * l + 3)
                apart(pool)
                pool.dma_start(o_tail[l], tail[:, :, :]).then_inc(st_small, 16)
                pool.dma_start(o_cbuf[l], cbn[:, :, :, :]).then_inc(st_small, 16)
                pool.dma_start(o_lru[l], lruo[:, :, :]).then_inc(st_small, 16)
                pool.wait_ge(x_mid, KT * l + KT)
                apart(pool)
                pool.dma_start(kT, keys[l]).then_inc(ld_keys, 16)
                pool.wait_ge(st_small, 48 * l + 48)
                pool.sem_inc(small_out, 1)
                pool.wait_ge(q_in, HC * l + HC)
                apart(pool)
                with pool.Fori(0, 5) as t:
                    pool.wait_ge(q_s, l * 5 + t + 1)
                    pool.tensor_copy(qs, qT.rearrange("p h (t c) -> p h t c", c=TT)[:, :, t, :]).then_inc(q_cp, 1)
            pool.wait_ge(st_p, 32 * DEPTH)
            pool.wait_ge(st_small, 48 * DEPTH)

        @block.tensor
        def _(pe):
            mm = pe.matmul

            def sums(src, n_tiles, bank):
                for h in range(2):
                    for k in range(n_tiles):
                        last = mm(PS[:, bank + h, 0:HALF], ones, src[:, k, hs(h)], start=(k == 0), stop=(k == n_tiles - 1))
                return last

            def unit(l, g, s, b, k0, k1, src, first=True, final=True):
                pe.wait_ge(ld_w[s], (l * (UNITS // RING) + g) * 16 + 16)
                for h in range(2):
                    for k in range(8):
                        last = mm(PS[:, 2 * b + h, 0:HALF], ring[:, s, k, :], src[:, k0 + k, hs(h)],
                                  start=(first and k == 0), stop=(final and k == 7), skip_group_check=True)
                return last

            pe.wait_ge(ld_x, 32)
            with pe.Fori(0, DEPTH) as l:
                tile0 = l * TILES_L
                pe.wait_ge(n_sq, 2 * l + 1)
                sums(hT, KT, 4).then_inc(n_ss, 1)
                pe.wait_ge(n_h, (2 * l + 1) * KT)
                pe.wait_ge(ld_small, 96 * l + 96)
                pe.wait_ge(pj_free, tile0 + 1)
                for h in range(2):
                    for k in range(KT):
                        last = mm(PS[0:H_SSD, 6 + h, 0:HALF], wd[:, k, :], hT[:, k, hs(h)], start=(k == 0), stop=(k == KT - 1))
                last.then_inc(pj, 1)
                with pe.Fori(0, NT // RING) as g:
                    for s in range(RING):
                        pe.wait_ge(pj_free, tile0 + g * RING + s + 2)
                        unit_last = unit(l, g, s, s % 2, 0, 8, hT)
                        unit_last.then_inc(pj, 1)
                pe.wait_ge(pj_free, tile0 + 1 + NT + 2)
                apart(pe)
                with pe.Fori(0, 4) as i:
                    for j, t0 in enumerate((KV, Q)):
                        pe.wait_ge(rot_x, l * 8 + i * 2 + 1)
                        for h in range(2):
                            last = mm(PS[:, 2 * j + h, 0:HALF], C[:, K_PERM:K_PERM + 128],
                                      P[:, t0 + i, hs(h)], start=True, stop=True)
                        last.then_inc(rot_p, 1)
                with pe.Fori(0, NCH) as c:
                    it = l * NCH + c
                    pe.wait_ge(ck_x, 3 * it + 3)
                    pe.wait_ge(ck_ye, 2 * it + 1)
                    pe.wait_ge(ck_S, 7 * it + 1)
                    for i in range(8):
                        pe.transpose(PS[:, i // 4, (i % 4) * CH:(i % 4 + 1) * CH], xc[:, i, :], ident)
                    for i in range(2):
                        pe.transpose(PS[:, 2, i * CH:(i + 1) * CH], xc[:, 8 + i, :], ident)
                    for i in range(4):
                        pe.transpose(PS[:, 3, i * CH:(i + 1) * CH], xc[:, 12 + i, :], ident)
                    for i in range(4):
                        pe.transpose(PS[:, 4, i * CH:(i + 1) * CH], xc[:, 16 + i, :], ident)
                    for i in range(2):
                        last = pe.transpose(PS[:, 7, i * H_SSD:(i + 1) * H_SSD], crow[0:H_SSD, R_DT + i, :], C[0:H_SSD, K_ID:K_ID + H_SSD])
                    last.then_inc(ck_t, 1)
                    for g in range(2):
                        mm(PS[:, 5, g * CH:(g + 1) * CH], xc[:, 8 + g, :], xc[:, 10 + g, :], start=True, stop=True)
                    for h in range(H_RET):
                        last = mm(PS[:, 6, h * CH:(h + 1) * CH], xc[:, 12 + h, :], xc[:, 20 + h, :], start=True, stop=True)
                    last.then_inc(ck_s, 1)

                    def decays(q):
                        if q == 0:
                            pe.wait_ge(ck_tok, 4 * it + 1)
                            pe.wait_ge(ck_atok, 2 * it + 1)
                        elif q == 1:
                            pe.wait_ge(ck_mr, 2 * it + 1)
                            pe.wait_ge(ck_tok, 4 * it + 4)
                        else:
                            pe.wait_ge(ck_exp, 8 * it + 2 * (q - 1))
                        seg, cum = 7 - q % 2, 2 + q % 2
                        mm(PS[:, seg, :], ident, C[:, K_MASK:K_MASK + CH].unsqueeze(1).to_broadcast([128, 4, CH]),
                           start=True, stop=False, skip_group_check=True)
                        for r in range(4):
                            h = 4 * q + r
                            pick = C[0:H_SSD, K_ID + h:K_ID + h + 1].to_broadcast([H_SSD, CH])
                            o = slice(r * CH, (r + 1) * CH)
                            mm(PS[:, seg, o], pick, crow[0:H_SSD, 0, :], start=False, stop=False, skip_group_check=True)
                            mm(PS[:, seg, o], crow[0:H_SSD, 1, :], pick, start=False, stop=(r == 3), skip_group_check=True)
                            last = mm(PS[:, cum, o], pick, crow[0:H_SSD, 0, :], start=True, stop=True)
                        last.then_inc(ck_seg, 1)

                    def outputs(q):
                        pe.wait_ge(ck_m, 12 * it + 3 * q + 3 + 1)
                        if q == 0:
                            pe.wait_ge(ck_tok, 4 * it + 3)
                        for r in range(4):
                            h = 4 * q + r
                            p0 = 64 * (h % 2)
                            o = PS[p0:p0 + 64, h // 8, (h // 2 % 4) * CH:(h // 2 % 4 + 1) * CH]
                            mm(o, vdt[:, h, :], dec[:, q % 2, r, :], start=True, stop=False, skip_group_check=True)
                            last = mm(o, S[:, h, :], ec[:, q % 2, r, :], start=False, stop=True, skip_group_check=True)
                        last.then_inc(ck_y, 1)

                    decays(0)
                    decays(1)
                    outputs(0)
                    decays(2)
                    outputs(1)
                    decays(3)
                    outputs(2)
                    outputs(3)
                    pe.wait_ge(ck_atok, 2 * it + 2)
                    pe.wait_ge(ck_mr, 2 * it + 2)
                    for h in range(H_RET):
                        o = PS[:, 4, h * CH:(h + 1) * CH]
                        mm(o, vtok[:, h, :], mr[:, h, :], start=True, stop=False, skip_group_check=True)
                        last = mm(o, Sr[:, h, :], xc[:, 20 + h, :], start=False, stop=True, skip_group_check=True)
                    last.then_inc(ck_yr, 1)
                    pe.wait_ge(ck_sc, it + 1)
                    pe.wait_ge(ck_exp, 8 * it + 8)
                    for g in range(2):
                        mm(PS[:, (5, 2)[g], :], btok[:, g, :], vend[:, 8 * g:8 * g + 8, :], start=True, stop=True)
                    for h in range(H_RET):
                        last = mm(PS[:, 3, h * CH:(h + 1) * CH], kend[:, h, :], vtok[:, h, :], start=True, stop=True)
                    last.then_inc(ck_st, 1)
                pe.wait_ge(ck_ye, 2 * NCH * (l + 1) + 1)
                pe.wait_ge(ck_S, 7 * NCH * (l + 1) + 1)
                for i in range(8):
                    pe.transpose(PS[0:NS, i // 4, (i % 4) * 128:(i % 4 + 1) * 128], P[:, XBC + i, SEQ:T], ident)
                for i in range(4):
                    pe.transpose(PS[0:NS, 2, i * 128:(i + 1) * 128], P[:, KV + 4 + i, SEQ:T], ident)
                for i, r in enumerate((R_DT, R_CUM)):
                    last = pe.transpose(PS[0:NS, 3, i * H_SSD:(i + 1) * H_SSD], row(r)[:, SEQ:T], C[0:H_SSD, K_ID:K_ID + H_SSD])
                last.then_inc(s_t, 1)
                with pe.Fori(0, NS // 2) as i:
                    for b in range(2):
                        n = l * NS + i * 2 + b
                        pe.wait_ge(s_rm, n + 1)
                        pe.wait_ge(s_new, n + 1)
                        one = C[0:NS, K_ONE:K_ONE + 128]
                        mm(PS[:, 7, 0:H_SSD], one, rm_s[0:NS, D:D + H_SSD], start=True, stop=True)
                        for g in range(2):
                            mm(PS[:, 4 + g, :], one, rm_s[0:NS, g * 512:(g + 1) * 512], start=True, stop=True)
                        mm(PS[:, 6, :], one, rm_s[0:NS, D + H_SSD:RW], start=True, stop=True).then_inc(s_bc, 1)
                        pe.wait_ge(s_new, n + 1 + 1)
                        pe.wait_ge(s_ye, n + 1)
                        cur = bass.ds(i * 2 + b + SEQ, 1)
                        for j in range(8):
                            mm(PS[:, 3, j:j + 1], st_s_t[b][:, 2 * j:2 * j + 2, :], P[:, XBC + 10 + j // 4, cur],
                               start=True, stop=True, skip_group_check=True)
                        for h in range(H_RET):
                            last = mm(PS[:, 3, 8 + h:9 + h], sr_s_t[b][:, h, :], P[:, Q + h, cur],
                                      start=True, stop=True, skip_group_check=True)
                        last.then_inc(s_y, 1)
                pe.wait_ge(yn_sq, 2 * l + 1)
                sums(hT, KT, 0).then_inc(yn_ss, 1)
                pe.wait_ge(yn_sq, 2 * l + 2)
                for h in range(H_RET):
                    mm(PS[:, 2 + h, :], ones, hT[:, h, 0:SEQ], start=True, stop=True)
                for h in range(H_RET):
                    last = mm(PS[:, 6, h * NS:(h + 1) * NS], ones, hT[:, h, SEQ:T], start=True, stop=True)
                last.then_inc(yn_ss, 1)
                pe.wait_ge(yn_rt, 3 * l + 3)
                for i in range(4):
                    for j in range(2):
                        n = 2 * i + j
                        if n >= 4:
                            pe.wait_ge(lr_a, 8 * l + n - 3)
                        for h in range(2):
                            last = mm(PS[:, 2 * (n % 4) + h, 0:HALF], blk[:, 4 * j + i, :], P[:, XR + i, hs(h)],
                                      start=True, stop=True)
                        last.then_inc(lr_p, 1)
                pe.wait_ge(lr_a, 8 * l + 8)
                pe.wait_ge(yn_m, 9 * l + 9)
                pe.wait_ge(lr_h, 3 * l + 3)
                apart(pe)
                with pe.Fori(0, 4) as g:
                    for s in range(RING):
                        m = s // 2
                        if s % 2 == 0:
                            pe.wait_ge(pj_free, tile0 + NT + 1 + g * 2 + m + 1)
                        last = unit(l, NT // RING + g, s, m, MIX + 8 * (s % 2), None, P, first=(s % 2 == 0), final=(s % 2 == 1))
                        if s % 2:
                            last.then_inc(pj, 1)
                pe.wait_ge(n_sq, 2 * l + 2)
                sums(hT, KT, 4).then_inc(n_ss, 1)
                pe.wait_ge(n_h, (2 * l + 2) * KT)
                apart(pe)
                with pe.Fori(0, 4) as g:
                    for s in range(RING):
                        pe.wait_ge(pj_free, tile0 + NT + 9 + g * RING + s + 1)
                        unit(l, NT // RING + 4 + g, s, s % 2, 0, 8, hT).then_inc(pj, 1)
                pe.wait_ge(ld_keys, 16 * l + 16)
                pe.wait_ge(pj_free, tile0 + TILES_L + 2)
                apart(pe)
                with pe.Fori(0, 5) as t:
                    n = l * 5 + t
                    pe.wait_ge(q_cp, n + 1)
                    pe.wait_ge(q_sc, n + 1)
                    for j in range(HC):
                        last = mm(PS[0:TT, j // 4, (j % 4) * KEYS:(j % 4 + 1) * KEYS], qs[:, j, :], kT[:, j, :], start=True, stop=True)
                    last.then_inc(q_s, 1)
                    pe.wait_ge(q_g, n + 1 + 1)
                    for j in range(3):
                        last = pe.transpose(PS[:, 4, j * TT:(j + 1) * TT], gij[0:TT, j, :], C[0:TT, K_ID:K_ID + TT])
                    last.then_inc(q_tp, 1)

                def gate_block(n):
                    for q in range(QUADS):
                        pe.wait_ge(g_cp, n * QUADS + q + 1)
                        pe.wait_ge(g_ab, (n * QUADS + q) * 8 + 8)
                        for r in range(4):
                            s = (4 * q + r) % 8
                            last = mm(PS[:, 5 + q % 2, r * KEYS:(r + 1) * KEYS], Bh[:, s, :], Ah[:, s, :], start=True, stop=True)
                        last.then_inc(g_mm, 1)

                with pe.Fori(0, NB // 2) as i:
                    gate_block(l * NB + i * 2)
                    gate_block(l * NB + i * 2 + 1)
                gate_block(l * NB + NB - 1)
                pe.wait_ge(g_cp, NB * QUADS * (l + 1) + 2)

                def products(n, b, loads):
                    pe.wait_ge(ld_u[b], 16 * loads)
                    for e in range(GRP):
                        pe.wait_ge(m_gelu, n * GRP + e + GE0 - 1)
                        for h in range(2):
                            for k in range(KT):
                                last = mm(PS[:, 2 * (e % 2) + h, 0:HALF], U[b][:, k, e * 128:(e + 1) * 128],
                                          hT[:, k, hs(h)], start=(k == 0), stop=(k == KT - 1))
                        last.then_inc(m_h, 1)

                def results(n, b, loads):
                    pe.wait_ge(ld_v[b], 16 * loads)
                    pe.wait_ge(m_w, n * GRP + GRP + W0)
                    for d in range(KT):
                        pe.wait_ge(m_acc, n * KT + d + ACC0 - 1)
                        for h in range(2):
                            for e in range(GRP):
                                last = mm(PS[:, 4 + 2 * (d % 2) + h, 0:HALF], V[b][:, e, d * 128:(d + 1) * 128],
                                          W[b][:, e, hs(h)], start=(e == 0), stop=(e == GRP - 1))
                        last.then_inc(m_y, 1)

                n0, ld0 = l * NG, l * (NG // 2)
                products(n0, 0, ld0 + 1)
                with pe.Fori(0, NG // 2 - 1) as i:
                    products(n0 + i * 2 + 1, 1, ld0 + i + 1)
                    results(n0 + i * 2, 0, ld0 + i + 1)
                    products(n0 + i * 2 + 2, 0, ld0 + i + 2)
                    results(n0 + i * 2 + 1, 1, ld0 + i + 1)
                products(n0 + NG - 1, 1, ld0 + NG // 2)
                results(n0 + NG - 2, 0, ld0 + NG // 2)
                results(n0 + NG - 1, 1, ld0 + NG // 2)
            pe.wait_ge(n_sq, 2 * DEPTH + 1)
            sums(hT, KT, 4).then_inc(n_ss, 1)

        @block.scalar
        def _(act):
            A = act.activation
            own = Order(act, a_seq)

            def norm(m):
                A(hT[:, :, :], xT[:, :, :], ACT.Square).then_inc(n_sq, 1)
                act.wait_ge(n_ss, m + 1)
                A(two(rs), halves(4), ACT.Sqrt, bias=eps[:, 0:1], scale=1.0 / D).then_inc(n_rt, 1)

            act.wait_ge(ld_x, 32)
            act.wait_ge(dt_q, 1)
            with act.Fori(0, DEPTH) as l:
                own.restart()
                tile0 = l * TILES_L
                act.wait_ge(m_acc, l * NG * KT + ACC0)
                norm(2 * l)
                act.wait_ge(pj, tile0 + 1)
                A(two(dtr[0:H_SSD, :]), PS[0:H_SSD, 6:8, 0:HALF], ACT.Copy).then_inc(dt_raw, 1)

                def take_tile(g, s, func, done):
                    act.wait_ge(pj, tile0 + g * RING + s + 2)
                    own.then(A(two(P[:, g * RING + s, :]), halves(2 * (s % 2)), func))
                    act.sem_inc(pj_free, 1)
                    act.sem_inc(w_free, 1)
                    act.sem_inc(done, 1)

                def activate(g, s, func):
                    act.wait_ge(conv, 16 * l + g * RING + s + 1)
                    A(P[:, g * RING + s, :], cv[:, s % 2, :], func).then_inc(act_x, 1)

                def group_loop(a, b, func, done, post=None, post_func=None):
                    with act.Fori(a, b) as g:
                        own.restart()
                        for s in range(RING):
                            take_tile(g, s, func, done)
                            if post is not None:
                                activate(g - post, s, post_func)

                act.sem_inc(pj_free, 1)
                group_loop(0, 4, ACT.Copy, raw)
                group_loop(4, 7, ACT.Copy, raw, 4, ACT.Silu)
                group_loop(7, 8, ACT.Silu, mixin, 4, ACT.Copy)
                group_loop(8, 10, ACT.Silu, mixin)
                group_loop(10, 11, ACT.Gelu, mixin)
                act.wait_ge(dt_q, 2 * l + 2)
                A(row(5), row(5), ACT.Exp, scale=-1.0).then_inc(dt_e, 1)
                A(c8[:, 1, :], c8[:, 1, :], ACT.Exp, scale=-1.0).then_inc(dt_e, 1)
                A(nA[:, :], head[:, 1:2], ACT.Exp).then_inc(dt_e, 1)
                act.wait_ge(dt_q, 2 * l + 3)
                A(row(R_TE)[:, 0:SEQ], row(R_TE)[:, 0:SEQ], ACT.Exp).then_inc(dt_e, 1)
                A(row(R_CUM)[:, SEQ:T], row(4)[:, SEQ:T], ACT.Exp).then_inc(dt_e, 1)
                with act.Fori(0, NCH) as c:
                    it = l * NCH + c
                    act.wait_ge(ck_t, it + 1)
                    act.wait_ge(ck_st, it + 1)
                    A(btok.rearrange("p a b -> p (a b)"), PS[:, 2, 0:2 * CH], ACT.Copy).then_inc(ck_atok, 1)
                    A(vtok.rearrange("p a b -> p (a b)"), PS[:, 4, :], ACT.Copy).then_inc(ck_atok, 1)
                    act.wait_ge(ck_s, it + 1)
                    act.wait_ge(ck_m, 12 * it + 1)
                    A(sc.rearrange("p a b -> p (a b)"), PS[:, 5, 0:2 * CH], ACT.Copy).then_inc(ck_sc, 1)
                    for q in range(4):
                        act.wait_ge(ck_seg, 4 * it + q + 1)
                        if q >= 2:
                            act.wait_ge(ck_y, 4 * it + q - 1)
                            act.wait_ge(ck_m, 12 * it + 3 * (q - 1) + 1)
                        A(dec[:, q % 2, :, :].rearrange("p a b -> p (a b)"), PS[:, 7 - q % 2, :], ACT.Exp).then_inc(ck_exp, 1)
                        A(ec[:, q % 2, :, :].rearrange("p a b -> p (a b)"), PS[:, 2 + q % 2, :], ACT.Exp).then_inc(ck_exp, 1)
                    act.wait_ge(ck_y, 4 * it + 4)
                    Pc = P[:, :, 0:SEQ].rearrange("p i (c j) -> p i c j", j=CH)
                    A(Pc[:, Y_SSD:Y_SSD + 8, c, :], PS[:, 0:2, :].rearrange("p b (i j) -> p (b i) j", j=CH), ACT.Copy).then_inc(ck_ye, 1)
                    act.wait_ge(ck_yr, it + 1)
                    A(Pc[:, Y_RET:Y_RET + 4, c, :], PS[:, 4, :].rearrange("p (i j) -> p i j", j=CH), ACT.Copy).then_inc(ck_ye, 1)
                with act.Fori(0, NS // 2) as i:
                    for b in range(2):
                        n = l * NS + i * 2 + b
                        act.wait_ge(s_y, n + 1)
                        act.dma_start(o_ssd_s[l, i * 2 + b], st_s_t[b].rearrange("p a b -> p (a b)")).then_inc(st_s[b], 16)
                        act.dma_start(o_ret_s[l, i * 2 + b], sr_s_t[b].rearrange("p a b -> p (a b)")).then_inc(st_s[b], 16)
                        A(P[:, Y_SSD:Y_SSD + 12, bass.ds(i * 2 + b + SEQ, 1)], PS[:, 3, 0:12].unsqueeze(2), ACT.Copy).then_inc(s_ye, 1)
                act.wait_ge(yn_y, l + 1)
                A(hT[:, :, :], P[:, Y_SSD:Y_SSD + 8, :], ACT.Square).then_inc(yn_sq, 1)
                act.wait_ge(yn_ss, 2 * l + 1)
                A(two(rs), halves(0), ACT.Sqrt, bias=eps[:, 0:1], scale=1.0 / D).then_inc(yn_rt, 1)
                A(hT[:, 0:4, :], P[:, Y_RET:Y_RET + 4, :], ACT.Square).then_inc(yn_sq, 1)
                act.wait_ge(yn_ss, 2 * l + 2)
                A(P[:, 0:4, 0:SEQ], PS[:, 2:6, :], ACT.Sqrt, bias=eps[:, 0:1], scale=1.0 / D_RET).then_inc(yn_rt, 1)
                A(P[:, 0:4, SEQ:T], PS[:, 6, 0:4 * NS].rearrange("p (h s) -> p h s", s=NS), ACT.Sqrt,
                  bias=eps[:, 0:1], scale=1.0 / D_RET).then_inc(yn_rt, 1)
                for i in range(4):
                    for j in range(2):
                        n = 2 * i + j
                        act.wait_ge(lr_p, 8 * l + n + 1)
                        b = 2 * (n % 4)
                        A(two(hT[:, 4 * j + i, :]), halves(b), ACT.Sigmoid,
                          bias=col[:, (C_BA, C_BI)[j] + i:(C_BA, C_BI)[j] + i + 1]).then_inc(lr_a, 1)
                act.wait_ge(lr_a, 8 * l + 8)
                for i in range(4):
                    A(P[:, 4 + i, :], hT[:, i, :], ACT.Exp, scale=c8[:, 4, i:i + 1]).then_inc(lr_t, 1)
                    A(P[:, 8 + i, :], hT[:, i, :], ACT.Tanh, scale=c8[:, 5, i:i + 1]).then_inc(lr_t, 1)
                act.wait_ge(lr_q, l + 1)
                A(P[:, 8:12, :], P[:, 8:12, :], ACT.Sqrt).then_inc(lr_r, 1)
                act.wait_ge(x_mid, KT * l + KT)
                norm(2 * l + 1)
                for b in range(2):
                    act.wait_ge(st_s[b], 32 * (NS // 2) * (l + 1) + 1)
                apart(act)
                with act.Fori(0, 4) as g:
                    own.restart()
                    for s in range(RING):
                        act.wait_ge(pj, tile0 + NT + 9 + g * RING + s + 1)
                        own.then(A(two(qT[:, g * RING + s, :]), halves(2 * (s % 2)), ACT.Copy))
                        act.sem_inc(pj_free, 1)
                        act.sem_inc(w_free, 1)
                        act.sem_inc(q_in, 1)
                with act.Fori(0, 5) as t:
                    n = l * 5 + t
                    act.wait_ge(q_s, n + 1 + 1)
                    act.wait_ge(q_g, n + 1)
                    A(s_sb[0:TT, :, :].rearrange("p a b -> p (a b)"), PS[0:TT, 0:4, :].rearrange("p a b -> p (a b)"), ACT.Copy).then_inc(q_sc, 1)
                    act.wait_ge(q_sm, n + 1)
                    A(gij[0:TT, 0, :], gij[0:TT, 0, :], ACT.Exp).then_inc(q_ex, 1)
                    act.wait_ge(q_tp, n + 1 + 1)
                    A(gijT.rearrange("p a (t c) -> p a t c", c=TT)[:, :, t, :],
                      PS[:, 4, 0:3 * TT].rearrange("p (a c) -> p a c", a=3), ACT.Copy).then_inc(q_tr, 1)

                def gate_block(n, blk_i, b, stored):
                    act.wait_ge(g_out[b], stored + 1)
                    for q in range(QUADS):
                        act.wait_ge(g_mm, n * QUADS + q + 1 + 2)
                        A(stage[b][:, :, 4 * q:4 * q + 4].rearrange("p k t -> p t k"),
                          PS[:, 5 + q % 2, :].rearrange("p (t k) -> p t k", k=KEYS), ACT.Copy).then_inc(g_cp, 1)
                    act.wait_ge(g_cp, n * QUADS + QUADS + 2)
                    act.dma_start(gates[blk_i], stage[b].rearrange("p k t -> p (k t)")).then_inc(g_out[b], 16)

                with act.Fori(0, NB // 2) as i:
                    gate_block(l * NB + i * 2, i * 2, 0, 16 * (7 * l + i))
                    gate_block(l * NB + i * 2 + 1, i * 2 + 1, 1, 16 * (6 * l + i))
                gate_block(l * NB + NB - 1, NB - 1, 0, 16 * (7 * l + 6))
                act.wait_ge(g_out[0], 16 * 7 * (l + 1) + 1)
                act.wait_ge(g_out[1], 16 * 6 * (l + 1) + 1)
                with act.Fori(0, NG) as i:
                    n = (l * NG + i) * GRP
                    for e in range(GRP):
                        act.wait_ge(m_h, n + e + 1 + H0)
                        act.wait_ge(m_w, n + e + W0 - 1)
                        A(two(gh[:, e % 2, :]), halves(2 * (e % 2)), ACT.Gelu).then_inc(m_gelu, 1)
            act.wait_ge(m_acc, DEPTH * NG * KT + ACC0)
            norm(2 * DEPTH)
            for b in range(2):
                act.wait_ge(st_s[b], 32 * DEPTH * (NS // 2) + 1)

        @block.vector
        def _(dve):
            own = Order(dve, v_seq)
            ts, tt, stt = dve.tensor_scalar, dve.tensor_tensor, dve.scalar_tensor_tensor

            def norm(m, w_col):
                dve.wait_ge(n_rt, m + 1)
                own.then(dve.reciprocal(rs, rs))
                for k in range(KT):
                    stt(hT[:, k, :], xT[:, k, :], w_col[:, k:k + 1], rs, ALU.mult, ALU.mult).then_inc(n_h, 1)

            def log1p_of(e, s, w, acc):
                own.then(ts(s, e, 2.0, None, ALU.add))
                own.then(dve.reciprocal(s, s))
                own.then(tt(s, e, s, ALU.mult))
                own.then(tt(w, s, s, ALU.mult))
                own.then(ts(acc, w, 1.0 / 17, None, ALU.mult))
                for k in (15, 13, 11, 9, 7, 5, 3):
                    own.then(stt(acc, acc, 1.0 / k, w, ALU.add, ALU.mult))
                own.then(stt(acc, acc, 1.0, s, ALU.add, ALU.mult))

            dve.memset(eps[:, :], EPS).then_inc(dt_q, 1)
            dve.wait_ge(ld_x, 32)
            with dve.Fori(0, DEPTH) as l:
                own.restart()
                tile0 = l * TILES_L
                dve.wait_ge(ld_small, 96 * l + 96)
                norm(2 * l, col[:, C_N1:C_N1 + 8])
                dve.wait_ge(small_out, l + 1)
                for tap in range(2):
                    own.mark(dve.tensor_copy(cbn[:, :, tap, :], cb[:, :, tap + 1, :]))
                own.settle()
                cw = col[:, C_CW:C_CW + 64].rearrange("p (i k) -> p i k", k=4)
                with dve.Fori(0, 4) as g:
                    own.restart()
                    for s in range(RING):
                        i = g * RING + s
                        X, o = P[:, i, :], cv[:, s % 2, :]
                        dve.wait_ge(raw, 28 * l + i + 1)
                        if s < 2:
                            dve.wait_ge(act_x, 16 * l + g * RING + 1)
                        else:
                            dve.wait_ge(act_x, 16 * l + i - 1 + 1)
                        own.then(ts(o, X, cw[:, i, 3:4], col[:, bass.ds(i + C_CB, 1)], ALU.mult, ALU.add))
                        for tap in range(3):
                            back = 3 - tap
                            own.mark(stt(o[:, back:SEQ], X[:, 0:SEQ - back], cw[:, i, tap:tap + 1], o[:, back:SEQ], ALU.mult, ALU.add))
                            own.then(stt(o[:, SEQ:T], cb[:, i, tap, :], cw[:, i, tap:tap + 1], o[:, SEQ:T], ALU.mult, ALU.add))
                        own.mark(dve.tensor_copy(tail[:, i, :], X[:, SEQ - 3:SEQ]))
                        own.then(dve.tensor_copy(cbn[:, i, 2, :], X[:, SEQ:T]))
                        dve.sem_inc(conv, 1)
                own.restart()
                dve.wait_ge(raw, 28 * l + 28)
                apart(dve)
                with dve.Fori(0, 4) as i:
                    own.restart()
                    for j, t0 in enumerate((KV, Q)):
                        X = P[:, t0 + i, :]
                        dve.wait_ge(rot_p, 8 * l + i * 2 + j + 1)
                        own.mark(tt(two(rt[:, j, :]), halves(2 * j), two(C[:, K_SIN:K_SIN + T]), ALU.mult))
                        own.then(tt(X, X, C[:, K_COS:K_COS + T], ALU.mult))
                        tt(X, X, rt[:, j, :], ALU.add).then_inc(rot_x, 1)
                own.restart()
                dve.wait_ge(dt_raw, l + 1)
                lam = col[:, C_LAM:C_LAM + 4]
                own.then(ts(row(4), dtr[0:H_SSD, :], head[:, 0:1], None, ALU.add))
                own.then(stt(row(5), row(4), -1.0, row(4), ALU.mult, ALU.max))
                own.mark(ts(row(4), row(4), 0.0, None, ALU.max))
                own.mark(ts(c8[:, 0, :], lam, -1.0, 0.0, ALU.mult, ALU.max))
                own.then(stt(c8[:, 1, :], lam, -1.0, lam, ALU.mult, ALU.max))
                dve.sem_inc(dt_q, 1)
                dve.wait_ge(dt_e, 5 * l + 3)
                log1p_of(row(5), row(6), row(7), row(2))
                own.then(stt(row(R_DT), row(2), 2.0, row(4), ALU.mult, ALU.add))
                log1p_of(c8[:, 1, :], c8[:, 2, :], c8[:, 3, :], c8[:, 5, :])
                own.then(stt(c8[:, 0, :], c8[:, 5, :], 2.0, c8[:, 0, :], ALU.mult, ALU.add))
                own.mark(ts(c8[:, 4, :], c8[:, 0, :], -8.0, None, ALU.mult))
                own.mark(ts(c8[:, 5, :], c8[:, 0, :], 8.0, None, ALU.mult))
                own.then(ts(nA[:, :], nA[:, :], -1.0, None, ALU.mult))
                own.then(ts(row(4), row(R_DT), nA[:, 0:1], None, ALU.mult))
                for c in range(NCH):
                    o = slice(c * CH, (c + 1) * CH)
                    own.mark(dve.tensor_tensor_scan(row(R_CUM)[:, o], C[0:H_SSD, K_ONE:K_ONE + CH], row(4)[:, o], 0.0, ALU.mult, ALU.add))
                own.settle()
                cum4 = row(R_CUM)[:, 0:SEQ].rearrange("p (c j) -> p c j", j=CH)
                own.mark(ts(row(R_NCUM)[:, 0:SEQ], row(R_CUM)[:, 0:SEQ], -1.0, None, ALU.mult))
                own.then(tt(row(R_TE)[:, 0:SEQ].rearrange("p (c j) -> p c j", j=CH),
                            cum4[:, :, CH - 1:CH].to_broadcast([H_SSD, NCH, CH]), cum4, ALU.subtract))
                dve.sem_inc(dt_q, 1)
                dve.wait_ge(dt_e, 5 * l + 5)
                tt(row(R_TE)[:, 0:SEQ], row(R_TE)[:, 0:SEQ], row(R_DT)[:, 0:SEQ], ALU.mult).then_inc(dt_r, 1)
                dve.wait_ge(states_out, l + 1)
                own.mark(dve.memset(S, 0.0))
                own.then(dve.memset(Sr, 0.0))
                dve.sem_inc(dt_r, 1)
                with dve.Fori(0, NCH) as c:
                    own.restart()
                    it = l * NCH + c
                    bc = lambda ap, n: ap.unsqueeze(2).to_broadcast([128, ap.shape[1], n])
                    X = PS[:, 0:2, :].rearrange("p b (h q) -> p (b h) q", q=P_SSD)
                    dve.wait_ge(ck_t, it + 1)
                    own.then(dve.tensor_copy(tok, PS[:, 7, 0:2 * H_SSD].rearrange("p (a h) -> p a h", a=2)))
                    dve.sem_inc(ck_tok, 1)
                    tt(vdt, X, bc(tok[:, 0, :], P_SSD), ALU.mult).then_inc(ck_tok, 1)
                    tt(vend, X, bc(tok[:, 1, :], P_SSD), ALU.mult).then_inc(ck_tok, 1)
                    tt(kend, PS[:, 3, :].rearrange("p (h j) -> p h j", j=CH), bc(C[:, K_TE:K_TE + 4], CH), ALU.mult).then_inc(ck_tok, 1)
                    dve.wait_ge(ck_s, it + 1)
                    tt(mr, PS[:, 6, :].rearrange("p (h j) -> p h j", j=CH), C[:, K_DM:K_DM + 4 * CH].rearrange("p (h j) -> p h j", j=CH),
                       ALU.mult).then_inc(ck_mr, 1)
                    tt(xc[:, 20:24, :], xc[:, 20:24, :], C[:, K_GAM:K_GAM + 4 * CH].rearrange("p (h j) -> p h j", j=CH),
                       ALU.mult).then_inc(ck_mr, 1)
                    dve.wait_ge(ck_sc, it + 1)
                    for q in range(4):
                        g = q // 2
                        dve.wait_ge(ck_exp, 8 * it + 2 * q + 2)
                        dve.tensor_copy(cd[:, 4 * q:4 * q + 4].unsqueeze(2), ec[:, q % 2, :, CH - 1:CH]).then_inc(ck_m, 1)
                        dve.wait_ge(ck_m, 12 * it + 3 * q + 1 + 1)
                        tt(dec[:, q % 2, :, :], dec[:, q % 2, :, :], sc[:, g:g + 1, :].to_broadcast([128, 4, CH]), ALU.mult).then_inc(ck_m, 1)
                        tt(ec[:, q % 2, :, :], ec[:, q % 2, :, :], xc[:, 10 + g:11 + g, :].to_broadcast([128, 4, CH]), ALU.mult).then_inc(ck_m, 1)
                    dve.wait_ge(ck_st, it + 1 + 1)
                    own.then(tt(S, S, bc(cd, P_SSD), ALU.mult))
                    for g in range(2):
                        tt(S[:, 8 * g:8 * g + 8, :], S[:, 8 * g:8 * g + 8, :],
                           PS[:, (5, 2)[g], :].rearrange("p (h q) -> p h q", q=P_SSD), ALU.add).then_inc(ck_S, 1)
                    for h in range(H_RET):
                        stt(Sr[:, h, :], Sr[:, h, :], GAMMA_CH[h], PS[:, 3, h * CH:(h + 1) * CH], ALU.mult, ALU.add).then_inc(ck_S, 1)
                    dve.wait_ge(ck_S, 7 * it + 6 + 1)
                    dve.sem_inc(ck_S, 1)
                own.restart()
                dve.wait_ge(s_t, l + 1)
                own.mark(dve.tensor_copy(sdt[0:NS, :], PS[0:NS, 3, 0:H_SSD]))
                own.mark(dve.tensor_copy(tk_s[0:NS, D:D + H_SSD], PS[0:NS, 3, H_SSD:2 * H_SSD]))
                own.then(ts(tk_s[0:NS, D + H_SSD:RW], PS[0:NS, 2, :], SCALE, None, ALU.mult))
                own.then(tt(tk_s[0:NS, 0:D].rearrange("p (h q) -> p h q", q=P_SSD), PS[0:NS, 0:2, :].rearrange("p b (h q) -> p (b h) q", q=P_SSD),
                            sdt[0:NS, :].unsqueeze(2).to_broadcast([NS, H_SSD, P_SSD]), ALU.mult))
                with dve.Fori(0, NS // 2) as i:
                    for b in range(2):
                        own.restart()
                        n = l * NS + i * 2 + b
                        cur = bass.ds(i * 2 + b + SEQ, 1)
                        s, r = st_s_t[b], sr_s_t[b]
                        dve.wait_ge(s_bc, n + 1)
                        ts(rm_s[0:NS, :], tk_s[0:NS, :], C[0:NS, bass.ds(i * 2 + b + K_ID, 1)], None, ALU.mult).then_inc(s_rm, 1)
                        dve.wait_ge(ld_s[b], 32 * (l * (NS // 2) + i + 1))
                        for h in range(H_RET):
                            own.mark(ts(r[:, h, :], r[:, h, :], GAMMA[h], None, ALU.mult))
                        dve.wait_ge(s_bc, n + 1 + 1)
                        own.then(dve.tensor_copy(ab_s, PS[:, 7, 0:H_SSD]))
                        own.then(tt(s, s, ab_s.unsqueeze(2).to_broadcast([128, H_SSD, P_SSD]), ALU.mult))
                        for g in range(2):
                            own.mark(stt(s[:, 8 * g:8 * g + 8, :].rearrange("p h q -> p (h q)"), PS[:, 4 + g, :], P[:, XBC + 8 + g, cur],
                                         s[:, 8 * g:8 * g + 8, :].rearrange("p h q -> p (h q)"), ALU.mult, ALU.add))
                        for h in range(H_RET):
                            own.mark(stt(r[:, h, :], PS[:, 6, h * D_RET:(h + 1) * D_RET], P[:, KV + h, cur], r[:, h, :], ALU.mult, ALU.add))
                        own.settle()
                        dve.sem_inc(s_new, 1)
                own.restart()
                dve.wait_ge(s_ye, NS * (l + 1) + 1)
                dve.wait_ge(mixin, 16 * (l + 1))
                for i in range(8):
                    own.mark(stt(P[:, Y_SSD + i, :], P[:, XBC + i, :], col[:, C_D + i:C_D + i + 1], P[:, Y_SSD + i, :], ALU.mult, ALU.add))
                own.settle()
                own.then(tt(P[:, Y_SSD:Y_SSD + 8, :], P[:, Y_SSD:Y_SSD + 8, :], P[:, Z:Z + 8, :], ALU.mult))
                dve.sem_inc(yn_y, 1)
                dve.wait_ge(yn_rt, 3 * l + 1)
                own.then(dve.reciprocal(rs, rs))
                for i in range(8):
                    stt(P[:, Z + i, :], P[:, Y_SSD + i, :], col[:, C_NW + i:C_NW + i + 1], rs, ALU.mult, ALU.mult).then_inc(yn_m, 1)
                dve.wait_ge(yn_rt, 3 * l + 3)
                own.then(dve.reciprocal(P[:, 0:4, :], P[:, 0:4, :]))
                own.then(tt(P[:, Y_RET:Y_RET + 4, :], P[:, Y_RET:Y_RET + 4, :], P[:, 0:4, :], ALU.mult))
                tt(P[:, G:G + 4, :], P[:, Y_RET:Y_RET + 4, :], P[:, G:G + 4, :], ALU.mult).then_inc(yn_m, 1)
                dve.wait_ge(lr_t, 8 * l + 8)
                own.then(ts(hT[:, 0:4, :], P[:, 8:12, :], 1.0, None, ALU.add))
                own.then(dve.reciprocal(hT[:, 0:4, :], hT[:, 0:4, :]))
                own.then(stt(P[:, 8:12, :].rearrange("p a b -> p (a b)"), P[:, 8:12, :].rearrange("p a b -> p (a b)"), 2.0,
                             hT[:, 0:4, :].rearrange("p a b -> p (a b)"), ALU.mult, ALU.mult))
                dve.sem_inc(lr_q, 1)
                own.then(tt(hT[:, 4:8, :], hT[:, 4:8, :], P[:, XR:XR + 4, :], ALU.mult))
                dve.wait_ge(lr_r, l + 1)
                own.then(tt(P[:, 8:12, :], P[:, 8:12, :], hT[:, 4:8, :], ALU.mult))
                for i in range(4):
                    own.mark(dve.tensor_tensor_scan(hT[:, i, 0:SEQ], P[:, 4 + i, 0:SEQ], P[:, 8 + i, 0:SEQ], 0.0, ALU.mult, ALU.add))
                own.then(tt(hT[:, 0:4, SEQ:T], P[:, 4:8, SEQ:T], lru0[:, :, :], ALU.mult))
                own.then(tt(hT[:, 0:4, SEQ:T], hT[:, 0:4, SEQ:T], P[:, 8:12, SEQ:T], ALU.add))
                dve.tensor_copy(lruo[:, :, :], hT[:, 0:4, SEQ - 1:T]).then_inc(lr_h, 1)
                tt(P[:, GATE:GATE + 4, :], hT[:, 0:4, :], P[:, GATE:GATE + 4, :], ALU.mult).then_inc(lr_h, 1)
                dve.wait_ge(lr_h, 3 * l + 2)
                dve.sem_inc(lr_h, 1)
                own.restart()
                with dve.Fori(0, 4) as g:
                    own.restart()
                    for m in range(2):
                        dve.wait_ge(pj, tile0 + NT + 1 + g * 2 + m + 1)
                        X = two(xT[:, g * 2 + m, :])
                        own.then(tt(X, X, halves(2 * m), ALU.add))
                        dve.sem_inc(x_mid, 1)
                        dve.sem_inc(pj_free, 1)
                        dve.sem_inc(w_free, 2)
                own.restart()
                norm(2 * l + 1, col[:, C_N2:C_N2 + 8])
                with dve.Fori(0, 5) as t:
                    own.restart()
                    n = l * 5 + t
                    R = slice(0, TT)

                    def top16(vals, rows, out, idx):
                        for half in range(2):
                            o = slice(8 * half, 8 * half + 8)
                            for i in range(rows):
                                own.mark(dve.max(out[R, i, o], vals[R, i, :]))
                            own.settle()
                            for i in range(rows):
                                own.mark(dve.max_index(idx[R, i, o], out[R, i, o], vals[R, i, :]))
                            own.settle()
                            if half == 0:
                                for i in range(rows):
                                    own.mark(dve.match_replace(vals[R, i, :], out[R, i, o], vals[R, i, :], -3.0e38))
                                own.settle()

                    dve.wait_ge(q_sc, n + 1 + 1)
                    apart(dve)
                    top16(s_sb, HC, s_top, i_u)
                    own.mark(dve.tensor_copy(i_f[R], i_u[R]))
                    pair = s_top[R].rearrange("p (h c) j -> p h c j", c=2)
                    c4 = cand[R].rearrange("p h (a b) -> p h a b", b=TOPK)
                    shape = [TT, H_PEER, TOPK, TOPK]
                    own.then(tt(c4, pair[:, :, 0, :].unsqueeze(3).to_broadcast(shape), pair[:, :, 1, :].unsqueeze(2).to_broadcast(shape), ALU.add))
                    top16(cand, H_PEER, c_top, sel)
                    sel1 = sel[R].rearrange("p h k -> p (h k)")
                    own.mark(ts(j_u[R, 0, :], sel1, 4, None, ALU.logical_shift_right))
                    own.mark(ts(j_u[R, 1, :], sel1, 15, None, ALU.bitwise_and))
                    dve.wait_ge(q_tp, n + 1)
                    own.then(tt(gij[R, 0, :].rearrange("p (h k) -> p h k", k=TOPK), c_top[R],
                                c_top[R, :, 0:1].to_broadcast([TT, H_PEER, TOPK]), ALU.subtract))
                    dve.sem_inc(q_sm, 1)
                    own.then(dve.tensor_copy(j_f[R], j_u[R]))
                    for side in range(2):
                        own.then(tt(oh[R], C[R, K_IOTA:K_IOTA + TOPK].unsqueeze(1).to_broadcast([TT, SLOTS, TOPK]),
                                    j_f[R, side, :].unsqueeze(2).to_broadcast([TT, SLOTS, TOPK]), ALU.is_equal))
                        oh4 = oh[R].rearrange("p (h k) j -> p h k j", k=TOPK)
                        own.then(tt(oh4, oh4, i_f[R].rearrange("p (h c) j -> p h c j", c=2)[:, :, side, :].unsqueeze(2).to_broadcast(shape), ALU.mult))
                        own.then(dve.tensor_reduce(gij[R, 1 + side, :].unsqueeze(2), oh[R], AX.X, ALU.add))
                    dve.wait_ge(q_ex, n + 1)
                    g3 = gij[R, 0, :].rearrange("p (h k) -> p h k", k=TOPK)
                    own.then(dve.tensor_reduce(gsum[R, 0, :].unsqueeze(2), g3, AX.X, ALU.add))
                    own.then(dve.reciprocal(gsum[R, 1, :], gsum[R, 0, :]))
                    tt(g3, g3, gsum[R, 1, :].unsqueeze(2).to_broadcast([TT, H_PEER, TOPK]), ALU.mult).then_inc(q_g, 1)

                dve.wait_ge(q_tr, 5 * l + 5)
                own.restart()
                with dve.Fori(0, T // 8) as i:
                    for s in range(8):
                        if s % 4 == 0:
                            dve.wait_ge(g_mm, (l * (T // 8) + i) * 2 + s // 4 + 1)
                        t = bass.ds(i * 8 + s, 1)
                        ts(Ah[:, s, :], iota, gijT[:, 1, t], gijT[:, 0, t], ALU.is_equal, ALU.mult).then_inc(g_ab, 1)
                        ts(Bh[:, s, :], iota, gijT[:, 2, t], None, ALU.is_equal).then_inc(g_ab, 1)

                def gating(n, b, loads):
                    dve.wait_ge(ld_g[b], 16 * loads)
                    dve.wait_ge(m_y, n * KT + Y0 - KT)
                    for e in range(GRP):
                        dve.wait_ge(m_gelu, n * GRP + e + 1 + GE0)
                        tt(W[b][:, e, :].rearrange("p (n c) -> p n c", c=BT), gh[:, e % 2, :].rearrange("p (n c) -> p n c", c=BT),
                           gt[b][:, :, e * BT:(e + 1) * BT], ALU.mult).then_inc(m_w, 1)

                def adding(n):
                    for d in range(KT):
                        dve.wait_ge(m_y, n * KT + d + 1 + Y0)
                        X = two(xT[:, d, :])
                        tt(X, X, halves(4 + 2 * (d % 2)), ALU.add).then_inc(m_acc, 1)

                n0, ld0 = l * NG, l * (NG // 2)
                gating(n0, 0, ld0 + 1)
                with dve.Fori(0, NG // 2 - 1) as i:
                    gating(n0 + i * 2 + 1, 1, ld0 + i + 1)
                    adding(n0 + i * 2)
                    gating(n0 + i * 2 + 2, 0, ld0 + i + 2)
                    adding(n0 + i * 2 + 1)
                gating(n0 + NG - 1, 1, ld0 + NG // 2)
                adding(n0 + NG - 2)
                adding(n0 + NG - 1)
                dve.wait_ge(m_acc, KT * NG * (l + 1) + ACC0)
            own.restart()
            norm(2 * DEPTH, C[:, K_FW:K_FW + 8])


def kernel(**inputs):
    import concourse.bacc as _bacc
    from concourse.bass_utils import run_bass_kernel_spmd as _run

    i = {k: np.ascontiguousarray(v) for k, v in inputs.items()}
    def feat(a):
        return a.reshape(DEPTH, -1, 128).transpose(0, 2, 1)

    stream = np.concatenate([i["x_prompt"][0], i["x_sample"][:, 0]])
    ins = {"x": stream.reshape(T, KT, 128).transpose(2, 1, 0)}

    wi = i["w_in"]
    cut = lambda a, b: wi[:, :, a:b]
    order = [cut(1024, 2560), cut(5136, 5648), cut(3088, 3600), cut(3600, 4112), cut(2576, 3088),
             cut(0, 1024), cut(4112, 4624), cut(4624, 5136)]
    w_main = np.concatenate(order, axis=2)
    units = lambda a: a.reshape(DEPTH, -1, 8, 128, a.shape[2] // 128, 128).transpose(0, 4, 1, 3, 2, 5).reshape(DEPTH, -1, 128, 8, 128)
    ins["w"] = np.concatenate([units(w_main), units(i["w_out"]), units(i["peer_wq"])], axis=1)
    ins["wdt"] = cut(2560, 2576).reshape(DEPTH, 8, 128, 16).transpose(0, 2, 1, 3)
    ins["keys"] = i["peer_keys"].reshape(DEPTH, HC, KEYS, 128).transpose(0, 3, 1, 2)
    ins["u_tab"] = i["peer_u"].reshape(DEPTH, NG, GRP * 128, 8, 128).transpose(0, 1, 4, 3, 2)
    ins["v_tab"] = i["peer_v"].reshape(DEPTH, NG, GRP, 128, D).transpose(0, 1, 3, 2, 4)
    convw = np.concatenate([i["ssd_conv_w"], i["lru_conv_w"]], axis=2)
    convb = np.concatenate([i["ssd_conv_b"], i["lru_conv_b"]], axis=1)
    ins["cols"] = np.concatenate([
        feat(i["norm1_w"]), feat(i["norm2_w"]),
        convw.reshape(DEPTH, 4, 16, 128).transpose(0, 3, 2, 1).reshape(DEPTH, 128, 64), feat(convb),
        feat(np.repeat(i["ssd_d"], P_SSD, axis=1)), feat(i["ssd_norm_w"]),
        feat(i["lru_ba"]), feat(i["lru_bi"]), feat(i["lru_lambda"])], axis=2)
    ins["heads"] = np.stack([i["ssd_dt_bias"], i["ssd_a_log"]], axis=2)
    cbuf = np.concatenate([i["state_ssd_conv"], i["state_lru_conv"]], axis=3)
    ins["cbuf"] = cbuf.reshape(DEPTH, NS, 3, 16, 128).transpose(0, 4, 3, 2, 1)
    ins["h0"] = i["state_lru"].reshape(DEPTH, NS, 4, 128).transpose(0, 3, 2, 1)
    blk = np.zeros((DEPTH, 128, 8, 128), np.float32)
    for j, name in enumerate(("lru_wa", "lru_wi")):
        for k in range(8):
            a = 64 * (k % 2)
            blk[:, a:a + 64, 4 * j + k // 2, a:a + 64] = i[name][:, k]
    ins["wblk"] = blk
    ins["s_ssd"] = i["state_ssd"].transpose(0, 1, 3, 2, 4)
    ins["s_ret"] = i["state_ret"].transpose(0, 1, 3, 2, 4)

    pos = np.concatenate([np.arange(SEQ), np.full(NS, PAST)]).astype(np.float32)
    inv = (np.float32(10000.0) ** (-np.arange(64, dtype=np.float32) / np.float32(64))).astype(np.float32)
    ang = np.tile((inv[:, None] * pos[None, :]).astype(np.float32), (2, 1)).astype(np.float64)
    perm = np.zeros((128, 128))
    perm[np.arange(64) + 64, np.arange(64)] = -1.0
    perm[np.arange(64), np.arange(64) + 64] = 1.0
    j, k = np.arange(CH)[:, None], np.arange(CH)[None, :]
    mask = np.where(k >= j, 0.0, -1e30)
    lg = np.log(1.0 - 2.0 ** (-5.0 - np.arange(H_RET)))
    dm = np.stack([np.where(k >= j, np.exp((k - j) * g), 0.0) * SCALE for g in lg], axis=1).reshape(128, -1)
    gam = np.tile(np.concatenate([np.exp((np.arange(CH) + 1) * g) for g in lg])[None], (128, 1))
    te = np.stack([np.exp((CH - 1 - np.arange(CH)) * g) * SCALE for g in lg], axis=1)
    cst = np.concatenate([np.cos(ang), np.sin(ang), perm, np.eye(128), mask, dm, gam, te,
                          np.tile(np.arange(128.0)[None], (128, 1)), np.ones((128, 128))], axis=1).astype(np.float32)
    ins["cst"] = np.concatenate([cst, i["final_norm_w"].reshape(KT, 128).T], axis=1)

    outs = {"y": (128, KT, T), "o_ssd_p": (DEPTH, 128, 1024), "o_ret_p": (DEPTH, 128, 512), "o_tail": (DEPTH, 128, 16, 3),
            "o_cbuf": (DEPTH, 128, 16, 3, NS), "o_lru": (DEPTH, 128, 4, 1 + NS),
            "o_ssd_s": (DEPTH, NS, 128, 1024), "o_ret_s": (DEPTH, NS, 128, 512)}
    nc = _bacc.Bacc("TRN2", target_bir_lowering=False, num_devices=1)
    ins = {n: np.ascontiguousarray(a, dtype=np.float32) for n, a in ins.items()}
    args = {n: nc.dram_tensor(n, a.shape, F32, kind="ExternalInput").ap() for n, a in ins.items()}
    args["gates"] = nc.dram_tensor("gates", (NB, 128, KEYS * BT), F32, kind="Internal").ap()
    args |= {n: nc.dram_tensor(n, s, F32, kind="ExternalOutput").ap() for n, s in outs.items()}
    decoder_step(nc, **args)
    r = _run(nc, [ins], core_ids=[0]).results[0]

    y = r["y"].transpose(2, 1, 0).reshape(T, D)
    tail = r["o_tail"].transpose(0, 3, 2, 1).reshape(DEPTH, 1, 3, 2048)
    cbn = r["o_cbuf"].transpose(0, 4, 3, 2, 1).reshape(DEPTH, NS, 3, 2048)
    lru = r["o_lru"].transpose(0, 3, 2, 1).reshape(DEPTH, 1 + NS, 512)
    head_major = lambda a, h: a.reshape(a.shape[:-1] + (h, -1)).swapaxes(-3, -2)
    c = np.ascontiguousarray
    return (c(y[None, :SEQ]), c(y[SEQ:, None]),
            c(head_major(r["o_ssd_p"], H_SSD)[:, None]), c(tail[..., :1536]), c(head_major(r["o_ret_p"], H_RET)[:, None]),
            c(lru[:, :1]), c(tail[..., 1536:]),
            c(head_major(r["o_ssd_s"], H_SSD)), c(cbn[..., :1536]), c(head_major(r["o_ret_s"], H_RET)),
            c(lru[:, 1:]), c(cbn[..., 1536:]))
```

```python
from contextlib import ExitStack

import numpy as np

import concourse.bass as bass
from concourse import mybir

F32 = mybir.dt.float32
U32 = mybir.dt.uint32
ACT = mybir.ActivationFunctionType
ALU = mybir.AluOpType
AX = mybir.AxisListType

DEPTH, D, SEQ, NS = 2, 1024, 512, 8
T = SEQ + NS
HALF = T // 2
PAST = 4096
EPS = 1e-6
KT = D // 128
H_SSD, P_SSD, N_SSD = 16, 64, 128
H_RET, D_RET = 4, 128
KEYS, H_PEER, TOPK = 128, 8, 16
HC = 2 * H_PEER
SLOTS = H_PEER * TOPK
CH = 128
NCH = SEQ // CH

XBC, XR, KV, Q, Z, G, GATE = 0, 12, 16, 24, 28, 36, 40
NT = 44
Y_SSD, Y_RET, MIX = 16, 24, 28
UNITS = NT + 16 + 16
RING = 4
TILES_L = 1 + NT + 8 + 16

TT = T // 5
NB, BT = 13, T // 13
QUADS = BT // 4
GRP = 4
NG = KEYS // GRP
EARLY = NG // 2
TILE_PAIR = 2 * (BT // 4)

C_N1, C_N2, C_CW, C_CB, C_D, C_NW, C_BA, C_BI, C_LAM, NCOL = 0, 8, 16, 80, 96, 104, 112, 116, 120, 124
K_COS, K_SIN, K_PERM, K_ID, K_MASK, K_DM, K_GAM, K_TE, K_IOTA, K_ONE, K_FW, NCST = np.cumsum(
    [0, T, T, 128, 128, 128, 4 * CH, 4 * CH, 4, 128, 128, 8]).tolist()
CHEAD = 16

GAMMA_CH = [float((1.0 - 2.0 ** (-5 - h)) ** CH) for h in range(H_RET)]
GAMMA = [float(1.0 - 2.0 ** (-5 - h)) for h in range(H_RET)]
SCALE = D_RET ** -0.5


def decoder_step(nc, x, w, wdt, keys, u_tab, v_tab, cols, heads, cbuf, h0, wblk, s_ssd, s_ret, cst, gates, early,
                 y, o_ssd_p, o_ret_p, o_tail, o_cbuf, o_lru, o_ssd_s, o_ret_s):
    with ExitStack() as ctx:
        def sb(name, shape):
            return ctx.enter_context(nc.sbuf_tensor(name, shape, F32))

        def sem(name):
            return ctx.enter_context(nc.semaphore(name))

        xT = sb("xT", [128, KT, T])
        hT = sb("hT", [128, KT, T])
        ring = sb("ring", [128, RING, 8, 128])
        C = sb("C", [128, NCST])
        col = sb("col", [128, NCOL])
        head = sb("head", [H_SSD, 2])
        cb = sb("cb", [128, 16, 3, NS])
        cbn = sb("cbn", [128, 16, 3, NS])
        tail = sb("tail", [128, 16, 3])
        lru0 = sb("lru0", [128, 4, NS])
        lruo = sb("lruo", [128, 4, 1 + NS])
        blk = sb("blk", [128, 8, 128])
        wd = sb("wd", [128, 8, 16])
        eps = sb("eps", [128, 1])
        c8 = sb("c8", [128, 6, 4])
        nA = sb("nA", [H_SSD, 1])
        PN = NT * T
        AN = PN + 11312
        AR = sb("AR", [128, AN])
        P = AR[:, 0:PN].rearrange("p (i t) -> p i t", t=T)
        top = [PN]

        def take(shape):
            n = int(np.prod(shape))
            ap = AR[:, top[0]:top[0] + n]
            top[0] += n
            assert top[0] <= AN, (top[0], AN)
            if len(shape) == 2:
                ap = ap.rearrange("p (a b) -> p a b", b=shape[1])
            if len(shape) == 3:
                ap = ap.rearrange("p (a b c) -> p a b c", b=shape[1], c=shape[2])
            return ap

        xc = take((24, CH))
        vdt = take((H_SSD, P_SSD))
        vend = take((H_SSD, P_SSD))
        btok = take((2, CH))
        vtok = take((H_RET, CH))
        kend = take((H_RET, CH))
        sc = take((2, CH))
        mr = take((H_RET, CH))
        dec = take((2, 4, CH))
        ec = take((2, 4, CH))
        cd = take((H_SSD,))
        tok = take((2, H_SSD))
        crow = take((4, CH))
        S = take((H_SSD, P_SSD))
        Sr = take((H_RET, D_RET))
        top[0] = PN
        rs = take((T,))
        cv = take((2, T))
        rt = take((2, T))
        dtr = take((T,))
        rows_tmp = take((4, T))
        top[0] = PN
        RW = H_SSD * P_SSD + H_SSD + H_RET * D_RET
        tk_s = take((RW,))
        rm_s = take((RW,))
        st_s_t = [take((H_SSD, P_SSD)) for _ in range(2)]
        sr_s_t = [take((H_RET, D_RET)) for _ in range(2)]
        ab_s = take((H_SSD,))
        sdt = take((H_SSD,))
        rows_kept = take((4, T))
        R_CUM, R_NCUM, R_DT, R_TE = range(4)

        def row(i):
            return (rows_kept[0:H_SSD, i, :] if i < 4 else rows_tmp[0:H_SSD, i - 4, :])

        top[0] = 0
        U = [take((8, GRP * 128)) for _ in range(2)]
        gh = take((2, T))
        gijT = take((3, T))
        PEER = top[0]
        qT = take((HC, T))
        kT = take((HC, KEYS))
        qs = take((HC, TT))
        s_sb = take((HC, KEYS))
        s_top = take((HC, TOPK))
        i_u = take((HC, TOPK)).bitcast(U32)
        i_f = take((HC, TOPK))
        c_top = take((H_PEER, TOPK))
        sel = take((H_PEER, TOPK)).bitcast(U32)
        j_u = take((2, SLOTS)).bitcast(U32)
        j_f = take((2, SLOTS))
        gsum = take((2, H_PEER))
        gij = take((3, SLOTS))
        oh = take((SLOTS, TOPK))
        cand = take((H_PEER, TOPK * TOPK))
        top[0] = PEER
        stage = [take((KEYS, BT)) for _ in range(2)]
        Ah = take((8, 128))
        Bh = take((8, 128))
        top[0] = PEER
        V = [take((GRP, D)) for _ in range(2)]
        gt = [take((NB, GRP * BT)) for _ in range(2)]
        W = [take((GRP, T)) for _ in range(2)]
        ga = [take((GRP, T)) for _ in range(2)]

        PS = ctx.enter_context(nc.psum_tensor("PS", [128, 8, 512], F32))
        ident, ones = C[:, K_ID:K_ID + 128], C[:, K_ONE:K_ONE + 128]
        iota = C[:, K_IOTA:K_IOTA + 128]

        def halves(bank):
            return PS[:, bank:bank + 2, 0:HALF]

        def two(ap):
            return ap.rearrange("p (h t) -> p h t", h=2)

        def hs(i):
            return slice(i * HALF, (i + 1) * HALF)

        ld_x, ld_small, ld_keys = sem("ld_x"), sem("ld_small"), sem("ld_keys")
        ld_w = [sem(f"ld_w{i}") for i in range(RING)]
        w_free, pj, pj_free = sem("w_free"), sem("pj"), sem("pj_free")
        w_half = sem("w_half")
        n_sq, n_ss, n_rt, n_h = sem("n_sq"), sem("n_ss"), sem("n_rt"), sem("n_h")
        raw, dt_raw = sem("raw"), sem("dt_raw")
        conv, act_x, mixin = sem("conv"), sem("act_x"), sem("mixin")
        rot_p, rot_x = sem("rot_p"), sem("rot_x")
        dt_q, dt_e, dt_r = sem("dt_q"), sem("dt_e"), sem("dt_r")
        ck_0 = sem("ck_0")
        ck_x = sem("ck_x")
        ck_t, ck_tok, ck_atok = sem("ck_t"), sem("ck_tok"), sem("ck_atok")
        ck_s, ck_sc, ck_mr = sem("ck_s"), sem("ck_sc"), sem("ck_mr")
        ck_seg, ck_exp, ck_m = sem("ck_seg"), sem("ck_exp"), sem("ck_m")
        ck_y, ck_yr, ck_ye = sem("ck_y"), sem("ck_yr"), sem("ck_ye")
        ck_st, ck_S, st_p = sem("ck_st"), sem("ck_S"), sem("st_p")
        s_t, s_tk = sem("s_t"), sem("s_tk")
        s_rm, s_bc, s_new = sem("s_rm"), sem("s_bc"), sem("s_new")
        s_y, s_ye = sem("s_y"), sem("s_ye")
        ld_s, st_s = [sem("ld_s0"), sem("ld_s1")], [sem("st_s0"), sem("st_s1")]
        yn_y, yn_sq, yn_ss, yn_rt, yn_m = (sem(f"yn_{n}") for n in ("y", "sq", "ss", "rt", "m"))
        lr_p, lr_a, lr_t = sem("lr_p"), sem("lr_a"), sem("lr_t")
        lr_q, lr_r, lr_h = sem("lr_q"), sem("lr_r"), sem("lr_h")
        states_out, small_out = sem("states_out"), sem("small_out")
        x_mid, st_small = sem("x_mid"), sem("st_small")
        q_in, q_cp, q_s, q_sc = sem("q_in"), sem("q_cp"), sem("q_s"), sem("q_sc")
        q_sm, q_ex, q_g = sem("q_sm"), sem("q_ex"), sem("q_g")
        q_tp, q_tr = sem("q_tp"), sem("q_tr")
        q_free = sem("q_free")
        g_ab, g_mm, g_cp = sem("g_ab"), sem("g_mm"), sem("g_cp")
        g_out = [sem("g_out0"), sem("g_out1")]
        ld_u, ld_v, ld_g = ([sem(f"ld_{n}{i}") for i in range(2)] for n in "uvg")
        m_h, m_gelu, m_w, m_y, m_acc = (sem(f"m_{n}") for n in ("h", "gelu", "w", "y", "acc"))
        a_out, ld_a = [sem("a_out0"), sem("a_out1")], [sem("ld_a0"), sem("ld_a1")]
        st_y = sem("st_y")
        passed = sem("passed")
        v_seq, a_seq = sem("v_seq"), sem("a_seq")

        def apart(eng):
            eng.sem_inc(passed, 1)

        class Order:

            def __init__(self, eng, s):
                self.eng, self.s, self.n, self.settled = eng, s, 0, 0

            def restart(self):
                assert self.settled == self.n
                apart(self.eng)
                self.eng.sem_clear(self.s)
                self.n = self.settled = 0

            def mark(self, ins):
                ins.then_inc(self.s, 1)
                self.n += 1

            def settle(self):
                self.eng.wait_ge(self.s, self.n)
                self.settled = self.n

            def then(self, ins):
                self.mark(ins)
                self.settle()

        H0, W0, Y0, GE0, ACC0 = 2 * GRP, 2 * GRP, 2 * KT, 2, 2
        block = ctx.enter_context(nc.Block())

        @block.sync
        def _(sp):
            sp.dma_start(C[:, :], cst).then_inc(ld_x, 16)
            sp.dma_start(xT[:, :, :], x).then_inc(ld_x, 16)
            for s, n in ((w_free, RING), (pj_free, 2), (m_h, H0), (m_w, W0), (m_y, Y0), (m_gelu, GE0), (m_acc, ACC0),
                         (g_mm, 2), (g_cp, 2)):
                sp.sem_inc(s, n)
            for s in (small_out, states_out, ck_S, ck_ye, ck_st, ck_m, s_new, s_ye, s_bc, act_x, rot_x, q_s, q_sc, q_g, q_tp, q_tr,
                      *st_s, *g_out, *a_out):
                sp.sem_inc(s, 1)
            with sp.Fori(0, DEPTH) as l:
                def load_unit(g, s):
                    sp.dma_start(ring[:, s, :, :], w[l, g * RING + s]).then_inc(ld_w[s], 16)

                G_IN, G_OUT, freed, tiles = NT // RING, 4, (NT + 16) * l, l * TILES_L + NT + 1
                with sp.Fori(0, G_IN) as g:
                    for s in range(RING):
                        sp.wait_ge(w_free, freed + g * RING + s + 1)
                        load_unit(g, s)
                for g in range(G_OUT + 1):
                    for s in range(RING):
                        if g == 0:
                            sp.wait_ge(w_free, freed + NT + s + 1)
                        elif g % 2:
                            sp.wait_ge(w_half, l * KT + (g // 2) * RING + s + 1)
                        else:
                            sp.wait_ge(pj, tiles + (g // 2 - 1) * RING + s + 1)
                        load_unit(G_IN + g, s)
                with sp.Fori(1, 4) as g:
                    for s in range(RING):
                        sp.wait_ge(w_free, freed + NT + g * RING + s + 1)
                        load_unit(g + G_IN + G_OUT, s)

                def load_u(j, n, b):
                    sp.wait_ge(m_h, n * GRP + H0 - GRP)
                    sp.dma_start(U[b], u_tab[l, j]).then_inc(ld_u[b], 16)

                def load_gates_v(j, n, b):
                    sp.wait_ge(m_w, n * GRP + W0 - GRP)
                    sp.dma_start(gt[b], gates[:, :, bass.ds(j * GRP * BT, GRP * BT)].rearrange("n p c -> p n c")).then_inc(ld_g[b], 16)
                    sp.wait_ge(m_y, n * KT + Y0 - KT)
                    sp.dma_start(V[b], v_tab[l, j]).then_inc(ld_v[b], 16)

                n0 = l * NG
                load_u(0, n0, 0)
                load_u(1, n0 + 1, 1)
                with sp.Fori(0, EARLY // 2) as i:
                    for b in range(2):
                        for e in range(GRP):
                            sp.wait_ge(m_gelu, (n0 + i * 2 + b) * GRP + e + 1 + GE0)
                            sp.dma_start(early[i * 2 + b, :, e * T:(e + 1) * T], gh[:, e % 2, :]).then_inc(a_out[e % 2], 16)
                        load_u(i * 2 + b + 2, n0 + i * 2 + b + 2, b)
                sp.wait_ge(g_out[0], 16 * 7 * (l + 1) + 1)
                apart(sp)
                sp.wait_ge(g_out[1], 16 * 6 * (l + 1) + 1)
                apart(sp)
                with sp.Fori(0, (NG - EARLY) // 2 - 1) as i:
                    for b in range(2):
                        load_gates_v(i * 2 + b + EARLY, n0 + i * 2 + b, b)
                        load_u(i * 2 + b + EARLY + 2, n0 + i * 2 + b + EARLY + 2, b)
                for b in range(2):
                    load_gates_v(NG - 2 + b, n0 + NG - EARLY - 2 + b, b)
                for b in range(2):
                    sp.wait_ge(a_out[b], 16 * 2 * EARLY * (l + 1) + 1)
                    apart(sp)
                with sp.Fori(0, EARLY // 2) as i:
                    for b in range(2):
                        n = n0 + NG - EARLY + i * 2 + b
                        sp.wait_ge(m_w, n * GRP + W0 - GRP)
                        sp.dma_start(ga[b].rearrange("p e t -> p (e t)"), early[i * 2 + b]).then_inc(ld_a[b], 16)
                        load_gates_v(i * 2 + b, n, b)
            sp.wait_ge(n_h, KT * (2 * DEPTH + 1))
            sp.dma_start(y, hT[:, :, :]).then_inc(st_y, 16)
            sp.wait_ge(st_y, 16)

        @block.gpsimd
        def _(pool):
            with pool.Fori(0, DEPTH) as l:
                pool.wait_ge(m_acc, l * NG * KT + ACC0)
                apart(pool)
                for dst, src in ((col[:, :], cols[l]), (head[:, :], heads[l]), (cb[:, :, :, :], cbuf[l]),
                                 (lru0[:, :, :], h0[l]), (blk[:, :, :], wblk[l]), (wd[:, :, :], wdt[l])):
                    pool.dma_start(dst, src).then_inc(ld_small, 16)
                pool.wait_ge(act_x, 16 * l + 16 + 1)
                pool.wait_ge(rot_x, 8 * l + 8 + 1)
                pool.wait_ge(dt_r, l + 1)
                apart(pool)
                with pool.Fori(0, NS // 2) as i:
                    for b in range(2):
                        pool.wait_ge(st_s[b], 32 * (l * (NS // 2) + i) + 1)
                        apart(pool)
                        pool.dma_start(st_s_t[b], s_ssd[l, i * 2 + b]).then_inc(ld_s[b], 16)
                        pool.dma_start(sr_s_t[b], s_ret[l, i * 2 + b]).then_inc(ld_s[b], 16)
                pool.wait_ge(ck_0, l + 1)
                apart(pool)
                with pool.Fori(0, NCH) as c:
                    pool.wait_ge(ck_S, 7 * (l * NCH + c) + 1)
                    rows = hT[0:H_SSD, 0:4, 0:SEQ].rearrange("p i (c j) -> p i c j", j=CH)
                    pool.tensor_copy(crow[0:H_SSD, :, :], rows[:, :, c, :]).then_inc(ck_x, 1)
                pool.wait_ge(ck_S, 7 * NCH * (l + 1) + 1)
                apart(pool)
                pool.dma_start(o_ssd_p[l], S.rearrange("p a b -> p (a b)")).then_inc(st_p, 16)
                pool.dma_start(o_ret_p[l], Sr.rearrange("p a b -> p (a b)")).then_inc(st_p, 16)
                pool.wait_ge(st_p, 32 * l + 32)
                pool.sem_inc(states_out, 1)
                pool.wait_ge(lr_h, 3 * l + 3)
                apart(pool)
                pool.dma_start(o_tail[l], tail[:, :, :]).then_inc(st_small, 16)
                pool.dma_start(o_cbuf[l], cbn[:, :, :, :]).then_inc(st_small, 16)
                pool.dma_start(o_lru[l], lruo[:, :, :]).then_inc(st_small, 16)
                pool.wait_ge(x_mid, KT * l + KT)
                apart(pool)
                pool.dma_start(kT, keys[l]).then_inc(ld_keys, 16)
                pool.wait_ge(st_small, 48 * l + 48)
                pool.sem_inc(small_out, 1)
                pool.wait_ge(q_in, HC * l + HC)
                apart(pool)
                with pool.Fori(0, 5) as t:
                    pool.wait_ge(q_s, l * 5 + t + 1)
                    pool.tensor_copy(qs, qT.rearrange("p h (t c) -> p h t c", c=TT)[:, :, t, :]).then_inc(q_cp, 1)
            pool.wait_ge(st_p, 32 * DEPTH)
            pool.wait_ge(st_small, 48 * DEPTH)

        @block.tensor
        def _(pe):
            mm = pe.matmul

            def sums(src, n_tiles, bank):
                for h in range(2):
                    for k in range(n_tiles):
                        last = mm(PS[:, bank + h, 0:HALF], ones, src[:, k, hs(h)], start=(k == 0), stop=(k == n_tiles - 1))
                return last

            def unit(l, g, s, b, k0, k1, src, first=True, final=True):
                pe.wait_ge(ld_w[s], (l * (UNITS // RING) + g) * 16 + 16)
                for h in range(2):
                    for k in range(8):
                        last = mm(PS[:, 2 * b + h, 0:HALF], ring[:, s, k, :], src[:, k0 + k, hs(h)],
                                  start=(first and k == 0), stop=(final and k == 7), skip_group_check=True)
                return last

            pe.wait_ge(ld_x, 32)
            with pe.Fori(0, DEPTH) as l:
                tile0 = l * TILES_L
                pe.wait_ge(n_sq, 2 * l + 1)
                sums(hT, KT, 4).then_inc(n_ss, 1)
                pe.wait_ge(n_h, (2 * l + 1) * KT)
                pe.wait_ge(ld_small, 96 * l + 96)
                pe.wait_ge(pj_free, tile0 + 1)
                for h in range(2):
                    for k in range(KT):
                        last = mm(PS[0:H_SSD, 6 + h, 0:HALF], wd[:, k, :], hT[:, k, hs(h)], start=(k == 0), stop=(k == KT - 1))
                last.then_inc(pj, 1)

                def project(g, s):
                    pe.wait_ge(pj_free, tile0 + g * RING + s + 2)
                    unit(l, g, s, s % 2, 0, 8, hT).then_inc(pj, 1)

                with pe.Fori(0, 7) as g:
                    for s in range(RING):
                        project(g, s)
                for i in range(4):
                    project(7, i)
                    pe.wait_ge(raw, 28 * l + 28)
                    for j, t0 in enumerate((KV, Q)):
                        pe.wait_ge(rot_x, l * 8 + i * 2 + 1)
                        for h in range(2):
                            last = mm(PS[:, 4 + 2 * j + h, 0:HALF], C[:, K_PERM:K_PERM + 128],
                                      P[:, t0 + i, hs(h)], start=True, stop=True)
                        last.then_inc(rot_p, 1)
                pe.wait_ge(act_x, 16 * l + 16 + 1)
                pe.wait_ge(rot_x, 8 * l + 8 + 1)
                pe.wait_ge(dt_r, l + 1)
                for i in range(8):
                    pe.transpose(PS[0:NS, 4 + i // 4, (i % 4) * 128:(i % 4 + 1) * 128], P[:, XBC + i, SEQ:T], ident)
                for i in range(4):
                    pe.transpose(PS[0:NS, 6, i * 128:(i + 1) * 128], P[:, KV + 4 + i, SEQ:T], ident)
                for i, r in enumerate((R_DT, R_CUM)):
                    last = pe.transpose(PS[0:NS, 7, i * H_SSD:(i + 1) * H_SSD], row(r)[:, SEQ:T], C[0:H_SSD, K_ID:K_ID + H_SSD])
                last.then_inc(s_t, 1)
                with pe.Fori(0, NS // RING) as i:
                    for s in range(RING):
                        n = l * NS + i * RING + s
                        b = s % 2
                        pe.wait_ge(s_rm, n + 1)
                        pe.wait_ge(s_new, n + 1)
                        pe.wait_ge(s_ye, n + 1)
                        one = C[0:NS, K_ONE:K_ONE + 128]
                        mm(PS[:, 7, 0:H_SSD], one, rm_s[0:NS, D:D + H_SSD], start=True, stop=True)
                        for g in range(2):
                            mm(PS[:, 4 + g, :], one, rm_s[0:NS, g * 512:(g + 1) * 512], start=True, stop=True)
                        mm(PS[:, 6, :], one, rm_s[0:NS, D + H_SSD:RW], start=True, stop=True).then_inc(s_bc, 1)
                        project(i + 8, s)
                        pe.wait_ge(s_new, n + 1 + 1)
                        cur = bass.ds(i * RING + s + SEQ, 1)
                        for j in range(8):
                            mm(PS[:, 7, H_SSD + j:H_SSD + j + 1], st_s_t[b][:, 2 * j:2 * j + 2, :], P[:, XBC + 10 + j // 4, cur],
                               start=True, stop=True, skip_group_check=True)
                        for h in range(H_RET):
                            last = mm(PS[:, 7, H_SSD + 8 + h:H_SSD + 9 + h], sr_s_t[b][:, h, :], P[:, Q + h, cur],
                                      start=True, stop=True, skip_group_check=True)
                        last.then_inc(s_y, 1)
                for s in range(RING):
                    project(10, s)
                pe.wait_ge(pj_free, tile0 + 1 + NT + 2)
                pe.wait_ge(s_ye, NS * (l + 1) + 1)
                apart(pe)
                with pe.Fori(0, NCH) as c:
                    it = l * NCH + c
                    pe.wait_ge(ck_x, 3 * it + 3)
                    pe.wait_ge(ck_ye, 2 * it + 1)
                    pe.wait_ge(ck_S, 7 * it + 1)
                    for i in range(8):
                        pe.transpose(PS[:, i // 4, (i % 4) * CH:(i % 4 + 1) * CH], xc[:, i, :], ident)
                    for i in range(2):
                        pe.transpose(PS[:, 2, i * CH:(i + 1) * CH], xc[:, 8 + i, :], ident)
                    for i in range(4):
                        pe.transpose(PS[:, 3, i * CH:(i + 1) * CH], xc[:, 12 + i, :], ident)
                    for i in range(4):
                        pe.transpose(PS[:, 4, i * CH:(i + 1) * CH], xc[:, 16 + i, :], ident)
                    for i in range(2):
                        last = pe.transpose(PS[:, 7, i * H_SSD:(i + 1) * H_SSD], crow[0:H_SSD, R_DT + i, :], C[0:H_SSD, K_ID:K_ID + H_SSD])
                    last.then_inc(ck_t, 1)
                    for g in range(2):
                        mm(PS[:, 5, g * CH:(g + 1) * CH], xc[:, 8 + g, :], xc[:, 10 + g, :], start=True, stop=True)
                    for h in range(H_RET):
                        last = mm(PS[:, 6, h * CH:(h + 1) * CH], xc[:, 12 + h, :], xc[:, 20 + h, :], start=True, stop=True)
                    last.then_inc(ck_s, 1)

                    def decays(q):
                        if q == 0:
                            pe.wait_ge(ck_tok, 4 * it + 1)
                            pe.wait_ge(ck_atok, 2 * it + 1)
                        elif q == 1:
                            pe.wait_ge(ck_mr, 2 * it + 1)
                            pe.wait_ge(ck_tok, 4 * it + 4)
                        else:
                            pe.wait_ge(ck_exp, 8 * it + 2 * (q - 1))
                        seg, cum = 7 - q % 2, 2 + q % 2
                        mm(PS[:, seg, :], ident, C[:, K_MASK:K_MASK + CH].unsqueeze(1).to_broadcast([128, 4, CH]),
                           start=True, stop=False, skip_group_check=True)
                        for r in range(4):
                            h = 4 * q + r
                            pick = C[0:H_SSD, K_ID + h:K_ID + h + 1].to_broadcast([H_SSD, CH])
                            o = slice(r * CH, (r + 1) * CH)
                            mm(PS[:, seg, o], pick, crow[0:H_SSD, 0, :], start=False, stop=False, skip_group_check=True)
                            mm(PS[:, seg, o], crow[0:H_SSD, 1, :], pick, start=False, stop=(r == 3), skip_group_check=True)
                            last = mm(PS[:, cum, o], pick, crow[0:H_SSD, 0, :], start=True, stop=True)
                        last.then_inc(ck_seg, 1)

                    def outputs(q):
                        pe.wait_ge(ck_m, 12 * it + 3 * q + 3 + 1)
                        if q == 0:
                            pe.wait_ge(ck_tok, 4 * it + 3)
                        for r in range(4):
                            h = 4 * q + r
                            p0 = 64 * (h % 2)
                            o = PS[p0:p0 + 64, h // 8, (h // 2 % 4) * CH:(h // 2 % 4 + 1) * CH]
                            mm(o, vdt[:, h, :], dec[:, q % 2, r, :], start=True, stop=False, skip_group_check=True)
                            last = mm(o, S[:, h, :], ec[:, q % 2, r, :], start=False, stop=True, skip_group_check=True)
                        last.then_inc(ck_y, 1)

                    decays(0)
                    decays(1)
                    outputs(0)
                    decays(2)
                    outputs(1)
                    decays(3)
                    outputs(2)
                    outputs(3)
                    pe.wait_ge(ck_atok, 2 * it + 2)
                    pe.wait_ge(ck_mr, 2 * it + 2)
                    for h in range(H_RET):
                        o = PS[:, 4, h * CH:(h + 1) * CH]
                        mm(o, vtok[:, h, :], mr[:, h, :], start=True, stop=False, skip_group_check=True)
                        last = mm(o, Sr[:, h, :], xc[:, 20 + h, :], start=False, stop=True, skip_group_check=True)
                    last.then_inc(ck_yr, 1)
                    pe.wait_ge(ck_sc, it + 1)
                    pe.wait_ge(ck_exp, 8 * it + 8)
                    for g in range(2):
                        mm(PS[:, (5, 2)[g], :], btok[:, g, :], vend[:, 8 * g:8 * g + 8, :], start=True, stop=True)
                    for h in range(H_RET):
                        last = mm(PS[:, 3, h * CH:(h + 1) * CH], kend[:, h, :], vtok[:, h, :], start=True, stop=True)
                    last.then_inc(ck_st, 1)
                pe.wait_ge(yn_sq, 2 * l + 1)
                sums(hT, KT, 0).then_inc(yn_ss, 1)
                pe.wait_ge(yn_sq, 2 * l + 2)
                for h in range(H_RET):
                    mm(PS[:, 2 + h, :], ones, hT[:, h, 0:SEQ], start=True, stop=True)
                for h in range(H_RET):
                    last = mm(PS[:, 6, h * NS:(h + 1) * NS], ones, hT[:, h, SEQ:T], start=True, stop=True)
                last.then_inc(yn_ss, 1)
                pe.wait_ge(yn_rt, 3 * l + 3)
                for i in range(4):
                    for j in range(2):
                        n = 2 * i + j
                        if n >= 4:
                            pe.wait_ge(lr_a, 8 * l + n - 3)
                        for h in range(2):
                            last = mm(PS[:, 2 * (n % 4) + h, 0:HALF], blk[:, 4 * j + i, :], P[:, XR + i, hs(h)],
                                      start=True, stop=True)
                        last.then_inc(lr_p, 1)
                with pe.Fori(0, 2) as g:
                    pe.wait_ge(lr_a, 8 * l + 8)
                    pe.wait_ge(yn_m, 9 * l + 8)
                    for s in range(RING):
                        pe.wait_ge(pj_free, tile0 + NT + g * RING + s)
                        unit(l, NT // RING + 2 * g, s, s, MIX, None, P, final=False).then_inc(w_half, 1)
                    pe.wait_ge(yn_m, 9 * l + 9)
                    pe.wait_ge(lr_h, 3 * l + 3)
                    for s in range(RING):
                        unit(l, NT // RING + 2 * g + 1, s, s, MIX + 8, None, P, first=False).then_inc(pj, 1)
                pe.wait_ge(n_sq, 2 * l + 2)
                sums(hT, KT, 4).then_inc(n_ss, 1)
                pe.wait_ge(n_h, (2 * l + 2) * KT)
                apart(pe)
                with pe.Fori(0, 4) as g:
                    for s in range(RING):
                        pe.wait_ge(pj_free, tile0 + NT + 9 + g * RING + s + 1)
                        unit(l, NT // RING + 4 + g, s, s % 2, 0, 8, hT).then_inc(pj, 1)
                def scores(n, transposed):
                    pe.wait_ge(q_cp, n + 1)
                    pe.wait_ge(q_sc, n + 1)
                    pe.wait_ge(q_tr, transposed + 1)
                    for j in range(HC):
                        last = mm(PS[0:TT, 4 + j // 4, (j % 4) * KEYS:(j % 4 + 1) * KEYS], qs[:, j, :], kT[:, j, :], start=True, stop=True)
                    last.then_inc(q_s, 1)

                def product(n, b, e):
                    pe.wait_ge(m_gelu, n * GRP + e + GE0 - 1)
                    for h in range(2):
                        for k in range(KT):
                            last = mm(PS[:, 2 * (e % 2) + h, 0:HALF], U[b][:, k, e * 128:(e + 1) * 128],
                                      hT[:, k, hs(h)], start=(k == 0), stop=(k == KT - 1))
                    last.then_inc(m_h, 1)

                def products(n, b, loads):
                    pe.wait_ge(ld_u[b], 16 * loads)
                    for e in range(GRP):
                        product(n, b, e)

                def choice(t, more):
                    n = l * 5 + t
                    if more:
                        scores(n + 1, n)
                    for b in range(2):
                        products(l * NG + t * 2 + b, b, l * (NG // 2) + t + 1)
                    pe.wait_ge(q_g, n + 1 + 1)
                    if more:
                        pe.wait_ge(q_sc, n + 2 + 1)
                    for j in range(3):
                        last = pe.transpose(PS[:, 4, j * TT:(j + 1) * TT], gij[0:TT, j, :], C[0:TT, K_ID:K_ID + TT])
                    last.then_inc(q_tp, 1)

                pe.wait_ge(ld_keys, 16 * l + 16)
                pe.wait_ge(pj_free, tile0 + TILES_L + 2)
                scores(l * 5, l * 5)
                with pe.Fori(0, 4) as t:
                    choice(t, True)
                choice(4, False)

                def gate_quad(n, q):
                    pe.wait_ge(g_cp, n + q + 1)
                    pe.wait_ge(g_ab, (n + q) * 8 + 8)
                    for r in range(4):
                        s = (4 * q + r) % 8
                        last = mm(PS[:, 5 + q % 2, r * KEYS:(r + 1) * KEYS], Bh[:, s, :], Ah[:, s, :], start=True, stop=True)
                    last.then_inc(g_mm, 1)

                with pe.Fori(0, NB // 4) as i:
                    for b in range(2):
                        pe.wait_ge(ld_u[b], 16 * (l * (NG // 2) + i + 6))
                        for e in range(GRP):
                            product(l * NG + i * 2 + 10 + b, b, e)
                            for q in range(e * TILE_PAIR // GRP, (e + 1) * TILE_PAIR // GRP):
                                gate_quad(l * NB * QUADS + (i * 2 + b) * TILE_PAIR, q)
                for q in range(QUADS):
                    gate_quad(l * NB * QUADS + (NB - 1) * QUADS, q)
                pe.wait_ge(g_cp, NB * QUADS * (l + 1) + 2)

                def results(n, b, loads):
                    pe.wait_ge(ld_v[b], 16 * loads)
                    pe.wait_ge(m_w, n * GRP + GRP + W0)
                    for d in range(KT):
                        pe.wait_ge(m_acc, n * KT + d + ACC0 - 1)
                        for h in range(2):
                            for e in range(GRP):
                                last = mm(PS[:, 4 + 2 * (d % 2) + h, 0:HALF], V[b][:, e, d * 128:(d + 1) * 128],
                                          W[b][:, e, hs(h)], start=(e == 0), stop=(e == GRP - 1))
                        last.then_inc(m_y, 1)

                u0, v0, ld0 = l * NG + EARLY, l * NG, l * (NG // 2)
                LATE = NG - EARLY
                products(u0, 0, ld0 + EARLY // 2 + 1)
                with pe.Fori(0, LATE // 2 - 1) as i:
                    products(u0 + i * 2 + 1, 1, ld0 + EARLY // 2 + i + 1)
                    results(v0 + i * 2, 0, ld0 + i + 1)
                    products(u0 + i * 2 + 2, 0, ld0 + EARLY // 2 + i + 2)
                    results(v0 + i * 2 + 1, 1, ld0 + i + 1)
                products(u0 + LATE - 1, 1, ld0 + NG // 2)
                with pe.Fori(0, EARLY // 2 + 1) as i:
                    for b in range(2):
                        results(v0 + LATE - 2 + i * 2 + b, b, ld0 + LATE // 2 + i)
            pe.wait_ge(n_sq, 2 * DEPTH + 1)
            sums(hT, KT, 4).then_inc(n_ss, 1)

        @block.scalar
        def _(act):
            A = act.activation
            own = Order(act, a_seq)

            def norm(m):
                A(hT[:, :, :], xT[:, :, :], ACT.Square).then_inc(n_sq, 1)
                act.wait_ge(n_ss, m + 1)
                A(two(rs), halves(4), ACT.Sqrt, bias=eps[:, 0:1], scale=1.0 / D).then_inc(n_rt, 1)

            act.wait_ge(ld_x, 32)
            act.wait_ge(dt_q, 1)
            with act.Fori(0, DEPTH) as l:
                own.restart()
                tile0 = l * TILES_L
                act.wait_ge(m_acc, l * NG * KT + ACC0)
                norm(2 * l)
                act.wait_ge(pj, tile0 + 1)
                A(two(dtr[0:H_SSD, :]), PS[0:H_SSD, 6:8, 0:HALF], ACT.Copy).then_inc(dt_raw, 1)

                def take_tile(g, s, func, done):
                    act.wait_ge(pj, tile0 + g * RING + s + 2)
                    own.then(A(two(P[:, g * RING + s, :]), halves(2 * (s % 2)), func))
                    act.sem_inc(pj_free, 1)
                    act.sem_inc(w_free, 1)
                    act.sem_inc(done, 1)

                def activate(g, s, func):
                    act.wait_ge(conv, 16 * l + g * RING + s + 1)
                    A(P[:, g * RING + s, :], cv[:, s % 2, :], func).then_inc(act_x, 1)

                def group_loop(a, b, func, done, post=None, post_func=None):
                    with act.Fori(a, b) as g:
                        own.restart()
                        for s in range(RING):
                            take_tile(g, s, func, done)
                            if post is not None:
                                activate(g - post, s, post_func)

                act.sem_inc(pj_free, 1)
                group_loop(0, 1, ACT.Copy, raw)
                act.wait_ge(dt_q, 2 * l + 2)
                A(row(5), row(5), ACT.Exp, scale=-1.0).then_inc(dt_e, 1)
                A(c8[:, 1, :], c8[:, 1, :], ACT.Exp, scale=-1.0).then_inc(dt_e, 1)
                A(nA[:, :], head[:, 1:2], ACT.Exp).then_inc(dt_e, 1)
                group_loop(1, 4, ACT.Copy, raw)
                act.wait_ge(dt_q, 2 * l + 3)
                A(row(R_TE)[:, 0:SEQ], row(R_TE)[:, 0:SEQ], ACT.Exp).then_inc(dt_e, 1)
                A(row(R_CUM)[:, SEQ:T], row(4)[:, SEQ:T], ACT.Exp).then_inc(dt_e, 1)
                group_loop(4, 7, ACT.Copy, raw, 4, ACT.Silu)
                group_loop(7, 8, ACT.Silu, mixin, 4, ACT.Copy)
                with act.Fori(0, NS // RING) as i:
                    own.restart()
                    for s in range(RING):
                        n = l * NS + i * RING + s
                        b = s % 2
                        take_tile(i + 8, s, ACT.Silu, mixin)
                        act.wait_ge(s_y, n + 1)
                        act.dma_start(o_ssd_s[l, i * RING + s], st_s_t[b].rearrange("p a b -> p (a b)")).then_inc(st_s[b], 16)
                        act.dma_start(o_ret_s[l, i * RING + s], sr_s_t[b].rearrange("p a b -> p (a b)")).then_inc(st_s[b], 16)
                        A(P[:, Y_SSD:Y_SSD + 12, bass.ds(i * RING + s + SEQ, 1)], PS[:, 7, H_SSD:H_SSD + 12].unsqueeze(2), ACT.Copy).then_inc(s_ye, 1)
                group_loop(10, 11, ACT.Gelu, mixin)
                act.wait_ge(ck_0, l + 1)
                act.wait_ge(act_x, 16 * l + 16 + 1)
                apart(act)
                with act.Fori(0, NCH) as c:
                    it = l * NCH + c
                    Pc = P[:, :, 0:SEQ].rearrange("p i (c j) -> p i c j", j=CH)
                    act.wait_ge(ck_S, 7 * it + 1)
                    A(xc[:, 0:12, :], Pc[:, XBC:XBC + 12, c, :], ACT.Copy).then_inc(ck_x, 1)
                    act.wait_ge(ck_t, it + 1)
                    act.wait_ge(ck_st, it + 1)
                    A(btok.rearrange("p a b -> p (a b)"), PS[:, 2, 0:2 * CH], ACT.Copy).then_inc(ck_atok, 1)
                    A(vtok.rearrange("p a b -> p (a b)"), PS[:, 4, :], ACT.Copy).then_inc(ck_atok, 1)
                    act.wait_ge(ck_s, it + 1)
                    act.wait_ge(ck_m, 12 * it + 1)
                    A(sc.rearrange("p a b -> p (a b)"), PS[:, 5, 0:2 * CH], ACT.Copy).then_inc(ck_sc, 1)
                    for q in range(4):
                        act.wait_ge(ck_seg, 4 * it + q + 1)
                        if q >= 2:
                            act.wait_ge(ck_y, 4 * it + q - 1)
                            act.wait_ge(ck_m, 12 * it + 3 * (q - 1) + 1)
                        A(dec[:, q % 2, :, :].rearrange("p a b -> p (a b)"), PS[:, 7 - q % 2, :], ACT.Exp).then_inc(ck_exp, 1)
                        A(ec[:, q % 2, :, :].rearrange("p a b -> p (a b)"), PS[:, 2 + q % 2, :], ACT.Exp).then_inc(ck_exp, 1)
                    act.wait_ge(ck_y, 4 * it + 4)
                    A(Pc[:, Y_SSD:Y_SSD + 8, c, :], PS[:, 0:2, :].rearrange("p b (i j) -> p (b i) j", j=CH), ACT.Copy).then_inc(ck_ye, 1)
                    act.wait_ge(ck_yr, it + 1)
                    A(Pc[:, Y_RET:Y_RET + 4, c, :], PS[:, 4, :].rearrange("p (i j) -> p i j", j=CH), ACT.Copy).then_inc(ck_ye, 1)
                act.wait_ge(yn_y, l + 1)
                A(hT[:, :, :], P[:, Y_SSD:Y_SSD + 8, :], ACT.Square).then_inc(yn_sq, 1)
                act.wait_ge(yn_ss, 2 * l + 1)
                A(two(rs), halves(0), ACT.Sqrt, bias=eps[:, 0:1], scale=1.0 / D).then_inc(yn_rt, 1)
                A(hT[:, 0:4, :], P[:, Y_RET:Y_RET + 4, :], ACT.Square).then_inc(yn_sq, 1)
                act.wait_ge(yn_ss, 2 * l + 2)
                A(P[:, 0:4, 0:SEQ], PS[:, 2:6, :], ACT.Sqrt, bias=eps[:, 0:1], scale=1.0 / D_RET).then_inc(yn_rt, 1)
                A(P[:, 0:4, SEQ:T], PS[:, 6, 0:4 * NS].rearrange("p (h s) -> p h s", s=NS), ACT.Sqrt,
                  bias=eps[:, 0:1], scale=1.0 / D_RET).then_inc(yn_rt, 1)
                for i in range(4):
                    for j in range(2):
                        n = 2 * i + j
                        act.wait_ge(lr_p, 8 * l + n + 1)
                        b = 2 * (n % 4)
                        A(two(hT[:, 4 * j + i, :]), halves(b), ACT.Sigmoid,
                          bias=col[:, (C_BA, C_BI)[j] + i:(C_BA, C_BI)[j] + i + 1]).then_inc(lr_a, 1)
                act.wait_ge(lr_a, 8 * l + 8)
                for i in range(4):
                    A(P[:, 4 + i, :], hT[:, i, :], ACT.Exp, scale=c8[:, 4, i:i + 1]).then_inc(lr_t, 1)
                    A(P[:, 8 + i, :], hT[:, i, :], ACT.Tanh, scale=c8[:, 5, i:i + 1]).then_inc(lr_t, 1)
                act.wait_ge(lr_q, l + 1)
                A(P[:, 8:12, :], P[:, 8:12, :], ACT.Sqrt).then_inc(lr_r, 1)
                act.wait_ge(x_mid, KT * l + KT)
                norm(2 * l + 1)
                for b in range(2):
                    act.wait_ge(st_s[b], 32 * (NS // 2) * (l + 1) + 1)
                apart(act)
                with act.Fori(0, 4) as g:
                    own.restart()
                    for s in range(RING):
                        act.wait_ge(pj, tile0 + NT + 9 + g * RING + s + 1)
                        own.then(A(two(qT[:, g * RING + s, :]), halves(2 * (s % 2)), ACT.Copy))
                        act.sem_inc(pj_free, 1)
                        act.sem_inc(w_free, 1)
                        act.sem_inc(q_in, 1)
                def early_gelu(j, e):
                    n = l * NG + j
                    act.wait_ge(m_h, n * GRP + e + 1 + H0)
                    act.wait_ge(a_out[e % 2], 16 * (2 * (l * EARLY + j) + e // 2) + 1)
                    A(two(gh[:, e % 2, :]), halves(2 * (e % 2)), ACT.Gelu).then_inc(m_gelu, 1)

                def take_scores(n):
                    act.wait_ge(q_s, n + 1 + 1)
                    A(s_sb[0:TT, :, :].rearrange("p a b -> p (a b)"), PS[0:TT, 4:8, :].rearrange("p a b -> p (a b)"), ACT.Copy).then_inc(q_sc, 1)

                def choice(t, more):
                    n = l * 5 + t
                    for e in range(GRP):
                        early_gelu(t * 2, e)
                    if more:
                        act.wait_ge(q_free, n + 1)
                        take_scores(n + 1)
                    for e in range(2):
                        early_gelu(t * 2 + 1, e)
                    act.wait_ge(q_sm, n + 1)
                    A(gij[0:TT, 0, :], gij[0:TT, 0, :], ACT.Exp).then_inc(q_ex, 1)
                    for e in range(2, GRP):
                        early_gelu(t * 2 + 1, e)
                    act.wait_ge(q_tp, n + 1 + 1)
                    o = gijT[:, :, 4 * TT:T] if not more else gijT.rearrange("p a (t c) -> p a t c", c=TT)[:, :, t, :]
                    A(o, PS[:, 4, 0:3 * TT].rearrange("p (a c) -> p a c", a=3), ACT.Copy).then_inc(q_tr, 1)

                take_scores(l * 5)
                with act.Fori(0, 4) as t:
                    choice(t, True)
                choice(4, False)

                def gate_quad(n, q, b):
                    act.wait_ge(g_mm, n + q + 1 + 2)
                    o = 4 * (q % QUADS)
                    A(stage[b][:, :, o:o + 4].rearrange("p k t -> p t k"),
                      PS[:, 5 + q % 2, :].rearrange("p (t k) -> p t k", k=KEYS), ACT.Copy).then_inc(g_cp, 1)

                def store_gates(n, blk_i, b):
                    act.wait_ge(g_cp, n + 2)
                    act.dma_start(gates[blk_i], stage[b].rearrange("p k t -> p (k t)")).then_inc(g_out[b], 16)

                with act.Fori(0, NB // 4) as i:
                    for b in range(2):
                        n = l * NB * QUADS + (i * 2 + b) * TILE_PAIR
                        for e in range(GRP):
                            early_gelu(i * 2 + 10 + b, e)
                            for q in range(e * TILE_PAIR // GRP, (e + 1) * TILE_PAIR // GRP):
                                if q == 0:
                                    act.wait_ge(g_out[0], 16 * (7 * l + i * 2 + b) + 1)
                                if q == QUADS:
                                    act.wait_ge(g_out[1], 16 * (6 * l + i * 2 + b) + 1)
                                gate_quad(n, q, q // QUADS)
                                if q % QUADS == QUADS - 1:
                                    store_gates(n + q + 1, (i * 2 + b) * 2 + q // QUADS, q // QUADS)
                n = l * NB * QUADS + (NB - 1) * QUADS
                act.wait_ge(g_out[0], 16 * (7 * l + 6) + 1)
                for q in range(QUADS):
                    gate_quad(n, q, 0)
                store_gates(n + QUADS, NB - 1, 0)
                for b in range(2):
                    act.wait_ge(g_out[b], 16 * (7, 6)[b] * (l + 1) + 1)
                    apart(act)
                    act.wait_ge(a_out[b], 16 * 2 * EARLY * (l + 1) + 1)
                    apart(act)
                with act.Fori(0, NG - EARLY) as i:
                    for e in range(GRP):
                        act.wait_ge(m_h, (l * NG + EARLY + i) * GRP + e + 1 + H0)
                        act.wait_ge(m_w, (l * NG + i) * GRP + e + W0 - 1)
                        A(two(gh[:, e % 2, :]), halves(2 * (e % 2)), ACT.Gelu).then_inc(m_gelu, 1)
            act.wait_ge(m_acc, DEPTH * NG * KT + ACC0)
            norm(2 * DEPTH)
            for b in range(2):
                act.wait_ge(st_s[b], 32 * DEPTH * (NS // 2) + 1)

        @block.vector
        def _(dve):
            own = Order(dve, v_seq)
            ts, tt, stt = dve.tensor_scalar, dve.tensor_tensor, dve.scalar_tensor_tensor

            def norm(m, w_col):
                dve.wait_ge(n_rt, m + 1)
                own.then(dve.reciprocal(rs, rs))
                for k in range(KT):
                    stt(hT[:, k, :], xT[:, k, :], w_col[:, k:k + 1], rs, ALU.mult, ALU.mult).then_inc(n_h, 1)

            def log1p_of(e, s, w, acc):
                own.then(ts(s, e, 2.0, None, ALU.add))
                own.then(dve.reciprocal(s, s))
                own.then(tt(s, e, s, ALU.mult))
                own.then(tt(w, s, s, ALU.mult))
                own.then(ts(acc, w, 1.0 / 17, None, ALU.mult))
                for k in (15, 13, 11, 9, 7, 5, 3):
                    own.then(stt(acc, acc, 1.0 / k, w, ALU.add, ALU.mult))
                own.then(stt(acc, acc, 1.0, s, ALU.add, ALU.mult))

            dve.memset(eps[:, :], EPS).then_inc(dt_q, 1)
            dve.wait_ge(ld_x, 32)
            with dve.Fori(0, DEPTH) as l:
                own.restart()
                tile0 = l * TILES_L
                dve.wait_ge(ld_small, 96 * l + 96)
                norm(2 * l, col[:, C_N1:C_N1 + 8])
                dve.wait_ge(small_out, l + 1)
                for tap in range(2):
                    own.mark(dve.tensor_copy(cbn[:, :, tap, :], cb[:, :, tap + 1, :]))
                own.settle()
                dve.wait_ge(dt_raw, l + 1)
                lam = col[:, C_LAM:C_LAM + 4]
                own.then(ts(row(4), dtr[0:H_SSD, :], head[:, 0:1], None, ALU.add))
                own.then(stt(row(5), row(4), -1.0, row(4), ALU.mult, ALU.max))
                own.mark(ts(row(4), row(4), 0.0, None, ALU.max))
                own.mark(ts(c8[:, 0, :], lam, -1.0, 0.0, ALU.mult, ALU.max))
                own.then(stt(c8[:, 1, :], lam, -1.0, lam, ALU.mult, ALU.max))
                dve.sem_inc(dt_q, 1)
                dve.wait_ge(dt_e, 5 * l + 3)
                log1p_of(row(5), row(6), row(7), row(2))
                own.then(stt(row(R_DT), row(2), 2.0, row(4), ALU.mult, ALU.add))
                log1p_of(c8[:, 1, :], c8[:, 2, :], c8[:, 3, :], c8[:, 5, :])
                own.then(stt(c8[:, 0, :], c8[:, 5, :], 2.0, c8[:, 0, :], ALU.mult, ALU.add))
                own.mark(ts(c8[:, 4, :], c8[:, 0, :], -8.0, None, ALU.mult))
                own.mark(ts(c8[:, 5, :], c8[:, 0, :], 8.0, None, ALU.mult))
                own.then(ts(nA[:, :], nA[:, :], -1.0, None, ALU.mult))
                own.then(ts(row(4), row(R_DT), nA[:, 0:1], None, ALU.mult))
                for c in range(NCH):
                    o = slice(c * CH, (c + 1) * CH)
                    own.mark(dve.tensor_tensor_scan(row(R_CUM)[:, o], C[0:H_SSD, K_ONE:K_ONE + CH], row(4)[:, o], 0.0, ALU.mult, ALU.add))
                own.settle()
                cum4 = row(R_CUM)[:, 0:SEQ].rearrange("p (c j) -> p c j", j=CH)
                own.mark(ts(row(R_NCUM)[:, 0:SEQ], row(R_CUM)[:, 0:SEQ], -1.0, None, ALU.mult))
                own.then(tt(row(R_TE)[:, 0:SEQ].rearrange("p (c j) -> p c j", j=CH),
                            cum4[:, :, CH - 1:CH].to_broadcast([H_SSD, NCH, CH]), cum4, ALU.subtract))
                dve.sem_inc(dt_q, 1)
                dve.wait_ge(dt_e, 5 * l + 5)
                tt(row(R_TE)[:, 0:SEQ], row(R_TE)[:, 0:SEQ], row(R_DT)[:, 0:SEQ], ALU.mult).then_inc(dt_r, 1)
                cw = col[:, C_CW:C_CW + 64].rearrange("p (i k) -> p i k", k=4)
                with dve.Fori(0, 4) as g:
                    own.restart()
                    for s in range(RING):
                        i = g * RING + s
                        X, o = P[:, i, :], cv[:, s % 2, :]
                        dve.wait_ge(raw, 28 * l + i + 1)
                        if s < 2:
                            dve.wait_ge(act_x, 16 * l + g * RING + 1)
                        else:
                            dve.wait_ge(act_x, 16 * l + i - 1 + 1)
                        own.then(ts(o, X, cw[:, i, 3:4], col[:, bass.ds(i + C_CB, 1)], ALU.mult, ALU.add))
                        for tap in range(3):
                            back = 3 - tap
                            own.mark(stt(o[:, back:SEQ], X[:, 0:SEQ - back], cw[:, i, tap:tap + 1], o[:, back:SEQ], ALU.mult, ALU.add))
                            own.then(stt(o[:, SEQ:T], cb[:, i, tap, :], cw[:, i, tap:tap + 1], o[:, SEQ:T], ALU.mult, ALU.add))
                        own.mark(dve.tensor_copy(tail[:, i, :], X[:, SEQ - 3:SEQ]))
                        own.then(dve.tensor_copy(cbn[:, i, 2, :], X[:, SEQ:T]))
                        dve.sem_inc(conv, 1)
                own.restart()
                dve.wait_ge(raw, 28 * l + 28)
                apart(dve)
                with dve.Fori(0, 4) as i:
                    own.restart()
                    for j, t0 in enumerate((KV, Q)):
                        X = P[:, t0 + i, :]
                        dve.wait_ge(rot_p, 8 * l + i * 2 + j + 1)
                        own.mark(tt(two(rt[:, j, :]), halves(4 + 2 * j), two(C[:, K_SIN:K_SIN + T]), ALU.mult))
                        own.then(tt(X, X, C[:, K_COS:K_COS + T], ALU.mult))
                        tt(X, X, rt[:, j, :], ALU.add).then_inc(rot_x, 1)
                own.restart()
                dve.wait_ge(s_t, l + 1)
                own.mark(dve.tensor_copy(sdt[0:NS, :], PS[0:NS, 7, 0:H_SSD]))
                own.mark(dve.tensor_copy(tk_s[0:NS, D:D + H_SSD], PS[0:NS, 7, H_SSD:2 * H_SSD]))
                own.then(ts(tk_s[0:NS, D + H_SSD:RW], PS[0:NS, 6, :], SCALE, None, ALU.mult))
                own.then(tt(tk_s[0:NS, 0:D].rearrange("p (h q) -> p h q", q=P_SSD), PS[0:NS, 4:6, :].rearrange("p b (h q) -> p (b h) q", q=P_SSD),
                            sdt[0:NS, :].unsqueeze(2).to_broadcast([NS, H_SSD, P_SSD]), ALU.mult))
                with dve.Fori(0, NS // 2) as i:
                    for b in range(2):
                        own.restart()
                        n = l * NS + i * 2 + b
                        cur = bass.ds(i * 2 + b + SEQ, 1)
                        s, r = st_s_t[b], sr_s_t[b]
                        dve.wait_ge(s_bc, n + 1)
                        ts(rm_s[0:NS, :], tk_s[0:NS, :], C[0:NS, bass.ds(i * 2 + b + K_ID, 1)], None, ALU.mult).then_inc(s_rm, 1)
                        dve.wait_ge(ld_s[b], 32 * (l * (NS // 2) + i + 1))
                        for h in range(H_RET):
                            own.mark(ts(r[:, h, :], r[:, h, :], GAMMA[h], None, ALU.mult))
                        dve.wait_ge(s_bc, n + 1 + 1)
                        own.then(dve.tensor_copy(ab_s, PS[:, 7, 0:H_SSD]))
                        own.then(tt(s, s, ab_s.unsqueeze(2).to_broadcast([128, H_SSD, P_SSD]), ALU.mult))
                        for g in range(2):
                            own.mark(stt(s[:, 8 * g:8 * g + 8, :].rearrange("p h q -> p (h q)"), PS[:, 4 + g, :], P[:, XBC + 8 + g, cur],
                                         s[:, 8 * g:8 * g + 8, :].rearrange("p h q -> p (h q)"), ALU.mult, ALU.add))
                        for h in range(H_RET):
                            own.mark(stt(r[:, h, :], PS[:, 6, h * D_RET:(h + 1) * D_RET], P[:, KV + h, cur], r[:, h, :], ALU.mult, ALU.add))
                        own.settle()
                        dve.sem_inc(s_new, 1)
                own.restart()
                dve.wait_ge(pj, tile0 + 1 + NT)
                own.then(dve.tensor_copy(hT[0:H_SSD, 0:4, 0:SEQ], rows_kept[0:H_SSD, :, 0:SEQ]))
                for b in range(2):
                    dve.wait_ge(st_s[b], 32 * (NS // 2) * (l + 1) + 1)
                    apart(dve)
                dve.wait_ge(states_out, l + 1)
                own.mark(dve.memset(S, 0.0))
                own.then(dve.memset(Sr, 0.0))
                dve.sem_inc(ck_0, 1)
                dve.wait_ge(rot_x, 8 * l + 8 + 1)
                apart(dve)
                with dve.Fori(0, NCH) as c:
                    own.restart()
                    it = l * NCH + c
                    bc = lambda ap, n: ap.unsqueeze(2).to_broadcast([128, ap.shape[1], n])
                    X = PS[:, 0:2, :].rearrange("p b (h q) -> p (b h) q", q=P_SSD)
                    Pc = P[:, :, 0:SEQ].rearrange("p i (c j) -> p i c j", j=CH)
                    dve.tensor_copy(xc[:, 12:24, :], Pc[:, KV:KV + 12, c, :]).then_inc(ck_x, 1)
                    dve.wait_ge(ck_t, it + 1)
                    own.then(dve.tensor_copy(tok, PS[:, 7, 0:2 * H_SSD].rearrange("p (a h) -> p a h", a=2)))
                    dve.sem_inc(ck_tok, 1)
                    tt(vdt, X, bc(tok[:, 0, :], P_SSD), ALU.mult).then_inc(ck_tok, 1)
                    tt(vend, X, bc(tok[:, 1, :], P_SSD), ALU.mult).then_inc(ck_tok, 1)
                    tt(kend, PS[:, 3, :].rearrange("p (h j) -> p h j", j=CH), bc(C[:, K_TE:K_TE + 4], CH), ALU.mult).then_inc(ck_tok, 1)
                    dve.wait_ge(ck_s, it + 1)
                    tt(mr, PS[:, 6, :].rearrange("p (h j) -> p h j", j=CH), C[:, K_DM:K_DM + 4 * CH].rearrange("p (h j) -> p h j", j=CH),
                       ALU.mult).then_inc(ck_mr, 1)
                    tt(xc[:, 20:24, :], xc[:, 20:24, :], C[:, K_GAM:K_GAM + 4 * CH].rearrange("p (h j) -> p h j", j=CH),
                       ALU.mult).then_inc(ck_mr, 1)
                    dve.wait_ge(ck_sc, it + 1)
                    for q in range(4):
                        g = q // 2
                        dve.wait_ge(ck_exp, 8 * it + 2 * q + 2)
                        dve.tensor_copy(cd[:, 4 * q:4 * q + 4].unsqueeze(2), ec[:, q % 2, :, CH - 1:CH]).then_inc(ck_m, 1)
                        dve.wait_ge(ck_m, 12 * it + 3 * q + 1 + 1)
                        tt(dec[:, q % 2, :, :], dec[:, q % 2, :, :], sc[:, g:g + 1, :].to_broadcast([128, 4, CH]), ALU.mult).then_inc(ck_m, 1)
                        tt(ec[:, q % 2, :, :], ec[:, q % 2, :, :], xc[:, 10 + g:11 + g, :].to_broadcast([128, 4, CH]), ALU.mult).then_inc(ck_m, 1)
                    dve.wait_ge(ck_st, it + 1 + 1)
                    own.then(tt(S, S, bc(cd, P_SSD), ALU.mult))
                    for g in range(2):
                        tt(S[:, 8 * g:8 * g + 8, :], S[:, 8 * g:8 * g + 8, :],
                           PS[:, (5, 2)[g], :].rearrange("p (h q) -> p h q", q=P_SSD), ALU.add).then_inc(ck_S, 1)
                    for h in range(H_RET):
                        stt(Sr[:, h, :], Sr[:, h, :], GAMMA_CH[h], PS[:, 3, h * CH:(h + 1) * CH], ALU.mult, ALU.add).then_inc(ck_S, 1)
                    dve.wait_ge(ck_S, 7 * it + 6 + 1)
                    dve.sem_inc(ck_S, 1)
                own.restart()
                dve.wait_ge(s_ye, NS * (l + 1) + 1)
                dve.wait_ge(ck_ye, 2 * NCH * (l + 1) + 1)
                dve.wait_ge(mixin, 16 * (l + 1))
                for i in range(8):
                    own.mark(stt(P[:, Y_SSD + i, :], P[:, XBC + i, :], col[:, C_D + i:C_D + i + 1], P[:, Y_SSD + i, :], ALU.mult, ALU.add))
                own.settle()
                own.then(tt(P[:, Y_SSD:Y_SSD + 8, :], P[:, Y_SSD:Y_SSD + 8, :], P[:, Z:Z + 8, :], ALU.mult))
                dve.sem_inc(yn_y, 1)
                dve.wait_ge(yn_rt, 3 * l + 1)
                own.then(dve.reciprocal(rs, rs))
                for i in range(8):
                    stt(P[:, Z + i, :], P[:, Y_SSD + i, :], col[:, C_NW + i:C_NW + i + 1], rs, ALU.mult, ALU.mult).then_inc(yn_m, 1)
                dve.wait_ge(yn_rt, 3 * l + 3)
                own.then(dve.reciprocal(P[:, 0:4, :], P[:, 0:4, :]))
                own.then(tt(P[:, Y_RET:Y_RET + 4, :], P[:, Y_RET:Y_RET + 4, :], P[:, 0:4, :], ALU.mult))
                tt(P[:, G:G + 4, :], P[:, Y_RET:Y_RET + 4, :], P[:, G:G + 4, :], ALU.mult).then_inc(yn_m, 1)
                dve.wait_ge(lr_t, 8 * l + 8)
                own.then(ts(hT[:, 0:4, :], P[:, 8:12, :], 1.0, None, ALU.add))
                own.then(dve.reciprocal(hT[:, 0:4, :], hT[:, 0:4, :]))
                own.then(stt(P[:, 8:12, :].rearrange("p a b -> p (a b)"), P[:, 8:12, :].rearrange("p a b -> p (a b)"), 2.0,
                             hT[:, 0:4, :].rearrange("p a b -> p (a b)"), ALU.mult, ALU.mult))
                dve.sem_inc(lr_q, 1)
                own.then(tt(hT[:, 4:8, :], hT[:, 4:8, :], P[:, XR:XR + 4, :], ALU.mult))
                dve.wait_ge(lr_r, l + 1)
                own.then(tt(P[:, 8:12, :], P[:, 8:12, :], hT[:, 4:8, :], ALU.mult))
                for i in range(4):
                    own.mark(dve.tensor_tensor_scan(hT[:, i, 0:SEQ], P[:, 4 + i, 0:SEQ], P[:, 8 + i, 0:SEQ], 0.0, ALU.mult, ALU.add))
                own.then(tt(hT[:, 0:4, SEQ:T], P[:, 4:8, SEQ:T], lru0[:, :, :], ALU.mult))
                own.then(tt(hT[:, 0:4, SEQ:T], hT[:, 0:4, SEQ:T], P[:, 8:12, SEQ:T], ALU.add))
                dve.tensor_copy(lruo[:, :, :], hT[:, 0:4, SEQ - 1:T]).then_inc(lr_h, 1)
                tt(P[:, GATE:GATE + 4, :], hT[:, 0:4, :], P[:, GATE:GATE + 4, :], ALU.mult).then_inc(lr_h, 1)
                dve.wait_ge(lr_h, 3 * l + 2)
                dve.sem_inc(lr_h, 1)
                own.restart()
                with dve.Fori(0, 2) as g:
                    own.restart()
                    for m in range(RING):
                        dve.wait_ge(pj, tile0 + NT + 1 + g * RING + m + 1)
                        X = two(xT[:, g * RING + m, :])
                        own.then(tt(X, X, halves(2 * m), ALU.add))
                        dve.sem_inc(x_mid, 1)
                        dve.sem_inc(pj_free, 1)
                own.restart()
                norm(2 * l + 1, col[:, C_N2:C_N2 + 8])
                with dve.Fori(0, 5) as t:
                    own.restart()
                    n = l * 5 + t
                    R = slice(0, TT)

                    def top16(vals, rows, out, idx):
                        for half in range(2):
                            o = slice(8 * half, 8 * half + 8)
                            for i in range(rows):
                                own.mark(dve.max(out[R, i, o], vals[R, i, :]))
                            own.settle()
                            for i in range(rows):
                                own.mark(dve.max_index(idx[R, i, o], out[R, i, o], vals[R, i, :]))
                            own.settle()
                            if half == 0:
                                for i in range(rows):
                                    own.mark(dve.match_replace(vals[R, i, :], out[R, i, o], vals[R, i, :], -3.0e38))
                                own.settle()

                    dve.wait_ge(q_sc, n + 1 + 1)
                    apart(dve)
                    top16(s_sb, HC, s_top, i_u)
                    dve.sem_inc(q_free, 1)
                    own.mark(dve.tensor_copy(i_f[R], i_u[R]))
                    pair = s_top[R].rearrange("p (h c) j -> p h c j", c=2)
                    c4 = cand[R].rearrange("p h (a b) -> p h a b", b=TOPK)
                    shape = [TT, H_PEER, TOPK, TOPK]
                    own.then(tt(c4, pair[:, :, 0, :].unsqueeze(3).to_broadcast(shape), pair[:, :, 1, :].unsqueeze(2).to_broadcast(shape), ALU.add))
                    top16(cand, H_PEER, c_top, sel)
                    sel1 = sel[R].rearrange("p h k -> p (h k)")
                    own.mark(ts(j_u[R, 0, :], sel1, 4, None, ALU.logical_shift_right))
                    own.mark(ts(j_u[R, 1, :], sel1, 15, None, ALU.bitwise_and))
                    dve.wait_ge(q_tp, n + 1)
                    own.then(tt(gij[R, 0, :].rearrange("p (h k) -> p h k", k=TOPK), c_top[R],
                                c_top[R, :, 0:1].to_broadcast([TT, H_PEER, TOPK]), ALU.subtract))
                    dve.sem_inc(q_sm, 1)
                    own.then(dve.tensor_copy(j_f[R], j_u[R]))
                    for side in range(2):
                        own.then(tt(oh[R], C[R, K_IOTA:K_IOTA + TOPK].unsqueeze(1).to_broadcast([TT, SLOTS, TOPK]),
                                    j_f[R, side, :].unsqueeze(2).to_broadcast([TT, SLOTS, TOPK]), ALU.is_equal))
                        oh4 = oh[R].rearrange("p (h k) j -> p h k j", k=TOPK)
                        own.then(tt(oh4, oh4, i_f[R].rearrange("p (h c) j -> p h c j", c=2)[:, :, side, :].unsqueeze(2).to_broadcast(shape), ALU.mult))
                        own.then(dve.tensor_reduce(gij[R, 1 + side, :].unsqueeze(2), oh[R], AX.X, ALU.add))
                    dve.wait_ge(q_ex, n + 1)
                    g3 = gij[R, 0, :].rearrange("p (h k) -> p h k", k=TOPK)
                    own.then(dve.tensor_reduce(gsum[R, 0, :].unsqueeze(2), g3, AX.X, ALU.add))
                    own.then(dve.reciprocal(gsum[R, 1, :], gsum[R, 0, :]))
                    tt(g3, g3, gsum[R, 1, :].unsqueeze(2).to_broadcast([TT, H_PEER, TOPK]), ALU.mult).then_inc(q_g, 1)

                dve.wait_ge(q_tr, 5 * l + 5 + 1)
                own.restart()
                with dve.Fori(0, T // 8) as i:
                    for s in range(8):
                        if s % 4 == 0:
                            dve.wait_ge(g_mm, (l * (T // 8) + i) * 2 + s // 4 + 1)
                        t = bass.ds(i * 8 + s, 1)
                        ts(Ah[:, s, :], iota, gijT[:, 1, t], gijT[:, 0, t], ALU.is_equal, ALU.mult).then_inc(g_ab, 1)
                        ts(Bh[:, s, :], iota, gijT[:, 2, t], None, ALU.is_equal).then_inc(g_ab, 1)

                def gating(n, b, loads, early_loads=None):
                    dve.wait_ge(ld_g[b], 16 * loads)
                    if early_loads is not None:
                        dve.wait_ge(ld_a[b], 16 * early_loads)
                    dve.wait_ge(m_y, n * KT + Y0 - KT)
                    for e in range(GRP):
                        if early_loads is None:
                            dve.wait_ge(m_gelu, (n + EARLY) * GRP + e + 1 + GE0)
                        g = gh[:, e % 2, :] if early_loads is None else ga[b][:, e, :]
                        tt(W[b][:, e, :].rearrange("p (n c) -> p n c", c=BT), g.rearrange("p (n c) -> p n c", c=BT),
                           gt[b][:, :, e * BT:(e + 1) * BT], ALU.mult).then_inc(m_w, 1)

                def adding(n):
                    for d in range(KT):
                        dve.wait_ge(m_y, n * KT + d + 1 + Y0)
                        X = two(xT[:, d, :])
                        tt(X, X, halves(4 + 2 * (d % 2)), ALU.add).then_inc(m_acc, 1)

                n0, ld0 = l * NG, l * (NG // 2)
                LATE = NG - EARLY
                gating(n0, 0, ld0 + 1)
                with dve.Fori(0, LATE // 2 - 1) as i:
                    gating(n0 + i * 2 + 1, 1, ld0 + i + 1)
                    adding(n0 + i * 2)
                    gating(n0 + i * 2 + 2, 0, ld0 + i + 2)
                    adding(n0 + i * 2 + 1)
                gating(n0 + LATE - 1, 1, ld0 + LATE // 2)
                adding(n0 + LATE - 2)
                with dve.Fori(0, EARLY // 2) as i:
                    for b in range(2):
                        n = n0 + LATE + i * 2 + b
                        gating(n, b, ld0 + LATE // 2 + i + 1, l * (EARLY // 2) + i + 1)
                        adding(n - 1)
                adding(n0 + NG - 1)
                dve.wait_ge(m_acc, KT * NG * (l + 1) + ACC0)
            own.restart()
            norm(2 * DEPTH, C[:, K_FW:K_FW + 8])


def kernel(**inputs):
    import concourse.bacc as _bacc
    from concourse.bass_utils import run_bass_kernel_spmd as _run

    i = {k: np.ascontiguousarray(v) for k, v in inputs.items()}
    def feat(a):
        return a.reshape(DEPTH, -1, 128).transpose(0, 2, 1)

    stream = np.concatenate([i["x_prompt"][0], i["x_sample"][:, 0]])
    ins = {"x": stream.reshape(T, KT, 128).transpose(2, 1, 0)}

    wi = i["w_in"]
    cut = lambda a, b: wi[:, :, a:b]
    order = [cut(1024, 2560), cut(5136, 5648), cut(3088, 3600), cut(3600, 4112), cut(2576, 3088),
             cut(0, 1024), cut(4112, 4624), cut(4624, 5136)]
    w_main = np.concatenate(order, axis=2)
    units = lambda a: a.reshape(DEPTH, -1, 8, 128, a.shape[2] // 128, 128).transpose(0, 4, 1, 3, 2, 5).reshape(DEPTH, -1, 128, 8, 128)
    out_units = units(i["w_out"]).reshape(DEPTH, 2, 4, 2, 128, 8, 128).swapaxes(2, 3).reshape(DEPTH, 16, 128, 8, 128)
    ins["w"] = np.concatenate([units(w_main), out_units, units(i["peer_wq"])], axis=1)
    ins["wdt"] = cut(2560, 2576).reshape(DEPTH, 8, 128, 16).transpose(0, 2, 1, 3)
    ins["keys"] = i["peer_keys"].reshape(DEPTH, HC, KEYS, 128).transpose(0, 3, 1, 2)
    ins["u_tab"] = i["peer_u"].reshape(DEPTH, NG, GRP * 128, 8, 128).transpose(0, 1, 4, 3, 2)
    ins["v_tab"] = i["peer_v"].reshape(DEPTH, NG, GRP, 128, D).transpose(0, 1, 3, 2, 4)
    convw = np.concatenate([i["ssd_conv_w"], i["lru_conv_w"]], axis=2)
    convb = np.concatenate([i["ssd_conv_b"], i["lru_conv_b"]], axis=1)
    ins["cols"] = np.concatenate([
        feat(i["norm1_w"]), feat(i["norm2_w"]),
        convw.reshape(DEPTH, 4, 16, 128).transpose(0, 3, 2, 1).reshape(DEPTH, 128, 64), feat(convb),
        feat(np.repeat(i["ssd_d"], P_SSD, axis=1)), feat(i["ssd_norm_w"]),
        feat(i["lru_ba"]), feat(i["lru_bi"]), feat(i["lru_lambda"])], axis=2)
    ins["heads"] = np.stack([i["ssd_dt_bias"], i["ssd_a_log"]], axis=2)
    cbuf = np.concatenate([i["state_ssd_conv"], i["state_lru_conv"]], axis=3)
    ins["cbuf"] = cbuf.reshape(DEPTH, NS, 3, 16, 128).transpose(0, 4, 3, 2, 1)
    ins["h0"] = i["state_lru"].reshape(DEPTH, NS, 4, 128).transpose(0, 3, 2, 1)
    blk = np.zeros((DEPTH, 128, 8, 128), np.float32)
    for j, name in enumerate(("lru_wa", "lru_wi")):
        for k in range(8):
            a = 64 * (k % 2)
            blk[:, a:a + 64, 4 * j + k // 2, a:a + 64] = i[name][:, k]
    ins["wblk"] = blk
    ins["s_ssd"] = i["state_ssd"].transpose(0, 1, 3, 2, 4)
    ins["s_ret"] = i["state_ret"].transpose(0, 1, 3, 2, 4)

    pos = np.concatenate([np.arange(SEQ), np.full(NS, PAST)]).astype(np.float32)
    inv = (np.float32(10000.0) ** (-np.arange(64, dtype=np.float32) / np.float32(64))).astype(np.float32)
    ang = np.tile((inv[:, None] * pos[None, :]).astype(np.float32), (2, 1)).astype(np.float64)
    perm = np.zeros((128, 128))
    perm[np.arange(64) + 64, np.arange(64)] = -1.0
    perm[np.arange(64), np.arange(64) + 64] = 1.0
    j, k = np.arange(CH)[:, None], np.arange(CH)[None, :]
    mask = np.where(k >= j, 0.0, -1e30)
    lg = np.log(1.0 - 2.0 ** (-5.0 - np.arange(H_RET)))
    dm = np.stack([np.where(k >= j, np.exp((k - j) * g), 0.0) * SCALE for g in lg], axis=1).reshape(128, -1)
    gam = np.tile(np.concatenate([np.exp((np.arange(CH) + 1) * g) for g in lg])[None], (128, 1))
    te = np.stack([np.exp((CH - 1 - np.arange(CH)) * g) * SCALE for g in lg], axis=1)
    cst = np.concatenate([np.cos(ang), np.sin(ang), perm, np.eye(128), mask, dm, gam, te,
                          np.tile(np.arange(128.0)[None], (128, 1)), np.ones((128, 128))], axis=1).astype(np.float32)
    ins["cst"] = np.concatenate([cst, i["final_norm_w"].reshape(KT, 128).T], axis=1)

    outs = {"y": (128, KT, T), "o_ssd_p": (DEPTH, 128, 1024), "o_ret_p": (DEPTH, 128, 512), "o_tail": (DEPTH, 128, 16, 3),
            "o_cbuf": (DEPTH, 128, 16, 3, NS), "o_lru": (DEPTH, 128, 4, 1 + NS),
            "o_ssd_s": (DEPTH, NS, 128, 1024), "o_ret_s": (DEPTH, NS, 128, 512)}
    nc = _bacc.Bacc("TRN2", target_bir_lowering=False, num_devices=1)
    ins = {n: np.ascontiguousarray(a, dtype=np.float32) for n, a in ins.items()}
    args = {n: nc.dram_tensor(n, a.shape, F32, kind="ExternalInput").ap() for n, a in ins.items()}
    args["gates"] = nc.dram_tensor("gates", (NB, 128, KEYS * BT), F32, kind="Internal").ap()
    args["early"] = nc.dram_tensor("early", (EARLY, 128, GRP * T), F32, kind="Internal").ap()
    args |= {n: nc.dram_tensor(n, s, F32, kind="ExternalOutput").ap() for n, s in outs.items()}
    decoder_step(nc, **args)
    r = _run(nc, [ins], core_ids=[0]).results[0]

    y = r["y"].transpose(2, 1, 0).reshape(T, D)
    tail = r["o_tail"].transpose(0, 3, 2, 1).reshape(DEPTH, 1, 3, 2048)
    cbn = r["o_cbuf"].transpose(0, 4, 3, 2, 1).reshape(DEPTH, NS, 3, 2048)
    lru = r["o_lru"].transpose(0, 3, 2, 1).reshape(DEPTH, 1 + NS, 512)
    head_major = lambda a, h: a.reshape(a.shape[:-1] + (h, -1)).swapaxes(-3, -2)
    c = np.ascontiguousarray
    return (c(y[None, :SEQ]), c(y[SEQ:, None]),
            c(head_major(r["o_ssd_p"], H_SSD)[:, None]), c(tail[..., :1536]), c(head_major(r["o_ret_p"], H_RET)[:, None]),
            c(lru[:, :1]), c(tail[..., 1536:]),
            c(head_major(r["o_ssd_s"], H_SSD)), c(cbn[..., :1536]), c(head_major(r["o_ret_s"], H_RET)),
            c(lru[:, 1:]), c(cbn[..., 1536:]))
```

```python
from contextlib import ExitStack

import numpy as np

import concourse.bass as bass
from concourse import mybir

F32 = mybir.dt.float32
U32 = mybir.dt.uint32
ACT = mybir.ActivationFunctionType
ALU = mybir.AluOpType
AX = mybir.AxisListType

DEPTH, D, SEQ, NS = 2, 1024, 512, 8
T = SEQ + NS
HALF = T // 2
PAST = 4096
EPS = 1e-6
KT = D // 128
H_SSD, P_SSD, N_SSD = 16, 64, 128
H_RET, D_RET = 4, 128
KEYS, H_PEER, TOPK = 128, 8, 16
HC = 2 * H_PEER
SLOTS = H_PEER * TOPK
CH = 128
NCH = SEQ // CH

XBC, XR, KV, Q, Z, G, GATE = 0, 12, 16, 24, 28, 36, 40
NT = 44
Y_SSD, Y_RET, MIX = 16, 24, 28
UNITS = NT + 16 + 16
RING = 4
TILES_L = 1 + NT + 8 + 16

TT = T // 5
NB, BT = 13, T // 13
QUADS = BT // 4
GRP = 4
NG = KEYS // GRP
EARLY = NG // 2
TILE_PAIR = 2 * QUADS
AB = BT

C_N1, C_N2, C_CW, C_CB, C_D, C_NW, C_BA, C_BI, C_LAM, NCOL = 0, 8, 16, 80, 96, 104, 112, 116, 120, 124
K_COS, K_SIN, K_PERM, K_ID, K_MASK, K_DM, K_GAM, K_TE, K_IOTA, K_ONE, K_FW, NCST = np.cumsum(
    [0, T, T, 128, 128, 128, 4 * CH, 4 * CH, 4, 128, 128, 8]).tolist()
CHEAD = 16

GAMMA_CH = [float((1.0 - 2.0 ** (-5 - h)) ** CH) for h in range(H_RET)]
GAMMA = [float(1.0 - 2.0 ** (-5 - h)) for h in range(H_RET)]
SCALE = D_RET ** -0.5


def decoder_step(nc, x, w, wdt, keys, u_tab, v_tab, cols, heads, cbuf, h0, wblk, s_ssd, s_ret, cst, gates, early,
                 y, o_ssd_p, o_ret_p, o_tail, o_cbuf, o_lru, o_ssd_s, o_ret_s):
    with ExitStack() as ctx:
        def sb(name, shape):
            return ctx.enter_context(nc.sbuf_tensor(name, shape, F32))

        def sem(name):
            return ctx.enter_context(nc.semaphore(name))

        xT = sb("xT", [128, KT, T])
        hT = sb("hT", [128, KT, T])
        ring = sb("ring", [128, RING, 8, 128])
        C = sb("C", [128, NCST])
        mask = ctx.enter_context(nc.sbuf_tensor("mask", [128, 2, 128], mybir.dt.bfloat16))
        col = sb("col", [128, NCOL])
        head = sb("head", [H_SSD, 2])
        cb = sb("cb", [128, 16, 3, NS])
        cbn = sb("cbn", [128, 16, 3, NS])
        tail = sb("tail", [128, 16, 3])
        lru0 = sb("lru0", [128, 4, NS])
        lruo = sb("lruo", [128, 4, 1 + NS])
        blk = sb("blk", [128, 8, 128])
        wd = sb("wd", [128, 8, 16])
        eps = sb("eps", [128, 1])
        c8 = sb("c8", [128, 6, 4])
        nA = sb("nA", [H_SSD, 1])
        PN = NT * T
        AN = PN + 11360
        AR = sb("AR", [128, AN])
        P = AR[:, 0:PN].rearrange("p (i t) -> p i t", t=T)
        top = [PN]

        def take(shape):
            n = int(np.prod(shape))
            ap = AR[:, top[0]:top[0] + n]
            top[0] += n
            assert top[0] <= AN, (top[0], AN)
            if len(shape) == 2:
                ap = ap.rearrange("p (a b) -> p a b", b=shape[1])
            if len(shape) == 3:
                ap = ap.rearrange("p (a b c) -> p a b c", b=shape[1], c=shape[2])
            return ap

        xc = take((24, CH))
        vdt = take((H_SSD, P_SSD))
        vend = take((H_SSD, P_SSD))
        btok = take((2, CH))
        vtok = take((H_RET, CH))
        kend = take((H_RET, CH))
        sc = take((2, CH))
        mr = take((H_RET, CH))
        dec = take((2, 4, CH))
        ec = take((2, 4, CH))
        cd = take((H_SSD,))
        tok = take((3, H_SSD))
        crow = take((4, CH))
        S = take((H_SSD, P_SSD))
        Sr = take((H_RET, D_RET))
        top[0] = PN
        rs = take((T,))
        cv = take((2, T))
        rt = take((2, T))
        dtr = take((T,))
        rows_tmp = take((4, T))
        top[0] = PN
        RW = H_SSD * P_SSD + H_SSD + H_RET * D_RET
        tk_s = take((RW,))
        rm_s = take((RW,))
        st_s_t = [take((H_SSD, P_SSD)) for _ in range(RING)]
        sr_s_t = [take((H_RET, D_RET)) for _ in range(RING)]
        ab_s = take((H_SSD,))
        sdt = take((H_SSD,))
        rows_kept = take((4, T))
        R_CUM, R_NCUM, R_DT, R_TE = range(4)

        def row(i):
            return (rows_kept[0:H_SSD, i, :] if i < 4 else rows_tmp[0:H_SSD, i - 4, :])

        top[0] = PN + T
        rr, la, lt = (take((4, T)) for _ in range(3))

        top[0] = 0
        U = [take((8, GRP * 128)) for _ in range(2)]
        gh = take((2, T))
        gijT = take((3, T))
        PEER = top[0]
        qT = take((HC, T))
        kT = take((HC, KEYS))
        qs = take((HC, TT))
        s_sb = take((HC, KEYS))
        s_top = take((HC, TOPK))
        i_u = take((HC, TOPK)).bitcast(U32)
        i_f = take((HC, TOPK))
        c_top = take((H_PEER, TOPK))
        sel = take((H_PEER, TOPK)).bitcast(U32)
        j_u = take((2, SLOTS)).bitcast(U32)
        j_f = take((2, SLOTS))
        gsum = take((2, H_PEER))
        gij = take((3, SLOTS))
        oh = take((SLOTS, TOPK))
        cand = take((H_PEER, TOPK * TOPK))
        top[0] = PEER
        stage = [take((KEYS, BT)) for _ in range(2)]
        Ah = take((AB, 128))
        Bh = take((AB, 128))
        top[0] = PEER
        V = [take((GRP, D)) for _ in range(2)]
        gt = [take((NB, GRP * BT)) for _ in range(2)]
        W = [take((GRP, T)) for _ in range(2)]
        ga = [take((GRP, T)) for _ in range(2)]

        PS = ctx.enter_context(nc.psum_tensor("PS", [128, 8, 512], F32))
        ident, ones = C[:, K_ID:K_ID + 128], C[:, K_ONE:K_ONE + 128]
        iota = C[:, K_IOTA:K_IOTA + 128]

        def halves(bank):
            return PS[:, bank:bank + 2, 0:HALF]

        def two(ap):
            return ap.rearrange("p (h t) -> p h t", h=2)

        def hs(i):
            return slice(i * HALF, (i + 1) * HALF)

        ld_x, ld_small, ld_keys = sem("ld_x"), sem("ld_small"), sem("ld_keys")
        ld_w = [sem(f"ld_w{i}") for i in range(RING)]
        w_free, pj, pj_free = sem("w_free"), sem("pj"), sem("pj_free")
        w_half = sem("w_half")
        n_sq, n_ss, n_rt, n_h = sem("n_sq"), sem("n_ss"), sem("n_rt"), sem("n_h")
        raw, dt_raw = sem("raw"), sem("dt_raw")
        conv, act_x, mixin = sem("conv"), sem("act_x"), sem("mixin")
        rot_p, rot_x = sem("rot_p"), sem("rot_x")
        dt_q, dt_e, dt_r = sem("dt_q"), sem("dt_e"), sem("dt_r")
        ck_0 = sem("ck_0")
        ck_x, ck_r = sem("ck_x"), sem("ck_r")
        ck_t, ck_tok, ck_atok = sem("ck_t"), sem("ck_tok"), sem("ck_atok")
        ck_s, ck_sc, ck_mr = sem("ck_s"), sem("ck_sc"), sem("ck_mr")
        ck_seg, ck_exp, ck_m = sem("ck_seg"), sem("ck_exp"), sem("ck_m")
        ck_y, ck_yr, ck_ye = sem("ck_y"), sem("ck_yr"), sem("ck_ye")
        ck_st, ck_S, st_p = sem("ck_st"), sem("ck_S"), sem("st_p")
        s_t = sem("s_t")
        s_rm, s_bc, s_new = sem("s_rm"), sem("s_bc"), sem("s_new")
        s_y, s_ye = sem("s_y"), sem("s_ye")
        ld_s, st_s = ([sem(f"{n}_s{i}") for i in range(RING)] for n in ("ld", "st"))
        yn_y, yn_sq, yn_ss, yn_rt, yn_m = (sem(f"yn_{n}") for n in ("y", "sq", "ss", "rt", "m"))
        yn_g = sem("yn_g")
        lr_p, lr_a, lr_t = sem("lr_p"), sem("lr_a"), sem("lr_t")
        lr_q, lr_r, lr_h = sem("lr_q"), sem("lr_r"), sem("lr_h")
        states_out, small_out = sem("states_out"), sem("small_out")
        x_mid, st_small = sem("x_mid"), sem("st_small")
        q_in, q_cp, q_s, q_sc = sem("q_in"), sem("q_cp"), sem("q_s"), sem("q_sc")
        q_sm, q_ex, q_g = sem("q_sm"), sem("q_ex"), sem("q_g")
        q_tp, q_tr = sem("q_tp"), sem("q_tr")
        q_free = sem("q_free")
        g_ab, g_mm, g_cp = sem("g_ab"), sem("g_mm"), sem("g_cp")
        g_out = [sem("g_out0"), sem("g_out1")]
        ld_u, ld_v, ld_g = ([sem(f"ld_{n}{i}") for i in range(2)] for n in "uvg")
        m_h, m_gelu, m_w, m_y, m_acc = (sem(f"m_{n}") for n in ("h", "gelu", "w", "y", "acc"))
        a_out, ld_a = [sem("a_out0"), sem("a_out1")], [sem("ld_a0"), sem("ld_a1")]
        st_y = sem("st_y")
        passed = sem("passed")
        v_seq, a_seq = sem("v_seq"), sem("a_seq")

        def apart(eng):
            eng.sem_inc(passed, 1)

        class Order:

            def __init__(self, eng, s):
                self.eng, self.s, self.n, self.settled = eng, s, 0, 0

            def restart(self):
                assert self.settled == self.n
                apart(self.eng)
                self.eng.sem_clear(self.s)
                self.n = self.settled = 0

            def mark(self, ins):
                ins.then_inc(self.s, 1)
                self.n += 1

            def settle(self):
                self.eng.wait_ge(self.s, self.n)
                self.settled = self.n

            def then(self, ins):
                self.mark(ins)
                self.settle()

        H0, W0, Y0, GE0, ACC0, G0 = 2 * GRP, 2 * GRP, 2 * KT, 2, KT, AB // 4
        block = ctx.enter_context(nc.Block())

        @block.sync
        def _(sp):
            sp.dma_start(xT[:, :, :], x).then_inc(ld_x, 16)
            sp.dma_start(C[:, :], cst).then_inc(ld_x, 16)
            for s, n in ((w_free, RING), (pj_free, 2), (m_h, H0), (m_w, W0), (m_y, Y0), (m_gelu, GE0), (m_acc, ACC0),
                         (g_mm, G0), (g_cp, 2)):
                sp.sem_inc(s, n)
            for s in (small_out, states_out, ck_seg, ck_S, ck_ye, ck_st, ck_m, s_new, s_ye, s_bc, act_x, rot_x, q_s, q_sc, q_g, q_tp, q_tr,
                      *st_s, *g_out, *a_out):
                sp.sem_inc(s, 1)
            with sp.Fori(0, DEPTH) as l:
                def load_unit(g, s):
                    sp.dma_start(ring[:, s, :, :], w[l, g * RING + s]).then_inc(ld_w[s], 16)

                G_IN, G_OUT, freed, tiles = NT // RING, 4, (NT + 16) * l, l * TILES_L + NT + 1
                with sp.Fori(0, G_IN) as g:
                    for s in range(RING):
                        sp.wait_ge(w_free, freed + g * RING + s + 1)
                        load_unit(g, s)
                for g in range(G_OUT + 1):
                    for s in range(RING):
                        if g == 0:
                            sp.wait_ge(w_free, freed + NT + s + 1)
                        elif g % 2:
                            sp.wait_ge(w_half, l * KT + (g // 2) * RING + s + 1)
                        else:
                            sp.wait_ge(pj, tiles + (g // 2 - 1) * RING + s + 1)
                        load_unit(G_IN + g, s)
                with sp.Fori(1, 4) as g:
                    for s in range(RING):
                        sp.wait_ge(w_free, freed + NT + g * RING + s + 1)
                        load_unit(g + G_IN + G_OUT, s)

                def load_u(j, n, b):
                    sp.wait_ge(m_h, n * GRP + H0 - GRP)
                    sp.dma_start(U[b], u_tab[l, j]).then_inc(ld_u[b], 16)

                def load_gates_v(j, n, b):
                    sp.wait_ge(m_w, n * GRP + W0 - GRP)
                    sp.dma_start(gt[b], gates[:, :, bass.ds(j * GRP * BT, GRP * BT)].rearrange("n p c -> p n c")).then_inc(ld_g[b], 16)
                    sp.wait_ge(m_y, n * KT + Y0 - KT)
                    sp.dma_start(V[b], v_tab[l, j]).then_inc(ld_v[b], 16)

                n0 = l * NG
                load_u(0, n0, 0)
                load_u(1, n0 + 1, 1)
                with sp.Fori(0, EARLY // 2) as i:
                    for b in range(2):
                        for e in range(GRP):
                            sp.wait_ge(m_gelu, (n0 + i * 2 + b) * GRP + e + 1 + GE0)
                            sp.dma_start(early[i * 2 + b, :, e * T:(e + 1) * T], gh[:, e % 2, :]).then_inc(a_out[e % 2], 16)
                        load_u(i * 2 + b + 2, n0 + i * 2 + b + 2, b)
                sp.wait_ge(g_out[0], 16 * 7 * (l + 1) + 1)
                apart(sp)
                sp.wait_ge(g_out[1], 16 * 6 * (l + 1) + 1)
                apart(sp)
                with sp.Fori(0, (NG - EARLY) // 2 - 1) as i:
                    for b in range(2):
                        load_gates_v(i * 2 + b + EARLY, n0 + i * 2 + b, b)
                        load_u(i * 2 + b + EARLY + 2, n0 + i * 2 + b + EARLY + 2, b)
                for b in range(2):
                    load_gates_v(NG - 2 + b, n0 + NG - EARLY - 2 + b, b)
                for b in range(2):
                    sp.wait_ge(a_out[b], 16 * 2 * EARLY * (l + 1) + 1)
                    apart(sp)
                with sp.Fori(0, EARLY // 2) as i:
                    for b in range(2):
                        n = n0 + NG - EARLY + i * 2 + b
                        sp.wait_ge(m_w, n * GRP + W0 - GRP)
                        sp.dma_start(ga[b].rearrange("p e t -> p (e t)"), early[i * 2 + b]).then_inc(ld_a[b], 16)
                        load_gates_v(i * 2 + b, n, b)
            sp.wait_ge(n_h, KT * (2 * DEPTH + 1))
            sp.dma_start(y, hT[:, :, :]).then_inc(st_y, 16)
            sp.wait_ge(st_y, 16)

        @block.gpsimd
        def _(pool):
            with pool.Fori(0, DEPTH) as l:
                pool.wait_ge(m_acc, l * NG * KT + ACC0)
                apart(pool)
                for dst, src in ((col[:, :], cols[l]), (head[:, :], heads[l]), (cb[:, :, :, :], cbuf[l]),
                                 (lru0[:, :, :], h0[l]), (blk[:, :, :], wblk[l]), (wd[:, :, :], wdt[l])):
                    pool.dma_start(dst, src).then_inc(ld_small, 16)
                pool.wait_ge(act_x, 16 * l + 16 + 1)
                pool.wait_ge(rot_x, 8 * l + 8 + 1)
                pool.wait_ge(dt_r, l + 1)
                apart(pool)
                with pool.Fori(0, NS // RING) as i:
                    for b in range(RING):
                        pool.wait_ge(st_s[b], 32 * (l * (NS // RING) + i) + 1)
                        apart(pool)
                        pool.dma_start(st_s_t[b], s_ssd[l, i * RING + b]).then_inc(ld_s[b], 16)
                        pool.dma_start(sr_s_t[b], s_ret[l, i * RING + b]).then_inc(ld_s[b], 16)
                pool.wait_ge(ck_0, l + 1)
                apart(pool)
                with pool.Fori(0, NCH) as c:
                    pool.wait_ge(ck_seg, 4 * (l * NCH + c) + 1)
                    rows = hT[0:H_SSD, 0:4, 0:SEQ].rearrange("p i (c j) -> p i c j", j=CH)
                    pool.tensor_copy(crow[0:H_SSD, :, :], rows[:, :, c, :]).then_inc(ck_r, 1)
                pool.wait_ge(ck_S, 7 * NCH * (l + 1) + 1)
                apart(pool)
                pool.dma_start(o_ssd_p[l], S.rearrange("p a b -> p (a b)")).then_inc(st_p, 16)
                pool.dma_start(o_ret_p[l], Sr.rearrange("p a b -> p (a b)")).then_inc(st_p, 16)
                pool.wait_ge(ck_ye, 2 * NCH * (l + 1) + 1)
                pool.wait_ge(mixin, 16 * (l + 1))
                pool.tensor_tensor(P[:, G:G + 4, :], P[:, Y_RET:Y_RET + 4, :], P[:, G:G + 4, :], ALU.mult).then_inc(yn_g, 1)
                pool.wait_ge(st_p, 32 * l + 32)
                pool.sem_inc(states_out, 1)
                pool.wait_ge(lr_h, 3 * l + 3)
                apart(pool)
                pool.dma_start(o_tail[l], tail[:, :, :]).then_inc(st_small, 16)
                pool.dma_start(o_cbuf[l], cbn[:, :, :, :]).then_inc(st_small, 16)
                pool.dma_start(o_lru[l], lruo[:, :, :]).then_inc(st_small, 16)
                pool.wait_ge(x_mid, KT * l + KT)
                apart(pool)
                pool.dma_start(kT, keys[l]).then_inc(ld_keys, 16)
                pool.wait_ge(st_small, 48 * l + 48)
                pool.sem_inc(small_out, 1)
                pool.wait_ge(q_in, HC * l + HC)
                apart(pool)
                with pool.Fori(1, 5) as t:
                    pool.wait_ge(q_s, l * 5 + t + 1)
                    pool.tensor_copy(qs, qT.rearrange("p h (t c) -> p h t c", c=TT)[:, :, t, :]).then_inc(q_cp, 1)
            pool.wait_ge(st_p, 32 * DEPTH)
            pool.wait_ge(st_small, 48 * DEPTH)

        @block.tensor
        def _(pe):
            mm = pe.matmul

            def sums(src, bank, done, base):
                for k in range(KT):
                    pe.wait_ge(done, base + k + 1)
                    for h in range(2):
                        last = mm(PS[:, bank + h, 0:HALF], ones, src[:, k, hs(h)], start=(k == 0), stop=(k == KT - 1))
                return last

            def unit(l, g, s, b, k0, src, first=True, final=True, normed=None):
                pe.wait_ge(ld_w[s], (l * (UNITS // RING) + g) * 16 + 16)
                for h in range(2):
                    for k in range(8):
                        if normed is not None and h == 0:
                            pe.wait_ge(n_h, normed + k + 1)
                        last = mm(PS[:, 2 * b + h, 0:HALF], ring[:, s, k, :], src[:, k0 + k, hs(h)],
                                  start=(first and k == 0), stop=(final and k == 7), skip_group_check=True)
                return last

            pe.wait_ge(ld_x, 32)
            with pe.Fori(0, DEPTH) as l:
                tile0 = l * TILES_L
                sums(hT, 0, n_sq, 2 * l * KT).then_inc(n_ss, 1)
                pe.wait_ge(ld_small, 96 * l + 96)
                pe.wait_ge(pj_free, tile0 + 1)
                for h in range(2):
                    for k in range(KT):
                        if h == 0:
                            pe.wait_ge(n_h, 2 * l * KT + k + 1)
                        last = mm(PS[0:H_SSD, 6 + h, 0:HALF], wd[:, k, :], hT[:, k, hs(h)], start=(k == 0), stop=(k == KT - 1))
                last.then_inc(pj, 1)

                def project(g, s):
                    pe.wait_ge(pj_free, tile0 + g * RING + s + 2)
                    unit(l, g, s, s % 2, 0, hT).then_inc(pj, 1)

                with pe.Fori(0, 7) as g:
                    for s in range(RING):
                        project(g, s)
                for i in range(4):
                    project(7, i)
                    pe.wait_ge(raw, 28 * l + 28)
                    for j, t0 in enumerate((KV, Q)):
                        pe.wait_ge(rot_x, l * 8 + i * 2 + 1)
                        for h in range(2):
                            last = mm(PS[:, 4 + 2 * j + h, 0:HALF], C[:, K_PERM:K_PERM + 128],
                                      P[:, t0 + i, hs(h)], start=True, stop=True)
                        last.then_inc(rot_p, 1)
                pe.wait_ge(act_x, 16 * l + 16 + 1)
                pe.wait_ge(rot_x, 8 * l + 8 + 1)
                pe.wait_ge(dt_r, l + 1)
                for i in range(8):
                    pe.transpose(PS[0:NS, 4 + i // 4, (i % 4) * 128:(i % 4 + 1) * 128], P[:, XBC + i, SEQ:T], ident)
                for i in range(4):
                    pe.transpose(PS[0:NS, 6, i * 128:(i + 1) * 128], P[:, KV + 4 + i, SEQ:T], ident)
                for i, r in enumerate((R_DT, R_CUM)):
                    last = pe.transpose(PS[0:NS, 7, i * H_SSD:(i + 1) * H_SSD], row(r)[:, SEQ:T], C[0:H_SSD, K_ID:K_ID + H_SSD])
                last.then_inc(s_t, 1)
                with pe.Fori(0, NS // RING) as i:
                    for s in range(RING):
                        n = l * NS + i * RING + s
                        pe.wait_ge(s_rm, n + 1)
                        pe.wait_ge(s_new, n + 1)
                        one = C[0:NS, K_ONE:K_ONE + 128]
                        for g in range(2):
                            mm(PS[:, 4 + g, :], one, rm_s[0:NS, g * 512:(g + 1) * 512], start=True, stop=True)
                        mm(PS[:, 6, :], one, rm_s[0:NS, D + H_SSD:RW], start=True, stop=True)
                        pe.wait_ge(s_ye, n + 1)
                        mm(PS[:, 7, 0:H_SSD], one, rm_s[0:NS, D:D + H_SSD], start=True, stop=True).then_inc(s_bc, 1)
                        project(i + 8, s)
                        pe.wait_ge(s_new, n + 1 + 1)
                        cur = bass.ds(i * RING + s + SEQ, 1)
                        for j in range(8):
                            mm(PS[:, 7, H_SSD + j:H_SSD + j + 1], st_s_t[s][:, 2 * j:2 * j + 2, :], P[:, XBC + 10 + j // 4, cur],
                               start=True, stop=True, skip_group_check=True)
                        for h in range(H_RET):
                            last = mm(PS[:, 7, H_SSD + 8 + h:H_SSD + 9 + h], sr_s_t[s][:, h, :], P[:, Q + h, cur],
                                      start=True, stop=True, skip_group_check=True)
                        last.then_inc(s_y, 1)
                for s in range(RING):
                    project(10, s)
                pe.wait_ge(pj_free, tile0 + 1 + NT + 2)
                pe.wait_ge(s_ye, NS * (l + 1) + 1)
                apart(pe)
                with pe.Fori(0, NCH) as c:
                    it = l * NCH + c
                    pe.wait_ge(ck_x, 2 * it + 2)
                    pe.wait_ge(ck_r, it + 1)
                    pe.wait_ge(ck_ye, 2 * it + 1)
                    for i in range(8):
                        pe.transpose(PS[:, i // 4, (i % 4) * CH:(i % 4 + 1) * CH], xc[:, i, :], ident)
                    for i in range(4):
                        pe.transpose(PS[:, 4, i * CH:(i + 1) * CH], xc[:, 16 + i, :], ident)
                    pe.wait_ge(ck_S, 7 * it + 1)
                    for i in range(2):
                        pe.transpose(PS[:, 2, i * CH:(i + 1) * CH], xc[:, 8 + i, :], ident)
                    for i in range(4):
                        pe.transpose(PS[:, 3, i * CH:(i + 1) * CH], xc[:, 12 + i, :], ident)
                    for i in range(3):
                        last = pe.transpose(PS[:, 7, i * H_SSD:(i + 1) * H_SSD], crow[0:H_SSD, R_NCUM + i, :], C[0:H_SSD, K_ID:K_ID + H_SSD])
                    last.then_inc(ck_t, 1)
                    for g in range(2):
                        mm(PS[:, 5, g * CH:(g + 1) * CH], xc[:, 8 + g, :], xc[:, 10 + g, :], start=True, stop=True)
                    for h in range(H_RET):
                        last = mm(PS[:, 6, h * CH:(h + 1) * CH], xc[:, 12 + h, :], xc[:, 20 + h, :], start=True, stop=True)
                    last.then_inc(ck_s, 1)

                    def decays(q):
                        if q == 0:
                            pe.wait_ge(ck_tok, 4 * it + 1)
                            pe.wait_ge(ck_atok, 2 * it + 1)
                        elif q == 1:
                            pe.wait_ge(ck_mr, 2 * it + 1)
                            pe.wait_ge(ck_tok, 4 * it + 4)
                        else:
                            pe.wait_ge(ck_exp, 20 * it + 5 * (q - 1))
                        seg, cum = 7 - q % 2, 2 + q % 2
                        mm(PS[:, seg, :], mask[:, 0, :], mask[:, 1:2, :].to_broadcast([128, 4, CH]),
                           start=True, stop=False, skip_group_check=True)
                        for r in range(4):
                            h = 4 * q + r
                            pick = C[0:H_SSD, K_ID + h:K_ID + h + 1].to_broadcast([H_SSD, CH])
                            o = slice(r * CH, (r + 1) * CH)
                            mm(PS[:, seg, o], pick, crow[0:H_SSD, 0, :], start=False, stop=(r == 3), skip_group_check=True)
                            last = mm(PS[:, cum, o], pick, crow[0:H_SSD, 0, :], start=True, stop=True)
                        last.then_inc(ck_seg, 1)

                    def outputs(q):
                        pe.wait_ge(ck_m, 12 * it + 3 * q + 3 + 1)
                        if q == 0:
                            pe.wait_ge(ck_tok, 4 * it + 3)
                        for r in range(4):
                            h = 4 * q + r
                            p0 = 64 * (h % 2)
                            o = PS[p0:p0 + 64, h // 8, (h // 2 % 4) * CH:(h // 2 % 4 + 1) * CH]
                            mm(o, vdt[:, h, :], dec[:, q % 2, r, :], start=True, stop=False, skip_group_check=True)
                            last = mm(o, S[:, h, :], ec[:, q % 2, r, :], start=False, stop=True, skip_group_check=True)
                        last.then_inc(ck_y, 1)

                    decays(0)
                    decays(1)
                    pe.wait_ge(ck_atok, 2 * it + 2)
                    pe.wait_ge(ck_mr, 2 * it + 2)
                    for h in range(H_RET):
                        o = PS[:, 4, h * CH:(h + 1) * CH]
                        mm(o, vtok[:, h, :], mr[:, h, :], start=True, stop=False, skip_group_check=True)
                        last = mm(o, Sr[:, h, :], xc[:, 20 + h, :], start=False, stop=True, skip_group_check=True)
                    last.then_inc(ck_yr, 1)
                    outputs(0)
                    decays(2)
                    outputs(1)
                    decays(3)
                    outputs(2)
                    pe.wait_ge(ck_sc, it + 1)
                    mm(PS[:, 5, :], btok[:, 0, :], vend[:, 0:8, :], start=True, stop=True)
                    outputs(3)
                    pe.wait_ge(ck_exp, 20 * it + 20)
                    mm(PS[:, 2, :], btok[:, 1, :], vend[:, 8:16, :], start=True, stop=True)
                    for h in range(H_RET):
                        last = mm(PS[:, 3, h * CH:(h + 1) * CH], kend[:, h, :], vtok[:, h, :], start=True, stop=True)
                    last.then_inc(ck_st, 1)
                pe.wait_ge(ck_ye, 2 * NCH * (l + 1) + 1)
                for n in range(8):
                    i, j = n // 2, n % 2
                    if n >= 2:
                        pe.wait_ge(lr_a, 8 * l + n - 1)
                    for h in range(2):
                        last = mm(PS[:, 6 * j + h, 0:HALF], blk[:, 4 * j + i, :], P[:, XR + i, hs(h)], start=True, stop=True)
                    last.then_inc(lr_p, 1)
                pe.wait_ge(yn_sq, 9 * l + 1)
                pe.wait_ge(lr_a, 8 * l + 8)
                pe.wait_ge(ck_S, 7 * NCH * (l + 1) + 1)
                for h in range(H_RET):
                    mm(PS[:, h, :], ones, P[:, 8 + h, 0:SEQ], start=True, stop=True)
                for h in range(H_RET):
                    last = mm(PS[:, 6, h * NS:(h + 1) * NS], ones, P[:, 8 + h, SEQ:T], start=True, stop=True)
                last.then_inc(yn_ss, 1)
                sums(P, 4, yn_sq, 9 * l + 1).then_inc(yn_ss, 1)
                with pe.Fori(0, 2) as g:
                    pe.wait_ge(yn_m, 9 * l + 8)
                    for s in range(RING):
                        pe.wait_ge(pj_free, tile0 + NT + g * RING + s)
                        unit(l, NT // RING + 2 * g, s, s, MIX, P, final=False).then_inc(w_half, 1)
                    pe.wait_ge(yn_m, 9 * l + 9)
                    pe.wait_ge(lr_h, 3 * l + 3)
                    for s in range(RING):
                        unit(l, NT // RING + 2 * g + 1, s, s, MIX + 8, P, first=False).then_inc(pj, 1)
                pe.wait_ge(pj_free, tile0 + NT + 1 + 5 + 2)
                sums(hT, 0, n_sq, (2 * l + 1) * KT).then_inc(n_ss, 1)
                with pe.Fori(0, 4) as g:
                    for s in range(RING):
                        pe.wait_ge(pj_free, tile0 + NT + 9 + g * RING + s + 1)
                        unit(l, NT // RING + 4 + g, s, s % 2, 0, hT, normed=(2 * l + 1) * KT if s == 0 else None).then_inc(pj, 1)
                def scores(n, transposed):
                    pe.wait_ge(q_cp, n + 1)
                    pe.wait_ge(q_sc, n + 1)
                    pe.wait_ge(q_tr, transposed + 1)
                    for j in range(HC):
                        last = mm(PS[0:TT, 4 + j // 4, (j % 4) * KEYS:(j % 4 + 1) * KEYS], qs[:, j, :], kT[:, j, :], start=True, stop=True)
                    last.then_inc(q_s, 1)

                def product(n, b, e):
                    pe.wait_ge(m_gelu, n * GRP + e + GE0 - 1)
                    for h in range(2):
                        for k in range(KT):
                            last = mm(PS[:, 2 * (e % 2) + h, 0:HALF], U[b][:, k, e * 128:(e + 1) * 128],
                                      hT[:, k, hs(h)], start=(k == 0), stop=(k == KT - 1))
                    last.then_inc(m_h, 1)

                def products(n, b, loads):
                    pe.wait_ge(ld_u[b], 16 * loads)
                    for e in range(GRP):
                        product(n, b, e)

                def choice(t, more):
                    n = l * 5 + t
                    products(l * NG + t * 2, 0, l * (NG // 2) + t + 1)
                    if more:
                        scores(n + 1, n)
                    products(l * NG + t * 2 + 1, 1, l * (NG // 2) + t + 1)
                    pe.wait_ge(q_g, n + 1 + 1)
                    if more:
                        pe.wait_ge(q_sc, n + 2 + 1)
                    for j in range(3):
                        last = pe.transpose(PS[:, 4, j * TT:(j + 1) * TT], gij[0:TT, j, :], C[0:TT, K_ID:K_ID + TT])
                    last.then_inc(q_tp, 1)

                pe.wait_ge(ld_keys, 16 * l + 16)
                pe.wait_ge(pj_free, tile0 + TILES_L + 2)
                scores(l * 5, l * 5)
                with pe.Fori(0, 4) as t:
                    choice(t, True)
                choice(4, False)

                def gate_quad(n, q):
                    pe.wait_ge(g_cp, n + q + 1)
                    pe.wait_ge(g_ab, (n + q) * 8 + 8)
                    for r in range(4):
                        s = (4 * q + r) % AB
                        last = mm(PS[:, 5 + q % 2, r * KEYS:(r + 1) * KEYS], Bh[:, s, :], Ah[:, s, :], start=True, stop=True)
                    last.then_inc(g_mm, 1)

                with pe.Fori(0, NB // 4) as i:
                    for b in range(2):
                        pe.wait_ge(ld_u[b], 16 * (l * (NG // 2) + i + 6))
                        for e in range(GRP):
                            product(l * NG + i * 2 + 10 + b, b, e)
                            for q in range(e * TILE_PAIR // GRP, (e + 1) * TILE_PAIR // GRP):
                                gate_quad(l * NB * QUADS + (i * 2 + b) * TILE_PAIR, q)
                for q in range(QUADS):
                    gate_quad(l * NB * QUADS + (NB - 1) * QUADS, q)
                pe.wait_ge(g_cp, NB * QUADS * (l + 1) + 2)

                def results(n, b, loads):
                    pe.wait_ge(ld_v[b], 16 * loads)
                    pe.wait_ge(m_w, n * GRP + GRP + W0)
                    for d in range(KT):
                        pe.wait_ge(m_acc, n * KT + d + ACC0 - 1)
                        for h in range(2):
                            for e in range(GRP):
                                last = mm(PS[:, 4 + 2 * (d % 2) + h, 0:HALF], V[b][:, e, d * 128:(d + 1) * 128],
                                          W[b][:, e, hs(h)], start=(e == 0), stop=(e == GRP - 1))
                        last.then_inc(m_y, 1)

                u0, v0, ld0 = l * NG + EARLY, l * NG, l * (NG // 2)
                LATE = NG - EARLY
                products(u0, 0, ld0 + EARLY // 2 + 1)
                with pe.Fori(0, LATE // 2 - 1) as i:
                    products(u0 + i * 2 + 1, 1, ld0 + EARLY // 2 + i + 1)
                    results(v0 + i * 2, 0, ld0 + i + 1)
                    products(u0 + i * 2 + 2, 0, ld0 + EARLY // 2 + i + 2)
                    results(v0 + i * 2 + 1, 1, ld0 + i + 1)
                products(u0 + LATE - 1, 1, ld0 + NG // 2)
                with pe.Fori(0, EARLY // 2 + 1) as i:
                    for b in range(2):
                        results(v0 + LATE - 2 + i * 2 + b, b, ld0 + LATE // 2 + i)
            sums(hT, 0, n_sq, 2 * DEPTH * KT).then_inc(n_ss, 1)

        @block.scalar
        def _(act):
            A = act.activation
            own = Order(act, a_seq)

            def norm(m, ready, base):
                for k in range(KT):
                    act.wait_ge(ready, base + k + 1)
                    A(hT[:, k, :], xT[:, k, :], ACT.Square).then_inc(n_sq, 1)
                act.wait_ge(n_ss, m + 1)
                A(two(rs), halves(0), ACT.Sqrt, bias=eps[:, 0:1], scale=1.0 / D).then_inc(n_rt, 1)

            act.wait_ge(ld_x, 32)
            act.wait_ge(dt_q, 1)
            with act.Fori(0, DEPTH) as l:
                own.restart()
                tile0 = l * TILES_L
                norm(2 * l, m_acc, l * NG * KT + ACC0 - KT)
                act.wait_ge(pj, tile0 + 1)
                A(two(dtr[0:H_SSD, :]), PS[0:H_SSD, 6:8, 0:HALF], ACT.Copy).then_inc(dt_raw, 1)

                def take_tile(g, s, func, done):
                    act.wait_ge(pj, tile0 + g * RING + s + 2)
                    own.then(A(two(P[:, g * RING + s, :]), halves(2 * (s % 2)), func))
                    act.sem_inc(pj_free, 1)
                    act.sem_inc(w_free, 1)
                    act.sem_inc(done, 1)

                def activate(g, s, func):
                    act.wait_ge(conv, 16 * l + g * RING + s + 1)
                    A(P[:, g * RING + s, :], cv[:, s % 2, :], func).then_inc(act_x, 1)

                def group_loop(a, b, func, done, post=None, post_func=None):
                    with act.Fori(a, b) as g:
                        own.restart()
                        for s in range(RING):
                            take_tile(g, s, func, done)
                            if post is not None:
                                activate(g - post, s, post_func)

                act.sem_inc(pj_free, 1)
                group_loop(0, 1, ACT.Copy, raw)
                act.wait_ge(dt_q, 2 * l + 2)
                A(row(5), row(5), ACT.Exp, scale=-1.0).then_inc(dt_e, 1)
                A(c8[:, 1, :], c8[:, 1, :], ACT.Exp, scale=-1.0).then_inc(dt_e, 1)
                A(nA[:, :], head[:, 1:2], ACT.Exp).then_inc(dt_e, 1)
                group_loop(1, 2, ACT.Copy, raw)
                act.wait_ge(dt_q, 2 * l + 3)
                A(row(R_TE)[:, 0:SEQ], row(R_TE)[:, 0:SEQ], ACT.Exp).then_inc(dt_e, 1)
                A(row(R_CUM)[:, SEQ:T], row(4)[:, SEQ:T], ACT.Exp).then_inc(dt_e, 1)
                group_loop(2, 5, ACT.Copy, raw, 2, ACT.Silu)
                group_loop(5, 6, ACT.Copy, raw, 2, ACT.Copy)
                group_loop(6, 7, ACT.Copy, raw)
                group_loop(7, 8, ACT.Silu, mixin)
                with act.Fori(0, NS // RING) as i:
                    own.restart()
                    for s in range(RING):
                        n = l * NS + i * RING + s
                        take_tile(i + 8, s, ACT.Silu, mixin)
                        act.wait_ge(s_y, n + 1)
                        A(P[:, Y_SSD:Y_SSD + 12, bass.ds(i * RING + s + SEQ, 1)], PS[:, 7, H_SSD:H_SSD + 12].unsqueeze(2), ACT.Copy).then_inc(s_ye, 1)
                        act.dma_start(o_ssd_s[l, i * RING + s], st_s_t[s].rearrange("p a b -> p (a b)")).then_inc(st_s[s], 16)
                        act.dma_start(o_ret_s[l, i * RING + s], sr_s_t[s].rearrange("p a b -> p (a b)")).then_inc(st_s[s], 16)
                group_loop(10, 11, ACT.Gelu, mixin)
                act.wait_ge(act_x, 16 * l + 16 + 1)
                apart(act)
                act.wait_ge(rot_x, 8 * l + 8 + 1)
                apart(act)
                with act.Fori(0, NCH) as c:
                    it = l * NCH + c
                    Pc = P[:, :, 0:SEQ].rearrange("p i (c j) -> p i c j", j=CH)
                    act.wait_ge(ck_m, 12 * it + 1)
                    apart(act)
                    A(xc[:, 0:12, :], Pc[:, XBC:XBC + 12, c, :], ACT.Copy).then_inc(ck_x, 1)
                    A(xc[:, 12:24, :], Pc[:, KV:KV + 12, c, :], ACT.Copy).then_inc(ck_x, 1)
                    act.wait_ge(ck_t, it + 1)
                    act.wait_ge(ck_st, it + 1)
                    A(btok.rearrange("p a b -> p (a b)"), PS[:, 2, 0:2 * CH], ACT.Copy).then_inc(ck_atok, 1)
                    A(vtok.rearrange("p a b -> p (a b)"), PS[:, 4, :], ACT.Copy).then_inc(ck_atok, 1)
                    act.wait_ge(ck_s, it + 1)
                    act.wait_ge(ck_m, 12 * it + 1)
                    A(sc.rearrange("p a b -> p (a b)"), PS[:, 5, 0:2 * CH], ACT.Copy).then_inc(ck_sc, 1)
                    act.wait_ge(ck_tok, 4 * it + 1)
                    for q in range(4):
                        act.wait_ge(ck_seg, 4 * it + q + 1 + 1)
                        if q >= 2:
                            act.wait_ge(ck_y, 4 * it + q - 1)
                            act.wait_ge(ck_m, 12 * it + 3 * (q - 1) + 1)
                        for r in range(4):
                            h = 4 * q + r
                            A(dec[:, q % 2, r, :], PS[:, 7 - q % 2, r * CH:(r + 1) * CH], ACT.Exp, bias=tok[:, 0, h:h + 1]).then_inc(ck_exp, 1)
                        A(ec[:, q % 2, :, :].rearrange("p a b -> p (a b)"), PS[:, 2 + q % 2, :], ACT.Exp).then_inc(ck_exp, 1)
                    act.wait_ge(ck_y, 4 * it + 4)
                    apart(act)
                    A(Pc[:, Y_SSD:Y_SSD + 8, c, :], PS[:, 0:2, :].rearrange("p b (i j) -> p (b i) j", j=CH), ACT.Copy).then_inc(ck_ye, 1)
                    act.wait_ge(ck_yr, it + 1)
                    apart(act)
                    A(Pc[:, Y_RET:Y_RET + 4, c, :], PS[:, 4, :].rearrange("p (i j) -> p i j", j=CH), ACT.Copy).then_inc(ck_ye, 1)
                for n in range(8):
                    i, j = n // 2, n % 2
                    act.wait_ge(lr_p, 8 * l + n + 1)
                    A(two(hT[:, 4 * j + i, :]), halves(6 * j), ACT.Sigmoid,
                      bias=col[:, (C_BA, C_BI)[j] + i:(C_BA, C_BI)[j] + i + 1]).then_inc(lr_a, 1)
                act.wait_ge(ck_ye, 2 * NCH * (l + 1) + 1)
                act.wait_ge(s_ye, NS * (l + 1) + 1)
                A(P[:, 8:12, :], P[:, Y_RET:Y_RET + 4, :], ACT.Square).then_inc(yn_sq, 1)
                for k in range(8):
                    act.wait_ge(yn_y, 8 * l + k + 1)
                    A(P[:, k, :], P[:, Y_SSD + k, :], ACT.Square).then_inc(yn_sq, 1)
                act.wait_ge(yn_ss, 2 * l + 1)
                A(rr[:, :, 0:SEQ], PS[:, 0:4, :], ACT.Sqrt, bias=eps[:, 0:1], scale=1.0 / D_RET).then_inc(yn_rt, 1)
                A(rr[:, :, SEQ:T], PS[:, 6, 0:4 * NS].rearrange("p (h s) -> p h s", s=NS), ACT.Sqrt,
                  bias=eps[:, 0:1], scale=1.0 / D_RET).then_inc(yn_rt, 1)
                act.wait_ge(yn_ss, 2 * l + 2)
                A(two(rs), halves(4), ACT.Sqrt, bias=eps[:, 0:1], scale=1.0 / D).then_inc(yn_rt, 1)
                act.wait_ge(lr_a, 8 * l + 8)
                for i in range(4):
                    A(la[:, i, :], hT[:, i, :], ACT.Exp, scale=c8[:, 4, i:i + 1]).then_inc(lr_t, 1)
                    A(lt[:, i, :], hT[:, i, :], ACT.Tanh, scale=c8[:, 5, i:i + 1]).then_inc(lr_t, 1)
                act.wait_ge(lr_t, 9 * l + 8)
                A(hT[:, 0:4, :], lt, ACT.Identity, bias=C[:, K_ONE:K_ONE + 1]).then_inc(lr_t, 1)
                act.wait_ge(lr_q, l + 1)
                A(lt, lt, ACT.Sqrt).then_inc(lr_r, 1)
                norm(2 * l + 1, x_mid, KT * l)
                for b in range(RING):
                    act.wait_ge(st_s[b], 32 * (NS // RING) * (l + 1) + 1)
                apart(act)
                with act.Fori(0, 4) as g:
                    own.restart()
                    for s in range(RING):
                        act.wait_ge(pj, tile0 + NT + 9 + g * RING + s + 1)
                        own.then(A(two(qT[:, g * RING + s, :]), halves(2 * (s % 2)), ACT.Copy))
                        act.sem_inc(pj_free, 1)
                        act.sem_inc(w_free, 1)
                        act.sem_inc(q_in, 1)
                def early_gelu(j, e):
                    n = l * NG + j
                    act.wait_ge(m_h, n * GRP + e + 1 + H0)
                    act.wait_ge(a_out[e % 2], 16 * (2 * (l * EARLY + j) + e // 2) + 1)
                    A(two(gh[:, e % 2, :]), halves(2 * (e % 2)), ACT.Gelu).then_inc(m_gelu, 1)

                def take_scores(n):
                    act.wait_ge(q_s, n + 1 + 1)
                    A(s_sb[0:TT, :, :].rearrange("p a b -> p (a b)"), PS[0:TT, 4:8, :].rearrange("p a b -> p (a b)"), ACT.Copy).then_inc(q_sc, 1)

                def choice(t, more):
                    n = l * 5 + t
                    for e in range(GRP):
                        early_gelu(t * 2, e)
                    if more:
                        act.wait_ge(q_free, n + 1)
                        take_scores(n + 1)
                    for e in range(2):
                        early_gelu(t * 2 + 1, e)
                    act.wait_ge(q_sm, n + 1)
                    A(gij[0:TT, 0, :], gij[0:TT, 0, :], ACT.Exp).then_inc(q_ex, 1)
                    for e in range(2, GRP):
                        early_gelu(t * 2 + 1, e)
                    act.wait_ge(q_tp, n + 1 + 1)
                    o = gijT[:, :, 4 * TT:T] if not more else gijT.rearrange("p a (t c) -> p a t c", c=TT)[:, :, t, :]
                    A(o, PS[:, 4, 0:3 * TT].rearrange("p (a c) -> p a c", a=3), ACT.Copy).then_inc(q_tr, 1)

                act.wait_ge(q_in, HC * (l + 1))
                A(qs, qT[:, :, 0:TT], ACT.Copy).then_inc(q_cp, 1)
                take_scores(l * 5)
                with act.Fori(0, 4) as t:
                    choice(t, True)
                choice(4, False)

                def gate_quad(n, q, b):
                    act.wait_ge(g_mm, n + q + 1 + G0)
                    o = 4 * (q % QUADS)
                    A(stage[b][:, :, o:o + 4].rearrange("p k t -> p t k"),
                      PS[:, 5 + q % 2, :].rearrange("p (t k) -> p t k", k=KEYS), ACT.Copy).then_inc(g_cp, 1)

                def store_gates(n, blk_i, b):
                    act.wait_ge(g_cp, n + 2)
                    act.dma_start(gates[blk_i], stage[b].rearrange("p k t -> p (k t)")).then_inc(g_out[b], 16)

                with act.Fori(0, NB // 4) as i:
                    for b in range(2):
                        n = l * NB * QUADS + (i * 2 + b) * TILE_PAIR
                        for e in range(GRP):
                            early_gelu(i * 2 + 10 + b, e)
                            for q in range(e * TILE_PAIR // GRP, (e + 1) * TILE_PAIR // GRP):
                                if q == 0:
                                    act.wait_ge(g_out[0], 16 * (7 * l + i * 2 + b) + 1)
                                if q == QUADS:
                                    act.wait_ge(g_out[1], 16 * (6 * l + i * 2 + b) + 1)
                                gate_quad(n, q, q // QUADS)
                                if q % QUADS == QUADS - 1:
                                    store_gates(n + q + 1, (i * 2 + b) * 2 + q // QUADS, q // QUADS)
                n = l * NB * QUADS + (NB - 1) * QUADS
                act.wait_ge(g_out[0], 16 * (7 * l + 6) + 1)
                for q in range(QUADS):
                    gate_quad(n, q, 0)
                store_gates(n + QUADS, NB - 1, 0)
                for b in range(2):
                    act.wait_ge(g_out[b], 16 * (7, 6)[b] * (l + 1) + 1)
                    apart(act)
                    act.wait_ge(a_out[b], 16 * 2 * EARLY * (l + 1) + 1)
                    apart(act)
                with act.Fori(0, NG - EARLY) as i:
                    for e in range(GRP):
                        act.wait_ge(m_h, (l * NG + EARLY + i) * GRP + e + 1 + H0)
                        act.wait_ge(m_w, (l * NG + i) * GRP + e + W0 - 1)
                        A(two(gh[:, e % 2, :]), halves(2 * (e % 2)), ACT.Gelu).then_inc(m_gelu, 1)
            norm(2 * DEPTH, m_acc, DEPTH * NG * KT + ACC0 - KT)
            for b in range(RING):
                act.wait_ge(st_s[b], 32 * DEPTH * (NS // RING) + 1)

        @block.vector
        def _(dve):
            own = Order(dve, v_seq)
            ts, tt, stt = dve.tensor_scalar, dve.tensor_tensor, dve.scalar_tensor_tensor

            def norm(m, w_col):
                dve.wait_ge(n_rt, m + 1)
                own.then(dve.reciprocal(rs, rs))
                for k in range(KT):
                    stt(hT[:, k, :], xT[:, k, :], w_col[:, k:k + 1], rs, ALU.mult, ALU.mult).then_inc(n_h, 1)

            def log1p_of(e, s, w, acc):
                own.then(ts(s, e, 2.0, None, ALU.add))
                own.then(dve.reciprocal(s, s))
                own.then(tt(s, e, s, ALU.mult))
                own.then(tt(w, s, s, ALU.mult))
                own.then(ts(acc, w, 1.0 / 17, None, ALU.mult))
                for k in (15, 13, 11, 9, 7, 5, 3):
                    own.then(stt(acc, acc, 1.0 / k, w, ALU.add, ALU.mult))
                own.then(stt(acc, acc, 1.0, s, ALU.add, ALU.mult))

            dve.memset(eps[:, :], EPS).then_inc(dt_q, 1)
            dve.wait_ge(ld_x, 32)
            dve.tensor_copy(mask[:, 0, :], ident)
            dve.tensor_copy(mask[:, 1, :], C[:, K_MASK:K_MASK + CH])
            with dve.Fori(0, DEPTH) as l:
                own.restart()
                tile0 = l * TILES_L
                dve.wait_ge(ld_small, 96 * l + 96)
                norm(2 * l, col[:, C_N1:C_N1 + 8])
                dve.wait_ge(small_out, l + 1)
                for tap in range(2):
                    own.mark(dve.tensor_copy(cbn[:, :, tap, :], cb[:, :, tap + 1, :]))
                own.settle()
                dve.wait_ge(dt_raw, l + 1)
                lam = col[:, C_LAM:C_LAM + 4]
                own.then(ts(row(4), dtr[0:H_SSD, :], head[:, 0:1], None, ALU.add))
                own.then(stt(row(5), row(4), -1.0, row(4), ALU.mult, ALU.max))
                own.mark(ts(row(4), row(4), 0.0, None, ALU.max))
                own.mark(ts(c8[:, 0, :], lam, -1.0, 0.0, ALU.mult, ALU.max))
                own.then(stt(c8[:, 1, :], lam, -1.0, lam, ALU.mult, ALU.max))
                dve.sem_inc(dt_q, 1)
                dve.wait_ge(dt_e, 5 * l + 3)
                log1p_of(row(5), row(6), row(7), row(2))
                own.then(stt(row(R_DT), row(2), 2.0, row(4), ALU.mult, ALU.add))
                log1p_of(c8[:, 1, :], c8[:, 2, :], c8[:, 3, :], c8[:, 5, :])
                own.then(stt(c8[:, 0, :], c8[:, 5, :], 2.0, c8[:, 0, :], ALU.mult, ALU.add))
                own.mark(ts(c8[:, 4, :], c8[:, 0, :], -8.0, None, ALU.mult))
                own.mark(ts(c8[:, 5, :], c8[:, 0, :], 8.0, None, ALU.mult))
                own.then(ts(nA[:, :], nA[:, :], -1.0, None, ALU.mult))
                own.then(ts(row(4), row(R_DT), nA[:, 0:1], None, ALU.mult))
                for c in range(NCH):
                    o = slice(c * CH, (c + 1) * CH)
                    own.mark(dve.tensor_tensor_scan(row(R_CUM)[:, o], C[0:H_SSD, K_ONE:K_ONE + CH], row(4)[:, o], 0.0, ALU.mult, ALU.add))
                own.settle()
                cum4 = row(R_CUM)[:, 0:SEQ].rearrange("p (c j) -> p c j", j=CH)
                own.mark(ts(row(R_NCUM)[:, 0:SEQ], row(R_CUM)[:, 0:SEQ], -1.0, None, ALU.mult))
                own.then(tt(row(R_TE)[:, 0:SEQ].rearrange("p (c j) -> p c j", j=CH),
                            cum4[:, :, CH - 1:CH].to_broadcast([H_SSD, NCH, CH]), cum4, ALU.subtract))
                dve.sem_inc(dt_q, 1)
                dve.wait_ge(dt_e, 5 * l + 5)
                tt(row(R_TE)[:, 0:SEQ], row(R_TE)[:, 0:SEQ], row(R_DT)[:, 0:SEQ], ALU.mult).then_inc(dt_r, 1)
                cw = col[:, C_CW:C_CW + 64].rearrange("p (i k) -> p i k", k=4)
                with dve.Fori(0, 4) as g:
                    own.restart()
                    for s in range(RING):
                        i = g * RING + s
                        X, o = P[:, i, :], cv[:, s % 2, :]
                        dve.wait_ge(raw, 28 * l + i + 1)
                        if s < 2:
                            dve.wait_ge(act_x, 16 * l + g * RING + 1)
                        else:
                            dve.wait_ge(act_x, 16 * l + i - 1 + 1)
                        own.then(ts(o, X, cw[:, i, 3:4], col[:, bass.ds(i + C_CB, 1)], ALU.mult, ALU.add))
                        for tap in range(3):
                            back = 3 - tap
                            own.mark(stt(o[:, back:SEQ], X[:, 0:SEQ - back], cw[:, i, tap:tap + 1], o[:, back:SEQ], ALU.mult, ALU.add))
                            own.then(stt(o[:, SEQ:T], cb[:, i, tap, :], cw[:, i, tap:tap + 1], o[:, SEQ:T], ALU.mult, ALU.add))
                        own.mark(dve.tensor_copy(tail[:, i, :], X[:, SEQ - 3:SEQ]))
                        own.then(dve.tensor_copy(cbn[:, i, 2, :], X[:, SEQ:T]))
                        dve.sem_inc(conv, 1)
                own.restart()
                dve.wait_ge(raw, 28 * l + 28)
                apart(dve)
                with dve.Fori(0, 4) as i:
                    own.restart()
                    for j, t0 in enumerate((KV, Q)):
                        X = P[:, t0 + i, :]
                        dve.wait_ge(rot_p, 8 * l + i * 2 + j + 1)
                        own.mark(tt(two(rt[:, j, :]), halves(4 + 2 * j), two(C[:, K_SIN:K_SIN + T]), ALU.mult))
                        own.then(tt(X, X, C[:, K_COS:K_COS + T], ALU.mult))
                        tt(X, X, rt[:, j, :], ALU.add).then_inc(rot_x, 1)
                own.restart()
                dve.wait_ge(s_t, l + 1)
                own.mark(dve.tensor_copy(sdt[0:NS, :], PS[0:NS, 7, 0:H_SSD]))
                own.mark(dve.tensor_copy(tk_s[0:NS, D:D + H_SSD], PS[0:NS, 7, H_SSD:2 * H_SSD]))
                own.then(ts(tk_s[0:NS, D + H_SSD:RW], PS[0:NS, 6, :], SCALE, None, ALU.mult))
                own.then(tt(tk_s[0:NS, 0:D].rearrange("p (h q) -> p h q", q=P_SSD), PS[0:NS, 4:6, :].rearrange("p b (h q) -> p (b h) q", q=P_SSD),
                            sdt[0:NS, :].unsqueeze(2).to_broadcast([NS, H_SSD, P_SSD]), ALU.mult))
                with dve.Fori(0, NS // RING) as i:
                    for b in range(RING):
                        own.restart()
                        n = l * NS + i * RING + b
                        cur = bass.ds(i * RING + b + SEQ, 1)
                        s, r = st_s_t[b], sr_s_t[b]
                        dve.wait_ge(s_bc, n + 1)
                        ts(rm_s[0:NS, :], tk_s[0:NS, :], C[0:NS, bass.ds(i * RING + b + K_ID, 1)], None, ALU.mult).then_inc(s_rm, 1)
                        dve.wait_ge(ld_s[b], 32 * (l * (NS // RING) + i + 1))
                        for h in range(H_RET):
                            own.mark(ts(r[:, h, :], r[:, h, :], GAMMA[h], None, ALU.mult))
                        dve.wait_ge(s_bc, n + 1 + 1)
                        own.then(dve.tensor_copy(ab_s, PS[:, 7, 0:H_SSD]))
                        own.then(tt(s, s, ab_s.unsqueeze(2).to_broadcast([128, H_SSD, P_SSD]), ALU.mult))
                        for g in range(2):
                            own.mark(stt(s[:, 8 * g:8 * g + 8, :].rearrange("p h q -> p (h q)"), PS[:, 4 + g, :], P[:, XBC + 8 + g, cur],
                                         s[:, 8 * g:8 * g + 8, :].rearrange("p h q -> p (h q)"), ALU.mult, ALU.add))
                        for h in range(H_RET):
                            own.mark(stt(r[:, h, :], PS[:, 6, h * D_RET:(h + 1) * D_RET], P[:, KV + h, cur], r[:, h, :], ALU.mult, ALU.add))
                        own.settle()
                        dve.sem_inc(s_new, 1)
                own.restart()
                dve.wait_ge(pj, tile0 + 1 + NT)
                own.then(dve.tensor_copy(hT[0:H_SSD, 0:4, 0:SEQ], rows_kept[0:H_SSD, :, 0:SEQ]))
                for b in range(RING):
                    dve.wait_ge(st_s[b], 32 * (NS // RING) * (l + 1) + 1)
                    apart(dve)
                dve.wait_ge(states_out, l + 1)
                own.mark(dve.memset(S, 0.0))
                own.then(dve.memset(Sr, 0.0))
                dve.sem_inc(ck_0, 1)
                with dve.Fori(0, NCH) as c:
                    own.restart()
                    it = l * NCH + c
                    bc = lambda ap, n: ap.unsqueeze(2).to_broadcast([128, ap.shape[1], n])
                    X = PS[:, 0:2, :].rearrange("p b (h q) -> p (b h) q", q=P_SSD)
                    dve.wait_ge(ck_t, it + 1)
                    own.then(dve.tensor_copy(tok, PS[:, 7, 0:3 * H_SSD].rearrange("p (a h) -> p a h", a=3)))
                    dve.sem_inc(ck_tok, 1)
                    tt(vdt, X, bc(tok[:, 1, :], P_SSD), ALU.mult).then_inc(ck_tok, 1)
                    tt(vend, X, bc(tok[:, 2, :], P_SSD), ALU.mult).then_inc(ck_tok, 1)
                    tt(kend, PS[:, 3, :].rearrange("p (h j) -> p h j", j=CH), bc(C[:, K_TE:K_TE + 4], CH), ALU.mult).then_inc(ck_tok, 1)
                    dve.wait_ge(ck_s, it + 1)
                    tt(mr, PS[:, 6, :].rearrange("p (h j) -> p h j", j=CH), C[:, K_DM:K_DM + 4 * CH].rearrange("p (h j) -> p h j", j=CH),
                       ALU.mult).then_inc(ck_mr, 1)
                    tt(xc[:, 20:24, :], xc[:, 20:24, :], C[:, K_GAM:K_GAM + 4 * CH].rearrange("p (h j) -> p h j", j=CH),
                       ALU.mult).then_inc(ck_mr, 1)
                    dve.wait_ge(ck_sc, it + 1)
                    for q in range(4):
                        g = q // 2
                        dve.wait_ge(ck_exp, 20 * it + 5 * q + 5)
                        dve.tensor_copy(cd[:, 4 * q:4 * q + 4].unsqueeze(2), ec[:, q % 2, :, CH - 1:CH]).then_inc(ck_m, 1)
                        dve.wait_ge(ck_m, 12 * it + 3 * q + 1 + 1)
                        tt(dec[:, q % 2, :, :], dec[:, q % 2, :, :], sc[:, g:g + 1, :].to_broadcast([128, 4, CH]), ALU.mult).then_inc(ck_m, 1)
                        tt(ec[:, q % 2, :, :], ec[:, q % 2, :, :], xc[:, 10 + g:11 + g, :].to_broadcast([128, 4, CH]), ALU.mult).then_inc(ck_m, 1)
                    dve.wait_ge(ck_y, 4 * it + 4)
                    own.then(tt(S, S, bc(cd, P_SSD), ALU.mult))
                    dve.wait_ge(ck_st, it + 1 + 1)
                    for g in range(2):
                        tt(S[:, 8 * g:8 * g + 8, :], S[:, 8 * g:8 * g + 8, :],
                           PS[:, (5, 2)[g], :].rearrange("p (h q) -> p h q", q=P_SSD), ALU.add).then_inc(ck_S, 1)
                    for h in range(H_RET):
                        stt(Sr[:, h, :], Sr[:, h, :], GAMMA_CH[h], PS[:, 3, h * CH:(h + 1) * CH], ALU.mult, ALU.add).then_inc(ck_S, 1)
                    dve.wait_ge(ck_S, 7 * it + 6 + 1)
                    dve.sem_inc(ck_S, 1)
                own.restart()
                dve.wait_ge(s_ye, NS * (l + 1) + 1)
                dve.wait_ge(ck_ye, 2 * NCH * (l + 1) + 1)
                dve.wait_ge(mixin, 16 * (l + 1))
                for i in range(8):
                    own.mark(stt(P[:, Y_SSD + i, :], P[:, XBC + i, :], col[:, C_D + i:C_D + i + 1], P[:, Y_SSD + i, :], ALU.mult, ALU.add))
                own.settle()
                for i in range(8):
                    tt(P[:, Y_SSD + i, :], P[:, Y_SSD + i, :], P[:, Z + i, :], ALU.mult).then_inc(yn_y, 1)
                dve.wait_ge(lr_a, 8 * l + 8)
                own.mark(tt(hT[:, 4:8, :], hT[:, 4:8, :], P[:, XR:XR + 4, :], ALU.mult))
                dve.wait_ge(yn_rt, 3 * l + 3)
                own.then(dve.reciprocal(rs, rs))
                dve.wait_ge(yn_y, 8 * l + 8)
                for i in range(8):
                    stt(P[:, Z + i, :], P[:, Y_SSD + i, :], col[:, C_NW + i:C_NW + i + 1], rs, ALU.mult, ALU.mult).then_inc(yn_m, 1)
                flat = lambda ap: ap.rearrange("p a b -> p (a b)")
                dve.wait_ge(lr_t, 9 * l + 9)
                own.then(dve.reciprocal(hT[:, 0:4, :], hT[:, 0:4, :]))
                own.then(stt(flat(lt), flat(lt), 2.0, flat(hT[:, 0:4, :]), ALU.mult, ALU.mult))
                dve.sem_inc(lr_q, 1)
                own.then(dve.reciprocal(rr, rr))
                dve.wait_ge(yn_g, l + 1)
                tt(P[:, G:G + 4, :], P[:, G:G + 4, :], rr, ALU.mult).then_inc(yn_m, 1)
                dve.wait_ge(lr_r, l + 1)
                own.then(tt(lt, lt, hT[:, 4:8, :], ALU.mult))
                for i in range(4):
                    own.mark(dve.tensor_tensor_scan(hT[:, i, 0:SEQ], la[:, i, 0:SEQ], lt[:, i, 0:SEQ], 0.0, ALU.mult, ALU.add))
                own.then(tt(hT[:, 0:4, SEQ:T], la[:, :, SEQ:T], lru0[:, :, :], ALU.mult))
                own.then(tt(hT[:, 0:4, SEQ:T], hT[:, 0:4, SEQ:T], lt[:, :, SEQ:T], ALU.add))
                dve.tensor_copy(lruo[:, :, :], hT[:, 0:4, SEQ - 1:T]).then_inc(lr_h, 1)
                tt(P[:, GATE:GATE + 4, :], hT[:, 0:4, :], P[:, GATE:GATE + 4, :], ALU.mult).then_inc(lr_h, 1)
                dve.wait_ge(lr_h, 3 * l + 2)
                dve.sem_inc(lr_h, 1)
                own.restart()
                with dve.Fori(0, 2) as g:
                    own.restart()
                    for m in range(RING):
                        dve.wait_ge(pj, tile0 + NT + 1 + g * RING + m + 1)
                        X = two(xT[:, g * RING + m, :])
                        own.then(tt(X, X, halves(2 * m), ALU.add))
                        dve.sem_inc(x_mid, 1)
                        dve.sem_inc(pj_free, 1)
                own.restart()
                norm(2 * l + 1, col[:, C_N2:C_N2 + 8])
                with dve.Fori(0, 5) as t:
                    own.restart()
                    n = l * 5 + t
                    R = slice(0, TT)

                    def top16(vals, rows, out, idx):
                        for half in range(2):
                            o = slice(8 * half, 8 * half + 8)
                            for i in range(rows):
                                own.mark(dve.max(out[R, i, o], vals[R, i, :]))
                            own.settle()
                            for i in range(rows):
                                own.mark(dve.max_index(idx[R, i, o], out[R, i, o], vals[R, i, :]))
                            own.settle()
                            if half == 0:
                                for i in range(rows):
                                    own.mark(dve.match_replace(vals[R, i, :], out[R, i, o], vals[R, i, :], -3.0e38))
                                own.settle()

                    dve.wait_ge(q_sc, n + 1 + 1)
                    apart(dve)
                    top16(s_sb, HC, s_top, i_u)
                    dve.sem_inc(q_free, 1)
                    own.mark(dve.tensor_copy(i_f[R], i_u[R]))
                    pair = s_top[R].rearrange("p (h c) j -> p h c j", c=2)
                    c4 = cand[R].rearrange("p h (a b) -> p h a b", b=TOPK)
                    shape = [TT, H_PEER, TOPK, TOPK]
                    own.then(tt(c4, pair[:, :, 0, :].unsqueeze(3).to_broadcast(shape), pair[:, :, 1, :].unsqueeze(2).to_broadcast(shape), ALU.add))
                    top16(cand, H_PEER, c_top, sel)
                    sel1 = sel[R].rearrange("p h k -> p (h k)")
                    own.mark(ts(j_u[R, 0, :], sel1, 4, None, ALU.logical_shift_right))
                    own.mark(ts(j_u[R, 1, :], sel1, 15, None, ALU.bitwise_and))
                    dve.wait_ge(q_tp, n + 1)
                    own.then(tt(gij[R, 0, :].rearrange("p (h k) -> p h k", k=TOPK), c_top[R],
                                c_top[R, :, 0:1].to_broadcast([TT, H_PEER, TOPK]), ALU.subtract))
                    dve.sem_inc(q_sm, 1)
                    own.then(dve.tensor_copy(j_f[R], j_u[R]))
                    for side in range(2):
                        own.then(tt(oh[R], C[R, K_IOTA:K_IOTA + TOPK].unsqueeze(1).to_broadcast([TT, SLOTS, TOPK]),
                                    j_f[R, side, :].unsqueeze(2).to_broadcast([TT, SLOTS, TOPK]), ALU.is_equal))
                        oh4 = oh[R].rearrange("p (h k) j -> p h k j", k=TOPK)
                        own.then(tt(oh4, oh4, i_f[R].rearrange("p (h c) j -> p h c j", c=2)[:, :, side, :].unsqueeze(2).to_broadcast(shape), ALU.mult))
                        own.then(dve.tensor_reduce(gij[R, 1 + side, :].unsqueeze(2), oh[R], AX.X, ALU.add))
                    dve.wait_ge(q_ex, n + 1)
                    g3 = gij[R, 0, :].rearrange("p (h k) -> p h k", k=TOPK)
                    own.then(dve.tensor_reduce(gsum[R, 0, :].unsqueeze(2), g3, AX.X, ALU.add))
                    own.then(dve.reciprocal(gsum[R, 1, :], gsum[R, 0, :]))
                    tt(g3, g3, gsum[R, 1, :].unsqueeze(2).to_broadcast([TT, H_PEER, TOPK]), ALU.mult).then_inc(q_g, 1)

                dve.wait_ge(q_tr, 5 * l + 5 + 1)
                own.restart()
                with dve.Fori(0, T // AB) as i:
                    for s in range(AB):
                        if s % 4 == 0:
                            dve.wait_ge(g_mm, (l * (T // AB) + i) * (AB // 4) + s // 4 + 1)
                        t = bass.ds(i * AB + s, 1)
                        ts(Ah[:, s, :], iota, gijT[:, 1, t], gijT[:, 0, t], ALU.is_equal, ALU.mult).then_inc(g_ab, 1)
                        ts(Bh[:, s, :], iota, gijT[:, 2, t], None, ALU.is_equal).then_inc(g_ab, 1)

                def gating(n, b, loads, early_loads=None):
                    dve.wait_ge(ld_g[b], 16 * loads)
                    if early_loads is not None:
                        dve.wait_ge(ld_a[b], 16 * early_loads)
                    dve.wait_ge(m_y, n * KT + Y0 - KT)
                    for e in range(GRP):
                        if early_loads is None:
                            dve.wait_ge(m_gelu, (n + EARLY) * GRP + e + 1 + GE0)
                        g = gh[:, e % 2, :] if early_loads is None else ga[b][:, e, :]
                        tt(W[b][:, e, :].rearrange("p (n c) -> p n c", c=BT), g.rearrange("p (n c) -> p n c", c=BT),
                           gt[b][:, :, e * BT:(e + 1) * BT], ALU.mult).then_inc(m_w, 1)

                def adding(n):
                    for d in range(KT):
                        dve.wait_ge(m_y, n * KT + d + 1 + Y0)
                        X = two(xT[:, d, :])
                        tt(X, X, halves(4 + 2 * (d % 2)), ALU.add).then_inc(m_acc, 1)

                n0, ld0 = l * NG, l * (NG // 2)
                LATE = NG - EARLY
                gating(n0, 0, ld0 + 1)
                with dve.Fori(0, LATE // 2 - 1) as i:
                    gating(n0 + i * 2 + 1, 1, ld0 + i + 1)
                    adding(n0 + i * 2)
                    gating(n0 + i * 2 + 2, 0, ld0 + i + 2)
                    adding(n0 + i * 2 + 1)
                gating(n0 + LATE - 1, 1, ld0 + LATE // 2)
                adding(n0 + LATE - 2)
                with dve.Fori(0, EARLY // 2) as i:
                    for b in range(2):
                        n = n0 + LATE + i * 2 + b
                        gating(n, b, ld0 + LATE // 2 + i + 1, l * (EARLY // 2) + i + 1)
                        adding(n - 1)
                adding(n0 + NG - 1)
                dve.wait_ge(m_acc, KT * NG * (l + 1) + ACC0)
            own.restart()
            norm(2 * DEPTH, C[:, K_FW:K_FW + 8])


def kernel(**inputs):
    import concourse.bacc as _bacc
    from concourse.bass_utils import run_bass_kernel_spmd as _run

    i = {k: np.ascontiguousarray(v) for k, v in inputs.items()}
    def feat(a):
        return a.reshape(DEPTH, -1, 128).transpose(0, 2, 1)

    stream = np.concatenate([i["x_prompt"][0], i["x_sample"][:, 0]])
    ins = {"x": stream.reshape(T, KT, 128).transpose(2, 1, 0)}

    wi = i["w_in"]
    cut = lambda a, b: wi[:, :, a:b]
    order = [cut(1024, 2560), cut(5136, 5648), cut(3088, 3600), cut(3600, 4112), cut(2576, 3088),
             cut(0, 1024), cut(4112, 4624), cut(4624, 5136)]
    w_main = np.concatenate(order, axis=2)
    units = lambda a: a.reshape(DEPTH, -1, 8, 128, a.shape[2] // 128, 128).transpose(0, 4, 1, 3, 2, 5).reshape(DEPTH, -1, 128, 8, 128)
    out_units = units(i["w_out"]).reshape(DEPTH, 2, 4, 2, 128, 8, 128).swapaxes(2, 3).reshape(DEPTH, 16, 128, 8, 128)
    ins["w"] = np.concatenate([units(w_main), out_units, units(i["peer_wq"])], axis=1)
    ins["wdt"] = cut(2560, 2576).reshape(DEPTH, 8, 128, 16).transpose(0, 2, 1, 3)
    ins["keys"] = i["peer_keys"].reshape(DEPTH, HC, KEYS, 128).transpose(0, 3, 1, 2)
    ins["u_tab"] = i["peer_u"].reshape(DEPTH, NG, GRP * 128, 8, 128).transpose(0, 1, 4, 3, 2)
    ins["v_tab"] = i["peer_v"].reshape(DEPTH, NG, GRP, 128, D).transpose(0, 1, 3, 2, 4)
    convw = np.concatenate([i["ssd_conv_w"], i["lru_conv_w"]], axis=2)
    convb = np.concatenate([i["ssd_conv_b"], i["lru_conv_b"]], axis=1)
    ins["cols"] = np.concatenate([
        feat(i["norm1_w"]), feat(i["norm2_w"]),
        convw.reshape(DEPTH, 4, 16, 128).transpose(0, 3, 2, 1).reshape(DEPTH, 128, 64), feat(convb),
        feat(np.repeat(i["ssd_d"], P_SSD, axis=1)), feat(i["ssd_norm_w"]),
        feat(i["lru_ba"]), feat(i["lru_bi"]), feat(i["lru_lambda"])], axis=2)
    ins["heads"] = np.stack([i["ssd_dt_bias"], i["ssd_a_log"]], axis=2)
    cbuf = np.concatenate([i["state_ssd_conv"], i["state_lru_conv"]], axis=3)
    ins["cbuf"] = cbuf.reshape(DEPTH, NS, 3, 16, 128).transpose(0, 4, 3, 2, 1)
    ins["h0"] = i["state_lru"].reshape(DEPTH, NS, 4, 128).transpose(0, 3, 2, 1)
    blk = np.zeros((DEPTH, 128, 8, 128), np.float32)
    for j, name in enumerate(("lru_wa", "lru_wi")):
        for k in range(8):
            a = 64 * (k % 2)
            blk[:, a:a + 64, 4 * j + k // 2, a:a + 64] = i[name][:, k]
    ins["wblk"] = blk
    ins["s_ssd"] = i["state_ssd"].transpose(0, 1, 3, 2, 4)
    ins["s_ret"] = i["state_ret"].transpose(0, 1, 3, 2, 4)

    pos = np.concatenate([np.arange(SEQ), np.full(NS, PAST)]).astype(np.float32)
    inv = (np.float32(10000.0) ** (-np.arange(64, dtype=np.float32) / np.float32(64))).astype(np.float32)
    ang = np.tile((inv[:, None] * pos[None, :]).astype(np.float32), (2, 1)).astype(np.float64)
    perm = np.zeros((128, 128))
    perm[np.arange(64) + 64, np.arange(64)] = -1.0
    perm[np.arange(64), np.arange(64) + 64] = 1.0
    j, k = np.arange(CH)[:, None], np.arange(CH)[None, :]
    mask = np.where(k >= j, 0.0, -1e30)
    lg = np.log(1.0 - 2.0 ** (-5.0 - np.arange(H_RET)))
    dm = np.stack([np.where(k >= j, np.exp((k - j) * g), 0.0) * SCALE for g in lg], axis=1).reshape(128, -1)
    gam = np.tile(np.concatenate([np.exp((np.arange(CH) + 1) * g) for g in lg])[None], (128, 1))
    te = np.stack([np.exp((CH - 1 - np.arange(CH)) * g) * SCALE for g in lg], axis=1)
    cst = np.concatenate([np.cos(ang), np.sin(ang), perm, np.eye(128), mask, dm, gam, te,
                          np.tile(np.arange(128.0)[None], (128, 1)), np.ones((128, 128))], axis=1).astype(np.float32)
    ins["cst"] = np.concatenate([cst, i["final_norm_w"].reshape(KT, 128).T], axis=1)

    outs = {"y": (128, KT, T), "o_ssd_p": (DEPTH, 128, 1024), "o_ret_p": (DEPTH, 128, 512), "o_tail": (DEPTH, 128, 16, 3),
            "o_cbuf": (DEPTH, 128, 16, 3, NS), "o_lru": (DEPTH, 128, 4, 1 + NS),
            "o_ssd_s": (DEPTH, NS, 128, 1024), "o_ret_s": (DEPTH, NS, 128, 512)}
    nc = _bacc.Bacc("TRN2", target_bir_lowering=False, num_devices=1)
    ins = {n: np.ascontiguousarray(a, dtype=np.float32) for n, a in ins.items()}
    args = {n: nc.dram_tensor(n, a.shape, F32, kind="ExternalInput").ap() for n, a in ins.items()}
    args["gates"] = nc.dram_tensor("gates", (NB, 128, KEYS * BT), F32, kind="Internal").ap()
    args["early"] = nc.dram_tensor("early", (EARLY, 128, GRP * T), F32, kind="Internal").ap()
    args |= {n: nc.dram_tensor(n, s, F32, kind="ExternalOutput").ap() for n, s in outs.items()}
    decoder_step(nc, **args)
    r = _run(nc, [ins], core_ids=[0]).results[0]

    y = r["y"].transpose(2, 1, 0).reshape(T, D)
    tail = r["o_tail"].transpose(0, 3, 2, 1).reshape(DEPTH, 1, 3, 2048)
    cbn = r["o_cbuf"].transpose(0, 4, 3, 2, 1).reshape(DEPTH, NS, 3, 2048)
    lru = r["o_lru"].transpose(0, 3, 2, 1).reshape(DEPTH, 1 + NS, 512)
    head_major = lambda a, h: a.reshape(a.shape[:-1] + (h, -1)).swapaxes(-3, -2)
    c = np.ascontiguousarray
    return (c(y[None, :SEQ]), c(y[SEQ:, None]),
            c(head_major(r["o_ssd_p"], H_SSD)[:, None]), c(tail[..., :1536]), c(head_major(r["o_ret_p"], H_RET)[:, None]),
            c(lru[:, :1]), c(tail[..., 1536:]),
            c(head_major(r["o_ssd_s"], H_SSD)), c(cbn[..., :1536]), c(head_major(r["o_ret_s"], H_RET)),
            c(lru[:, 1:]), c(cbn[..., 1536:]))
```
